# Optimizing a Trainium2 kernel written in Bass

```python
import jax, jax.numpy as jnp
from jax import lax
import numpy as np

D_MODEL = 2048
BATCH = 1
SEQ = 256
DEPTH = 1

HEAD_DIM = 128
SB_HEADS = 6
SB_BLOCK = 128
DIL_GROUPS = ((128, 1), (512, 4), (2048, 16))
DIL_HEADS_PER_GROUP = 2
DIL_HEADS = DIL_HEADS_PER_GROUP * len(DIL_GROUPS)
GLA_HEADS = 4
GLA_DK = 128
GLA_DV = 256
GLA_GATE_RANK = 16
GLA_GATE_TAU = 16.0
GLA_CHUNK = 64
N_BRANCH = 3
D_FF = -(-8 * D_MODEL // (3 * 256)) * 256
N_MOD = 6
EPS = 1e-6

SB_W = SB_HEADS * HEAD_DIM
DIL_W = DIL_HEADS * HEAD_DIM
DIL_OUT_W = DIL_HEADS_PER_GROUP * HEAD_DIM
GLA_QK_W = GLA_HEADS * GLA_DK
GLA_V_W = GLA_HEADS * GLA_DV
IN_SPLITS = (SB_W, SB_W, SB_W, DIL_W, DIL_W, DIL_W, GLA_QK_W, GLA_QK_W, GLA_V_W, GLA_V_W, GLA_GATE_RANK, N_BRANCH * D_MODEL)
IN_WIDTH = sum(IN_SPLITS)


def rms_norm(x, gain):
    xf = x.astype(jnp.float32)
    y = xf * lax.rsqrt(jnp.mean(jnp.square(xf), axis=-1, keepdims=True) + EPS)
    return (y * gain.astype(jnp.float32)).astype(x.dtype)

def split_heads(x, n):
    b, t, w = x.shape
    return x.reshape(b, t, n, w // n).transpose(0, 2, 1, 3)

def merge_heads(x):
    b, h, t, d = x.shape
    return x.transpose(0, 2, 1, 3).reshape(b, t, h * d)

def alibi_slopes(n):
    return 2.0 ** (-8.0 * jnp.arange(1, n + 1, dtype=jnp.float32) / n)

def stick_breaking_attention(q, k, v):
    b, h, t, d = q.shape
    scale = d ** -0.5
    outs = []
    for blk in range(t // SB_BLOCK):
        start = blk * SB_BLOCK
        end = start + SB_BLOCK
        qb = q[:, :, start:end]
        kb = k[:, :, :end]
        vb = v[:, :, :end]
        z = jnp.einsum('bhqd,bhkd->bhqk', qb, kb).astype(jnp.float32) * scale
        t_pos = start + jnp.arange(SB_BLOCK)[:, None]
        s_pos = jnp.arange(end)[None, :]
        causal = s_pos < t_pos
        log_beta = jax.nn.log_sigmoid(z)
        log_rest = jnp.where(causal, jax.nn.log_sigmoid(-z), 0.0)
        after = lax.cumsum(log_rest, axis=3, reverse=True) - log_rest
        w = jnp.where(causal, jnp.exp(log_beta + after), 0.0)
        outs.append(jnp.einsum('bhqk,bhkd->bhqd', w.astype(v.dtype), vb))
    return jnp.concatenate(outs, axis=2)

def dilated_group_attention(q, k, v, window, dilation, slopes):
    b, h, t, d = q.shape
    blk = window // dilation
    u_len = t // dilation
    nb = -(-u_len // blk)
    u_pad = nb * blk

    def strided(x):
        x = x.reshape(b, h, u_len, dilation, d).transpose(0, 1, 3, 2, 4)
        x = jnp.pad(x, ((0, 0), (0, 0), (0, 0), (0, u_pad - u_len), (0, 0)))
        return x.reshape(b, h, dilation, nb, blk, d)

    def with_prev(x):
        prev = jnp.pad(x[:, :, :, :-1], ((0, 0), (0, 0), (0, 0), (1, 0), (0, 0), (0, 0)))
        return jnp.concatenate([prev, x], axis=4)

    qs = strided(q)
    kk = with_prev(strided(k))
    vv = with_prev(strided(v))
    s = jnp.einsum('bhrnqd,bhrnkd->bhrnqk', qs, kk).astype(jnp.float32) * (d ** -0.5)
    i = jnp.arange(blk)[:, None]
    j = jnp.arange(2 * blk)[None, :]
    delta = blk + i - j
    n = jnp.arange(nb)[:, None, None]
    valid = (delta >= 0) & (delta <= blk) & (n * blk - blk + j >= 0)
    bias = -(slopes.astype(jnp.float32)[:, None, None] * (dilation * delta).astype(jnp.float32))
    logits = jnp.where(valid, s + bias[None, :, None, None], -jnp.inf)
    lse = jax.nn.logsumexp(logits, axis=-1)
    p = jnp.exp(logits - lse[..., None])
    o = jnp.einsum('bhrnqk,bhrnkd->bhrnqd', p.astype(v.dtype), vv)
    o = o.reshape(b, h, dilation, u_pad, d)[:, :, :, :u_len].transpose(0, 1, 3, 2, 4).reshape(b, h, t, d)
    lse = lse.reshape(b, h, dilation, u_pad)[..., :u_len].transpose(0, 1, 3, 2).reshape(b, h, t)
    return o, lse

def dilated_mixture(q, k, v, slopes):
    outs, lses = [], []
    for g, (window, dilation) in enumerate(DIL_GROUPS):
        sl = slice(g * DIL_HEADS_PER_GROUP, (g + 1) * DIL_HEADS_PER_GROUP)
        o, l = dilated_group_attention(q[:, sl], k[:, sl], v[:, sl], window, dilation, slopes[sl])
        outs.append(o)
        lses.append(l)
    weights = jax.nn.softmax(jnp.stack(lses, axis=0), axis=0)
    mixed = jnp.sum(weights[..., None] * jnp.stack(outs, axis=0).astype(jnp.float32), axis=0)
    return mixed.astype(q.dtype)

def gla_chunked(q, k, v, log_a):
    b, h, t, dk = q.shape
    dv = v.shape[-1]
    c = GLA_CHUNK
    n = t // c

    def chunks(x):
        return x.reshape(b, h, n, c, x.shape[-1]).transpose(2, 0, 1, 3, 4)

    qc = chunks((q.astype(jnp.float32) * (dk ** -0.5)))
    kc = chunks(k.astype(jnp.float32))
    vc = chunks(v.astype(jnp.float32))
    ac = chunks(log_a.astype(jnp.float32))
    mask = jnp.tril(jnp.ones((c, c), dtype=bool))

    def step(state, inp):
        qi, ki, vi, ai = inp
        cum = jnp.cumsum(ai, axis=2)
        inter = jnp.einsum('bhcd,bhde->bhce', qi * jnp.exp(cum), state)
        diff = cum[:, :, :, None, :] - cum[:, :, None, :, :]
        decay = jnp.exp(jnp.where(mask[:, :, None], diff, -jnp.inf))
        scores = jnp.einsum('bhid,bhjd,bhijd->bhij', qi, ki, decay)
        intra = jnp.einsum('bhij,bhje->bhie', scores, vi)
        last = cum[:, :, -1:, :]
        new_state = jnp.exp(last[:, :, 0, :])[..., None] * state + jnp.einsum('bhcd,bhce->bhde', ki * jnp.exp(last - cum), vi)
        return new_state, inter + intra

    s0 = jnp.zeros((b, h, dk, dv), jnp.float32)
    _, o = lax.scan(step, s0, (qc, kc, vc, ac))
    return o.transpose(1, 2, 0, 3, 4).reshape(b, h, t, dv).astype(v.dtype)

def mixing_sublayer(h, w_in, sb_q_gain, sb_k_gain, dil_q_gain, dil_k_gain, w_gla_a, b_gla_a, gla_out_gain,
                    w_br_sb, w_br_dil, w_br_gla, w_out):
    b, t, d = h.shape
    proj = h @ w_in
    idx = [int(i) for i in np.cumsum(IN_SPLITS)[:-1]]
    (q_sb, k_sb, v_sb, q_dil, k_dil, v_dil, q_gla, k_gla, v_gla, r_gla, a_gla, gate_cols) = jnp.split(proj, idx, axis=-1)

    qa = rms_norm(split_heads(q_sb, SB_HEADS), sb_q_gain)
    ka = rms_norm(split_heads(k_sb, SB_HEADS), sb_k_gain)
    o_sb = merge_heads(stick_breaking_attention(qa, ka, split_heads(v_sb, SB_HEADS)))

    qb = rms_norm(split_heads(q_dil, DIL_HEADS), dil_q_gain)
    kb = rms_norm(split_heads(k_dil, DIL_HEADS), dil_k_gain)
    o_dil = merge_heads(dilated_mixture(qb, kb, split_heads(v_dil, DIL_HEADS), alibi_slopes(DIL_HEADS)))

    a = (a_gla @ w_gla_a + b_gla_a).astype(jnp.float32)
    log_a = jax.nn.log_sigmoid(a) / GLA_GATE_TAU
    o_g = gla_chunked(split_heads(q_gla, GLA_HEADS), split_heads(k_gla, GLA_HEADS),
                      split_heads(v_gla, GLA_HEADS), split_heads(log_a, GLA_HEADS))
    o_gla = merge_heads(rms_norm(o_g, gla_out_gain)) * jax.nn.silu(r_gla)

    g = jax.nn.sigmoid(gate_cols.reshape(b, t, N_BRANCH, d))
    y = (g[:, :, 0] * (o_sb @ w_br_sb)
         + g[:, :, 1] * (o_dil @ w_br_dil)
         + g[:, :, 2] * (o_gla @ w_br_gla))
    return y @ w_out

def swiglu(h, w_ffn_in, w_ffn_out):
    gate, up = jnp.split(h @ w_ffn_in, 2, axis=-1)
    return (jax.nn.silu(gate) * up) @ w_ffn_out

def first_inputs(seed: int = 0) -> dict:
    key = jax.random.key(seed)
    ks = jax.random.split(key, 20)
    L, D = DEPTH, D_MODEL

    def normal(k, shape, scale):
        return jax.random.normal(k, shape, jnp.float32) * scale

    return {
        "x": normal(ks[0], (BATCH, SEQ, D), 1.0),
        "c": normal(ks[1], (BATCH, D), 1.0),
        "w_ada": normal(ks[2], (L, D, N_MOD * D), 0.5 * D ** -0.5),
        "b_ada": normal(ks[3], (L, N_MOD * D), 0.02),
        "norm1_gain": 1.0 + normal(ks[4], (L, D), 0.02),
        "norm2_gain": 1.0 + normal(ks[5], (L, D), 0.02),
        "w_in": normal(ks[6], (L, D, IN_WIDTH), D ** -0.5),
        "sb_q_gain": 1.0 + normal(ks[7], (L, HEAD_DIM), 0.02),
        "sb_k_gain": 1.0 + normal(ks[8], (L, HEAD_DIM), 0.02),
        "dil_q_gain": 1.0 + normal(ks[9], (L, HEAD_DIM), 0.02),
        "dil_k_gain": 1.0 + normal(ks[10], (L, HEAD_DIM), 0.02),
        "w_gla_a": normal(ks[11], (L, GLA_GATE_RANK, GLA_QK_W), GLA_GATE_RANK ** -0.5),
        "b_gla_a": normal(ks[12], (L, GLA_QK_W), 0.02),
        "gla_out_gain": 1.0 + normal(ks[13], (L, GLA_DV), 0.02),
        "w_br_sb": normal(ks[14], (L, SB_W, D), SB_W ** -0.5),
        "w_br_dil": normal(ks[15], (L, DIL_OUT_W, D), DIL_OUT_W ** -0.5),
        "w_br_gla": normal(ks[16], (L, GLA_V_W, D), GLA_V_W ** -0.5),
        "w_out": normal(ks[17], (L, D, D), D ** -0.5),
        "w_ffn_in": normal(ks[18], (L, D, 2 * D_FF), D ** -0.5),
        "w_ffn_out": normal(ks[19], (L, D_FF, D), D_FF ** -0.5),
    }

def first_block(x, c, w_ada, b_ada, norm1_gain, norm2_gain, w_in, sb_q_gain, sb_k_gain, dil_q_gain, dil_k_gain,
              w_gla_a, b_gla_a, gla_out_gain, w_br_sb, w_br_dil, w_br_gla, w_out, w_ffn_in, w_ffn_out):
    for l in range(DEPTH):
        mod = jax.nn.silu(c) @ w_ada[l] + b_ada[l]
        shift1, scale1, gate1, shift2, scale2, gate2 = jnp.split(mod[:, None, :], N_MOD, axis=-1)
        h = rms_norm(x, norm1_gain[l]) * (1 + scale1) + shift1
        x = x + gate1 * mixing_sublayer(h, w_in[l], sb_q_gain[l], sb_k_gain[l], dil_q_gain[l], dil_k_gain[l],
                                        w_gla_a[l], b_gla_a[l], gla_out_gain[l],
                                        w_br_sb[l], w_br_dil[l], w_br_gla[l], w_out[l])
        h = rms_norm(x, norm2_gain[l]) * (1 + scale2) + shift2
        x = x + gate2 * swiglu(h, w_ffn_in[l], w_ffn_out[l])
    return x


D_MIX = D_MODEL
ATT_HEADS = (D_MIX // 2) // HEAD_DIM
D_ATT = ATT_HEADS * HEAD_DIM
D_RNN = D_MIX - D_ATT
RNN_BLOCKS = 8
RNN_BLOCK = D_RNN // RNN_BLOCKS
CONV_WIDTH = 4
LRU_C = 8.0
Q_BLOCK = 128
COL_Q = 0
COL_K = COL_Q + D_ATT
COL_V = COL_K + D_ATT
COL_F = COL_V + D_ATT
COL_RX = COL_F + ATT_HEADS
COL_RG = COL_RX + D_RNN
D_IN_PROJ = COL_RG + D_RNN
N_GROUPS = 4
EXPERTS_PER_GROUP = 8
N_EXPERTS = N_GROUPS * EXPERTS_PER_GROUP
TOP_K_INNER = 2
D_EXPERT = D_MODEL // 8
D_PLE = 256
FORGET_BIAS_INIT = 2.0


def rms_norm_2(x, gain):
    x32 = x.astype(jnp.float32)
    y = x32 * lax.rsqrt(jnp.mean(x32 * x32, axis=-1, keepdims=True) + EPS)
    return (y * gain.astype(jnp.float32)).astype(x.dtype)

def forgetting_attention(q, k, v, log_f):
    b, s, h, dh = q.shape
    nb = s // Q_BLOCK
    scale = dh ** -0.5
    c = jnp.cumsum(log_f, axis=1).transpose(0, 2, 1)
    kh = k.transpose(0, 2, 1, 3)
    vh = v.transpose(0, 2, 1, 3)
    q_blocks = q.transpose(0, 2, 1, 3).reshape(b, h, nb, Q_BLOCK, dh).transpose(2, 0, 1, 3, 4)
    c_blocks = c.reshape(b, h, nb, Q_BLOCK).transpose(2, 0, 1, 3)
    k_pos = jnp.arange(s, dtype=jnp.int32)
    starts = jnp.arange(nb, dtype=jnp.int32) * Q_BLOCK

    def one_block(args):
        qb, cb, start = args
        logits = jnp.einsum('bhqd,bhkd->bhqk', qb, kh,
                            preferred_element_type=jnp.float32) * scale
        logits = logits + cb[..., :, None] - c[:, :, None, :]
        q_pos = start + jnp.arange(Q_BLOCK, dtype=jnp.int32)
        causal = k_pos[None, :] <= q_pos[:, None]
        logits = jnp.where(causal, logits, -jnp.inf)
        probs = jax.nn.softmax(logits, axis=-1)
        return jnp.einsum('bhqk,bhkd->bhqd', probs.astype(vh.dtype), vh)

    out = lax.map(one_block, (q_blocks, c_blocks, starts))
    return out.transpose(1, 0, 3, 2, 4).reshape(b, s, h * dh)

def causal_depthwise_conv(x, w, bias):
    y = lax.conv_general_dilated(
        x, w[:, None, :].astype(x.dtype), window_strides=(1,),
        padding=[(CONV_WIDTH - 1, 0)],
        dimension_numbers=('NWC', 'WIO', 'NWC'),
        feature_group_count=x.shape[-1])
    return y + bias

def rg_lru(x, w_a, b_a, w_i, b_i, lam):
    b, s, d = x.shape
    xb = x.reshape(b, s, RNN_BLOCKS, RNN_BLOCK)
    r = jax.nn.sigmoid(jnp.einsum('bsni,nij->bsnj', xb, w_a).reshape(b, s, d) + b_a)
    i = jax.nn.sigmoid(jnp.einsum('bsni,nij->bsnj', xb, w_i).reshape(b, s, d) + b_i)
    log_a = -LRU_C * r.astype(jnp.float32) * jax.nn.softplus(-lam.astype(jnp.float32))
    a = jnp.exp(log_a)
    u = jnp.sqrt(-jnp.expm1(2.0 * log_a)) * (i * x).astype(jnp.float32)

    def combine(left, right):
        a1, b1 = left
        a2, b2 = right
        return a1 * a2, a2 * b1 + b2

    _, h = lax.associative_scan(combine, (a, u), axis=1)
    return h.astype(x.dtype)

def hierarchical_moe(hn, w_router_group, w_router_expert, w_gate, w_up, w_down):
    b, s, d = hn.shape
    t = hn.reshape(b * s, d)
    g_probs = jax.nn.softmax(jnp.dot(t, w_router_group, preferred_element_type=jnp.float32), axis=-1)
    g_w, g_idx = lax.top_k(g_probs, 1)
    e_logits = jnp.dot(t, w_router_expert, preferred_element_type=jnp.float32)
    e_logits = e_logits.reshape(-1, N_GROUPS, EXPERTS_PER_GROUP)
    e_in_group = jnp.take_along_axis(e_logits, g_idx[:, :, None], axis=1)[:, 0]
    top_l, top_i = lax.top_k(e_in_group, TOP_K_INNER)
    weights = jax.nn.softmax(top_l, axis=-1) * g_w
    ids = g_idx * EXPERTS_PER_GROUP + top_i
    comb = jnp.sum(jax.nn.one_hot(ids, N_EXPERTS, dtype=jnp.float32) * weights[..., None], axis=1)
    out = jnp.zeros((b * s, d), jnp.float32)
    for e in range(N_EXPERTS):
        hid = jax.nn.silu(t @ w_gate[e]) * (t @ w_up[e])
        out = out + (hid @ w_down[e]).astype(jnp.float32) * comb[:, e:e + 1]
    return out.astype(hn.dtype).reshape(b, s, d)

def second_inputs(seed: int = 0) -> dict:
    key = jax.random.key(seed)
    ks = jax.random.split(key, 32)
    f32 = jnp.float32

    def nrm(k, shape, scale):
        return jax.random.normal(k, shape, f32) * scale

    def gain(k, shape):
        return 1.0 + 0.02 * jax.random.normal(k, shape, f32)

    u = jax.random.uniform(ks[12], (DEPTH, D_RNN), f32, 0.9, 0.999)
    s_lam = u ** (1.0 / LRU_C)
    lru_lambda = jnp.log(s_lam) - jnp.log1p(-s_lam)
    return {
        "x": nrm(ks[0], (BATCH, SEQ, D_MODEL), 1.0),
        "p": nrm(ks[1], (DEPTH, BATCH, SEQ, D_PLE), 1.0),
        "mix_norm": gain(ks[2], (DEPTH, D_MODEL)),
        "w_in": nrm(ks[3], (DEPTH, D_MODEL, D_IN_PROJ), D_MODEL ** -0.5),
        "b_forget": FORGET_BIAS_INIT + 0.1 * jax.random.normal(ks[4], (DEPTH, ATT_HEADS), f32),
        "q_norm": gain(ks[5], (DEPTH, HEAD_DIM)),
        "k_norm": gain(ks[6], (DEPTH, HEAD_DIM)),
        "conv_w": nrm(ks[7], (DEPTH, CONV_WIDTH, D_RNN), CONV_WIDTH ** -0.5),
        "conv_b": nrm(ks[8], (DEPTH, D_RNN), 0.02),
        "w_rec_gate": nrm(ks[9], (DEPTH, RNN_BLOCKS, RNN_BLOCK, RNN_BLOCK), RNN_BLOCK ** -0.5),
        "b_rec_gate": nrm(ks[10], (DEPTH, D_RNN), 0.02),
        "w_in_gate": nrm(ks[11], (DEPTH, RNN_BLOCKS, RNN_BLOCK, RNN_BLOCK), RNN_BLOCK ** -0.5),
        "b_in_gate": nrm(ks[13], (DEPTH, D_RNN), 0.02),
        "lru_lambda": lru_lambda,
        "w_out": nrm(ks[14], (DEPTH, D_MIX, D_MODEL), D_MIX ** -0.5),
        "ffn_norm": gain(ks[15], (DEPTH, D_MODEL)),
        "w_router_group": nrm(ks[16], (DEPTH, D_MODEL, N_GROUPS), D_MODEL ** -0.5),
        "w_router_expert": nrm(ks[17], (DEPTH, D_MODEL, N_EXPERTS), D_MODEL ** -0.5),
        "w_expert_gate": nrm(ks[18], (DEPTH, N_EXPERTS, D_MODEL, D_EXPERT), D_MODEL ** -0.5),
        "w_expert_up": nrm(ks[19], (DEPTH, N_EXPERTS, D_MODEL, D_EXPERT), D_MODEL ** -0.5),
        "w_expert_down": nrm(ks[20], (DEPTH, N_EXPERTS, D_EXPERT, D_MODEL), D_EXPERT ** -0.5),
        "ple_norm": gain(ks[21], (DEPTH, D_MODEL)),
        "w_ple_gate": nrm(ks[22], (DEPTH, D_MODEL, D_MODEL), D_MODEL ** -0.5),
        "w_ple_up": nrm(ks[23], (DEPTH, D_PLE, D_MODEL), D_PLE ** -0.5),
    }

def second_block(x, p, mix_norm, w_in, b_forget, q_norm, k_norm, conv_w, conv_b,
              w_rec_gate, b_rec_gate, w_in_gate, b_in_gate, lru_lambda, w_out,
              ffn_norm, w_router_group, w_router_expert, w_expert_gate,
              w_expert_up, w_expert_down, ple_norm, w_ple_gate, w_ple_up):
    h = x
    b, s, _ = x.shape
    for i in range(DEPTH):
        hn = rms_norm_2(h, mix_norm[i])
        proj = hn @ w_in[i]
        q = rms_norm_2(proj[..., COL_Q:COL_K].reshape(b, s, ATT_HEADS, HEAD_DIM), q_norm[i])
        k = rms_norm_2(proj[..., COL_K:COL_V].reshape(b, s, ATT_HEADS, HEAD_DIM), k_norm[i])
        v = proj[..., COL_V:COL_F].reshape(b, s, ATT_HEADS, HEAD_DIM)
        log_f = jax.nn.log_sigmoid((proj[..., COL_F:COL_RX] + b_forget[i]).astype(jnp.float32))
        att_out = forgetting_attention(q, k, v, log_f)

        rx = causal_depthwise_conv(proj[..., COL_RX:COL_RG], conv_w[i], conv_b[i])
        rnn = rg_lru(rx, w_rec_gate[i], b_rec_gate[i], w_in_gate[i], b_in_gate[i], lru_lambda[i])
        rnn_out = jax.nn.gelu(proj[..., COL_RG:D_IN_PROJ], approximate=True) * rnn

        h = h + jnp.concatenate([att_out, rnn_out], axis=-1) @ w_out[i]

        hn = rms_norm_2(h, ffn_norm[i])
        h = h + hierarchical_moe(hn, w_router_group[i], w_router_expert[i],
                                 w_expert_gate[i], w_expert_up[i], w_expert_down[i])

        gate = jax.nn.sigmoid(rms_norm_2(h, ple_norm[i]) @ w_ple_gate[i])
        h = h + gate * (p[i] @ w_ple_up[i])
    return h


def setup_inputs(seed=0):
    out = dict(first_inputs(seed))
    for name, value in second_inputs(seed + 1).items():
        if name != "x":
            out[name + "_2"] = value
    return out


def reference(
    x, c, w_ada, b_ada, norm1_gain, norm2_gain, w_in, sb_q_gain, sb_k_gain, dil_q_gain,
    dil_k_gain, w_gla_a, b_gla_a, gla_out_gain, w_br_sb, w_br_dil, w_br_gla, w_out, w_ffn_in,
    w_ffn_out, p_2, mix_norm_2, w_in_2, b_forget_2, q_norm_2, k_norm_2, conv_w_2, conv_b_2,
    w_rec_gate_2, b_rec_gate_2, w_in_gate_2, b_in_gate_2, lru_lambda_2, w_out_2, ffn_norm_2,
    w_router_group_2, w_router_expert_2, w_expert_gate_2, w_expert_up_2, w_expert_down_2,
    ple_norm_2, w_ple_gate_2, w_ple_up_2,
):
    x = first_block(
        x, c, w_ada, b_ada, norm1_gain, norm2_gain, w_in, sb_q_gain, sb_k_gain, dil_q_gain,
        dil_k_gain, w_gla_a, b_gla_a, gla_out_gain, w_br_sb, w_br_dil, w_br_gla, w_out,
        w_ffn_in, w_ffn_out,
    )
    return second_block(
        x, p_2, mix_norm_2, w_in_2, b_forget_2, q_norm_2, k_norm_2, conv_w_2, conv_b_2,
        w_rec_gate_2, b_rec_gate_2, w_in_gate_2, b_in_gate_2, lru_lambda_2, w_out_2, ffn_norm_2,
        w_router_group_2, w_router_expert_2, w_expert_gate_2, w_expert_up_2, w_expert_down_2,
        ple_norm_2, w_ple_gate_2, w_ple_up_2,
    )


_drawn_inputs = setup_inputs


def setup_inputs(seed=0):
    import zlib

    import numpy as np

    out = dict(_drawn_inputs(seed))
    spreads = {}
    factors = {'norm2_gain': 3.123,
     'sb_q_gain': 8.0,
     'sb_k_gain': 8.0,
     'dil_q_gain': 8.0,
     'dil_k_gain': 8.0,
     'b_gla_a': 8.0,
     'gla_out_gain': 8.0,
     'q_norm_2': 6.019,
     'k_norm_2': 8.0,
     'b_rec_gate_2': 8.0,
     'b_in_gate_2': 7.652,
     'ffn_norm_2': 3.129,
     'ple_norm_2': 8.0}
    for name, (base, spread) in spreads.items():
        noise = np.random.default_rng([zlib.crc32(name.encode()), seed]).standard_normal(out[name].shape)
        drawn = base * np.exp(spread * noise) if base else spread * noise
        out[name] = __import__('jax').numpy.asarray(drawn.astype(out[name].dtype))
    for name, factor in factors.items():
        out[name] = (out[name] * factor).astype(out[name].dtype)
    return out
```

```python
import concourse.bass as bass
from concourse import mybir
from contextlib import ExitStack
import numpy as np

F32 = mybir.dt.float32
F32R = mybir.dt.float32r
ACT = mybir.ActivationFunctionType
ALU = mybir.AluOpType
AX = mybir.AxisListType

P = 128
D = 2048
TB = 2
DC = D // P
COLS = 512
EPS = 1e-6
DH = 128
QSCALE = DH ** -0.5
SB_HEADS, DIL_SLOTS, DIL_GROUPS, GLA_HEADS, FOX_HEADS = 6, 2, 3, 4, 8
DILATION = (1, 4, 16)
DV = 256
N_GLA = GLA_HEADS * DV
RNN_CHUNKS = 8
CONV_W = 4
D_FF = 5632
N_EXPERTS, EXPERTS_PER_GROUP, N_ROUTE_GROUPS = 32, 8, 4
HID = 256
FFN_PARTS = D_FF // HID
BIG_NEG = -1.0e30

PROJ1 = 7680
A_COL = PROJ1
GATE_COL = A_COL + 16
PROJ2_QKV, F_COLS = 3072, 8
PROJ2 = 5120

V_BADA, V_N1, V_N2, V_MIX, V_PLE, V_CB, V_BR, V_BI, V_LAM, V_CW = 0, 96, 112, 128, 144, 160, 168, 176, 184, 192
V_SBQ, V_SBK, V_DQ, V_DK, V_FQ, V_FK, V_GG, V_C = 224, 225, 226, 227, 228, 229, 230, 232
V_ALL = 248

C_ID, C_U, C_STRICT, C_STRICTNEG, C_CAUSNEG, C_TRI, C_R, C_GMASK, C_DIL = 0, 128, 256, 384, 512, 640, 768, 1152, 1216
C_ALL = C_DIL + 2 * 3 * 384


def shape_constants():
    c = np.zeros((P, C_ALL), np.float32)
    i = np.arange(P)[:, None]
    j = np.arange(P)[None, :]
    c[:, C_ID:C_ID + P] = i == j
    c[:, C_U:C_U + P] = np.where(i >= j, 1.0, 0.0)
    c[:, C_STRICT:C_STRICT + P] = i < j
    c[:, C_STRICTNEG:C_STRICTNEG + P] = np.where(i < j, 0.0, BIG_NEG)
    c[:, C_CAUSNEG:C_CAUSNEG + P] = np.where(j <= i, 0.0, BIG_NEG)
    c[:, C_TRI:C_TRI + P] = i <= j
    same = (i // 64) == (j // 64)
    mid = (j // 64) * 64 + 31
    c[:, C_R:C_R + P] = (same & (i <= j)) / 16.0
    c[:, C_R + P:C_R + 2 * P] = ((same & (i <= j)) * 1.0 - (same & (i <= mid)) * 1.0) / 16.0
    c[:, C_R + 2 * P:C_R + 3 * P] = (same & (i > j)) / 16.0
    jj = np.arange(64)[None, :]
    c[:, C_GMASK:C_GMASK + 64] = (i % 64) <= jj
    n_heads = 2 * 3
    for slot in range(2):
        for g in range(3):
            head = g * 2 + slot
            slope = np.float32(2.0 ** (-8.0 * (head + 1) / n_heads))
            dil = DILATION[g]

            def bias(t, s):
                d = t - s
                ok = (d >= 0) & (d % dil == 0) & (d // dil <= 128)
                return np.where(ok, -slope * d, BIG_NEG)
            at = C_DIL + (slot * 3 + g) * 384
            c[:, at:at + 128] = bias(i, j)
            c[:, at + 128:at + 384] = bias(i + 128, np.arange(256)[None, :])
    return c


def program(nc, I, out):
    ctx = ExitStack()
    with ctx:
        def sb(name, shape, dt=F32):
            return ctx.enter_context(nc.sbuf_tensor(name, shape, dt))

        sems = {}

        def S(name):
            if name not in sems:
                sems[name] = ctx.enter_context(nc.semaphore(name))
            return sems[name]

        raw = sb("raw", [P, 8, 2, COLS])
        whi = sb("whi", [P, 4, 2, COLS], F32R)
        wlo = sb("wlo", [P, 4, 2, COLS], F32R)
        ahi = sb("ahi", [P, DC, TB * P], F32R)
        alo = sb("alo", [P, DC, TB * P], F32R)
        bhi = sb("bhi", [P, DC, TB * P], F32R)
        blo = sb("blo", [P, DC, TB * P], F32R)
        xres = sb("xres", [P, TB, D])
        big = sb("big", [P, TB * PROJ1])
        ident = sb("ident", [P, P])
        ones = sb("ones", [P, 2 * P])
        vec = sb("vec", [P, V_ALL])
        modt = sb("modt", [P, 96])
        gain_ffn2 = sb("gain_ffn2", [P, DC])
        geff = sb("geff", [P, DC])
        stat = sb("stat", [P, 64])
        silu_c = sb("silu_c", [P, DC])
        gl_a16 = sb("gl_a16", [P, TB * 16])
        seed = sb("seed", [P, 4])
        bank = [ctx.enter_context(nc.psum_tensor(f"bank{i}", [P, COLS], F32)) for i in range(8)]

        xf = xres[:].rearrange("p b n -> p (b n)")

        def region(base, off, n):
            return base[:, off:off + n]

        landed = [S(f"raw_landed{i}") for i in range(8)]
        landed_up = [S(f"raw_up_landed{i}") for i in range(8)]
        hi_ready = S("hi_ready")
        lo_ready = S("lo_ready")
        tile_used = S("tile_used")
        evac_act = S("evac_act")
        evac_dve = S("evac_dve")
        ENG = ("pe", "act", "dve")
        stage_sem = {e: S(f"stage_{e}") for e in ENG}
        stage_no = {e: 0 for e in ENG}
        T_ADA = 24 * 8

        def stage_end(eng, key):
            eng.drain().then_inc(stage_sem[key], 1)
            stage_no[key] += 1
            for e in ENG:
                if e != key:
                    eng.wait_ge(stage_sem[e], stage_no[key])

        def wait_stage(eng, n, keys=ENG):
            for e in keys:
                eng.wait_ge(stage_sem[e], n)

        class Chain:

            def __init__(self, eng, name):
                self.eng, self.sem, self.n = eng, S(name), 0

            def step(self, ins):
                ins.then_inc(self.sem, 1)
                self.n += 1
                self.eng.wait_ge(self.sem, self.n)

        (ST_LOAD, ST_ADA, ST_NORM1, ST_PROJ1, ST_SB, ST_DIL, ST_GLA, ST_BRANCH, ST_YT, ST_OUT1, ST_NORM2, ST_FFN,
         ST_NORM3, ST_PROJ2, ST_FOX, ST_RNN, ST_OUT2, ST_NORM4, ST_MOE, ST_NORM5, ST_PLE) = range(1, 22)

        t_proj1 = T_ADA
        t_branch = t_proj1 + 15 * 8
        t_out1 = t_branch + 4 * 32
        t_ffn = t_out1 + 4 * 8
        t_proj2 = t_ffn + 22 * 8 + 8 * 8 + 4 * 6
        t_out2 = t_proj2 + 10 * 8
        t_moe = t_out2 + 4 * 8
        t_ple = t_moe + 4 * 12 * 8
        n_proj1, n_branch = 0, 15
        n_out1 = n_branch + 24
        n_ffn = n_out1 + 4
        n_proj2 = n_ffn + 22 + 12
        n_out2 = n_proj2 + 10
        n_moe = n_out2 + 4
        n_ple = n_moe + 48

        def drive(eng, groups, tiles, tile, events=None, follow=None, prologue=True):
            events = events or {}
            if prologue:
                for k in range(4):
                    tile(k, 0, 0)

            def body(g, par, last):
                for k in range(4, tiles + 4):
                    if k < tiles:
                        tile(k, g, par)
                    elif not last:
                        tile(k - tiles, g + 1, 1 - par)
                    elif follow:
                        follow(k - tiles)
                    if k in events:
                        events[k](g, par)
            pairs = (groups - 1) // 2
            if pairs > 0:
                with eng.Fori(0, pairs) as i:
                    body(i * 2, 0, False)
                    body(i * 2 + 1, 1, False)
            for g in range(2 * pairs, groups):
                body(g, g % 2, g == groups - 1)

        def nat(w):
            return w.rearrange("(k p) n -> p k n", p=P)

        w_ada_v = nat(I["w_ada"])
        w_in_v = nat(I["w_in"])
        w_out_v = nat(I["w_out"])
        w_in2_v = nat(I["w_in_2"])
        w_out2_v = nat(I["w_out_2"])
        w_ple_v = nat(I["w_ple_gate_2"])
        w_up_v = nat(I["w_ple_up_2"])
        br_v = [nat(I["w_br_sb"]), nat(I["w_br_dil"]), nat(I["w_br_gla"])]
        BR_TILES = (3, 1, 4)
        ffn_in_v = I["w_ffn_in"].rearrange("(k p) (h n) -> p k h n", p=P, h=2)
        ffn_out_v = nat(I["w_ffn_out"])
        eg_v = I["w_expert_gate_2"].rearrange("e (p k) n -> p e k n", k=DC)
        eu_v = I["w_expert_up_2"].rearrange("e (p k) n -> p e k n", k=DC)
        ed_v = I["w_expert_down_2"].rearrange("e (k p) n -> p e k n", p=P)

        block = ctx.enter_context(nc.Block())

        @block.sync
        def _(sp):
            def slot_free(t, r):
                if isinstance(r, int):
                    if t + 8 * r >= 8:
                        sp.wait_ge(lo_ready, t + 8 * r - 7)
                else:
                    sp.wait_ge(lo_ready, r * 8 + (t - 7))

            def load(t, src, r=0):
                sp.lower_ap_dma(src)
                slot_free(t, r)
                sp.dma_start(raw[:, t % 8], src).then_inc(landed[t % 8], 16)

            sp.dma_start(ident[:], I["consts"][:, C_ID:C_ID + P]).then_inc(S("small_landed"), 16)
            vrows = region(big, 0, 3 * P)
            r1 = lambda name, k: I[name].rearrange("(k p) -> k p", p=P)
            rows = [(0, 0, "b_ada", 96), (1, 0, "norm1_gain", 16), (1, 16, "norm2_gain", 16), (1, 32, "mix_norm_2", 16),
                    (1, 48, "ple_norm_2", 16), (1, 64, "conv_b_2", 8), (1, 72, "b_rec_gate_2", 8),
                    (1, 80, "b_in_gate_2", 8), (1, 88, "lru_lambda_2", 8),
                    (2, 0, "sb_q_gain", 1), (2, 1, "sb_k_gain", 1), (2, 2, "dil_q_gain", 1), (2, 3, "dil_k_gain", 1),
                    (2, 4, "q_norm_2", 1), (2, 5, "k_norm_2", 1), (2, 6, "gla_out_gain", 2), (2, 8, "c", 16)]
            for tile_no, at, name, k in rows:
                sp.dma_start(vrows[at:at + k, tile_no * P:(tile_no + 1) * P], r1(name, k)).then_inc(S("small_landed"), 16)
            sp.dma_start(vrows[96:128, P:2 * P], I["conv_w_2"].rearrange("w (k p) -> (w k) p", p=P))\
              .then_inc(S("small_landed"), 16)
            sp.dma_start(gain_ffn2[:], I["ffn_norm_2"].rearrange("(p k) -> p k", k=DC)).then_inc(S("small_landed"), 16)

            for s in range(8):
                load(s, w_ada_v[:, 2 * s:2 * s + 2, 0:COLS])
            sp.dma_start(xres[:], I["x"].rearrange("(b p) n -> p b n", p=P)).then_inc(S("x_landed"), 16)
            with sp.Fori(1, 24) as g:
                for s in range(8):
                    load(s, w_ada_v[:, 2 * s:2 * s + 2, bass.ds(g * COLS, COLS)], g)
            with sp.Fori(0, 15) as g:
                for s in range(8):
                    load(t_proj1 + s, w_in_v[:, 2 * s:2 * s + 2, bass.ds(g * COLS, COLS)], g)
            with sp.Fori(0, 4) as g:
                k = 0
                for i in range(3):
                    for s in range(8):
                        load(t_branch + k, w_in_v[:, 2 * s:2 * s + 2, bass.ds(g * COLS + (GATE_COL + i * D), COLS)],
                             g * 4)
                        k += 1
                    for s in range(BR_TILES[i]):
                        load(t_branch + k, br_v[i][:, 2 * s:2 * s + 2, bass.ds(g * COLS, COLS)], g * 4)
                        k += 1
            with sp.Fori(0, 4) as g:
                for s in range(8):
                    load(t_out1 + s, w_out_v[:, 2 * s:2 * s + 2, bass.ds(g * COLS, COLS)], g)

            def ffn_in_tile(t, s, part, r=0):
                slot_free(t, r)
                for half, sem in ((0, landed), (1, landed_up)):
                    sp.dma_start(raw[:, t % 8, :, half * HID:(half + 1) * HID],
                                 ffn_in_v[:, 2 * s:2 * s + 2, half, bass.ds(part * HID, HID)]).then_inc(sem[t % 8], 16)
            with sp.Fori(0, 2) as rnd:
                with sp.Fori(0, 8) as e:
                    for s in range(8):
                        ffn_in_tile(t_ffn + s, s, rnd * 8 + e, rnd * 12 + e)
                with sp.Fori(0, 4) as g:
                    for s in range(8):
                        load(t_ffn + 64 + s, ffn_out_v[:, bass.ds(rnd * 16 + 2 * s, 2), bass.ds(g * COLS, COLS)],
                             rnd * 12 + g)
            t = t_ffn + 192
            with sp.Fori(0, 6) as e:
                for s in range(8):
                    ffn_in_tile(t + s, s, e + 16, e)
            for g in range(4):
                for s in range(6):
                    load(t + 48 + 6 * g + s, ffn_out_v[:, 32 + 2 * s:34 + 2 * s, g * COLS:(g + 1) * COLS])

            with sp.Fori(0, 6) as g:
                for s in range(8):
                    load(t_proj2 + s, w_in2_v[:, 2 * s:2 * s + 2, bass.ds(g * COLS, COLS)], g)
            with sp.Fori(0, 4) as g:
                for s in range(8):
                    load(t_proj2 + 48 + s,
                         w_in2_v[:, 2 * s:2 * s + 2, bass.ds(g * COLS + (PROJ2_QKV + F_COLS), COLS)], g)
            with sp.Fori(0, 4) as g:
                for s in range(8):
                    load(t_out2 + s, w_out2_v[:, 2 * s:2 * s + 2, bass.ds(g * COLS, COLS)], g)

            with sp.Fori(0, 4) as rnd:
                with sp.Fori(0, 8) as e:
                    for s in range(8):
                        t = t_moe + s
                        slot_free(t, rnd * 12 + e)
                        for half, v, sem in ((0, eg_v, landed), (1, eu_v, landed_up)):
                            src = v[:, bass.ds(rnd * 8 + e, 1), 2 * s:2 * s + 2, :].rearrange("p e k n -> p (e k) n")
                            sp.dma_start(raw[:, t % 8, :, half * HID:(half + 1) * HID], src).then_inc(sem[t % 8], 16)
                with sp.Fori(0, 4) as g:
                    for s in range(8):
                        src = ed_v[:, bass.ds(rnd * 8 + s, 1), :, bass.ds(g * COLS, COLS)]
                        load(t_moe + 64 + s, src.rearrange("p e k n -> p (e k) n"), rnd * 12 + g)

            for g in range(4):
                for s in range(8):
                    load(t_ple + 9 * g + s, w_ple_v[:, 2 * s:2 * s + 2, g * COLS:(g + 1) * COLS])
                load(t_ple + 9 * g + 8, w_up_v[:, 0:2, g * COLS:(g + 1) * COLS])
            for g in range(4):
                sp.wait_ge(evac_dve, 2 + n_ple + 2 * g + 2)
                sp.dma_start(out.rearrange("(b p) n -> p b n", p=P)[:, :, g * COLS:(g + 1) * COLS],
                             xres[:, :, g * COLS:(g + 1) * COLS]).then_inc(S(f"stored{g}"), 16)
            for g in range(4):
                sp.wait_ge(S(f"stored{g}"), 16)

        X_QKT, X_L, X_ZS, X_SBC = 0, 1024, 1792, 3328
        X_L2, X_PT = 1024, 3328
        proj1 = big[:].rearrange("p (b n) -> p b n", b=TB)
        proj2 = big[:, 0:TB * PROJ2].rearrange("p (b n) -> p b n", b=TB)
        T2 = TB * PROJ2
        side1 = region(xf, 0, DC * 16).rearrange("p (k n) -> p k n", k=DC)
        side2 = region(big, T2, DC * 8).rearrange("p (k n) -> p k n", k=DC)
        route = region(big, 8192, DC * 36).rearrange("p (k n) -> p k n", k=DC)
        dil_mask = [proj1[:, j, 0:3 * 384].rearrange("p (h n) -> p h n", h=3) for j in range(2)]
        G_R, G_MASK, G_W, G_B, G_AT, G_OG = 0, 384, 448, 960, 1472, 1728
        F_QKT, F_L, F_PT, F_CROW, F_NEGROW, F_CAUS, F_U = (T2, T2 + 1024, T2 + 1792, T2 + 2560, T2 + 4608,
                                                            T2 + 4736, T2 + 4864)
        F_BF = T2 + 4992
        R_RXP, R_W = T2, T2 + 2080

        @block.gpsimd
        def _(pool):
            def fetch(name, dst, src):
                pool.dma_start(dst, src).then_inc(S(name), 16)

            wait_stage(pool, ST_NORM1)
            fetch("side1_landed", side1, w_in_v[:, :, A_COL:A_COL + 16])
            wait_stage(pool, ST_PROJ1)
            fetch("sbc_landed", region(xf, X_SBC, 3 * P), I["consts"][:, C_U:C_U + 3 * P])
            wait_stage(pool, ST_SB)
            for j in range(2):
                at = C_DIL + j * 3 * 384
                fetch("dmask_landed", proj1[:, j, 0:3 * 384], I["consts"][:, at:at + 3 * 384])
            wait_stage(pool, ST_DIL)
            fetch("glac_landed", region(xf, G_R, 448), I["consts"][:, C_R:C_R + 448])
            fetch("glac_landed", xf[0:16, G_W:G_W + 512], I["w_gla_a"])
            fetch("glac_landed", xf[0:1, G_B:G_B + 512], I["b_gla_a"].rearrange("(a n) -> a n", a=1))
            wait_stage(pool, ST_GLA)
            fetch("x_back", xres[:], I["x"].rearrange("(b p) n -> p b n", p=P))
            wait_stage(pool, ST_NORM3)
            fetch("side2_landed", side2, w_in2_v[:, :, PROJ2_QKV:PROJ2_QKV + F_COLS])
            fetch("side2_landed", big[0:1, F_BF:F_BF + 8], I["b_forget_2"].rearrange("(a n) -> a n", a=1))
            wait_stage(pool, ST_PROJ2)
            fetch("foxc_landed", region(big, F_CAUS, 2 * P), I["consts"][:, C_CAUSNEG:C_CAUSNEG + 2 * P])
            wait_stage(pool, ST_FOX)
            wrec = region(big, R_W, 2048).rearrange("p (g k n) -> p g k n", g=2, k=RNN_CHUNKS)
            fetch("wrec_landed", wrec[:, 0], I["w_rec_gate_2"].rearrange("k p n -> p k n"))
            fetch("wrec_landed", wrec[:, 1], I["w_in_gate_2"].rearrange("k p n -> p k n"))
            wait_stage(pool, ST_NORM4)
            fetch("route_landed", route[:, :, 0:4], I["w_router_group_2"].rearrange("(p k) n -> p k n", k=DC))
            fetch("route_landed", route[:, :, 4:36], I["w_router_expert_2"].rearrange("(p k) n -> p k n", k=DC))
            wait_stage(pool, ST_MOE)
            fetch("p_landed", region(big, 0, 512).rearrange("p (b n) -> p b n", b=TB),
                  I["p_2"].rearrange("(b p) n -> p b n", p=P))

        vrows = region(big, 0, 3 * P)
        acc = region(big, 1024, 2 * COLS).rearrange("p (r n) -> p r n", r=2)
        N_JUNK, N_XN = 4096, 8192
        junk = region(big, N_JUNK, D)
        xn = region(big, N_XN, TB * D).rearrange("p (b n) -> p b n", b=TB)
        htmp = region(big, 14336, 4 * TB * P).rearrange("p (r n) -> p r n", r=4)
        gate_bc = region(big, 6144, D)
        gate_dg = region(big, 12288, D)
        ysum = region(big, 0, TB * D).rearrange("p (b n) -> p b n", b=TB)
        gsig = region(big, TB * D, 3 * TB * COLS).rearrange("p (i b n) -> p i b n", i=3, b=TB)
        ymul = region(big, TB * D + 3 * TB * COLS, TB * COLS).rearrange("p (b n) -> p b n", b=TB)
        silu_g = region(big, 0, TB * HID).rearrange("p (b n) -> p b n", b=TB)
        hid = region(big, 512, TB * HID).rearrange("p (b n) -> p b n", b=TB)
        prod = region(big, 1024, TB * COLS).rearrange("p (b n) -> p b n", b=TB)
        comb = region(big, 2048 + 2048, TB * N_EXPERTS).rearrange("p (b n) -> p b n", b=TB)
        rt = region(big, 4352, 1024)

        GATE_NO = {"g1": 1, "g2": 2, "n1": 1, "n2": 2}
        NORMS = {
            "n1": dict(no=0, stats=0, src=xres, gain=geff, bias=modt[:, 0:16], norm=True),
            "y": dict(no=1, src=ysum, gain=None, bias=None, norm=False),
            "n2": dict(no=2, stats=1, src=xres, gain=geff, bias=modt[:, 48:64], norm=True),
            "n3": dict(no=3, stats=2, src=xres, gain=vec[:, V_MIX:V_MIX + 16], bias=None, norm=True),
            "n4": dict(no=4, stats=3, src=xres, gain=gain_ffn2[:], bias=None, norm=True, strided=True),
            "n5": dict(no=5, stats=4, src=xres, gain=vec[:, V_PLE:V_PLE + 16], bias=None, norm=True),
        }

        def att_cols(kind, h):
            if kind == "sb":
                return proj1, h * DH, 768 + h * DH, 1536 + h * DH
            if kind == "dil":
                return proj1, 2304 + h * DH, 3072 + h * DH, 3840 + h * DH
            return proj2, h * DH, 1024 + h * DH, 2048 + h * DH

        HEAD0 = {"sb": 0, "dil": 0, "fox": 6}
        UNIT0 = {"sb": 0, "dil": 0, "fox": 2}
        NORM_NO = {"sb": 0, "fox": 1}

        def att(kind):
            return "sb" if kind == "sb" else "att"

        ATT = {
            "dil": dict(units=DIL_SLOTS, per=DIL_GROUPS, head=lambda u, i: i * 2 + u, qkt=region(xf, X_QKT, 1024),
                        logit=region(xf, X_L2, 2304), pt=region(xf, X_PT, 768), dst=6),
            "fox": dict(units=FOX_HEADS, per=1, head=lambda u, i: u, qkt=region(big, F_QKT, 1024),
                        logit=region(big, F_L, 768), pt=region(big, F_PT, 768), dst=0),
        }
        for a in ATT.values():
            a["qkt"] = a["qkt"].rearrange("p (r i n) -> p r i n", r=2, i=2)
            a["logit"] = a["logit"].rearrange("p (r h n) -> p r h n", r=2, h=a["per"])
            a["pt"] = a["pt"].rearrange("p (r n) -> p r n", r=2)
        qkt_sb = region(xf, X_QKT, 1024).rearrange("p (r i n) -> p r i n", r=2, i=2)
        l_sb = region(xf, X_L, 768).rearrange("p (r n) -> p r n", r=2)
        z_sb = region(xf, X_ZS, 768).rearrange("p (r n) -> p r n", r=2)
        u_tri, strict, strictneg = (region(xf, X_SBC + i * P, P) for i in range(3))
        negones = region(xf, X_SBC + 3 * P, P)
        negtri = region(xf, X_SBC + 4 * P, P)
        SQ1 = region(xf, 256, 3072).rearrange("p (r n) -> p r n", r=2)
        SQ2F = region(big, T2, 2048).rearrange("p (r n) -> p r n", r=2)
        f_logit = stat[:, 48:64].rearrange("p (b n) -> p b n", b=TB)

        A0, A1 = proj1[:, 0, 0:4608], proj1[:, 1, 0:4608]
        gl_ls = A0[:, 0:1024].rearrange("p (b n) -> p b n", b=TB)
        gl_qm = A0[:, 1024:2048].rearrange("p (h n) -> p h n", h=4)
        gl_km = A0[:, 2048:3072].rearrange("p (h n) -> p h n", h=4)
        gl_qc = A0[:, 3072:4096].rearrange("p (h n) -> p h n", h=4)
        gl_sc = A0[:, 4096:4608].rearrange("p (s n) -> p s n", s=8)
        gl_kd = A1[:, 0:1024].rearrange("p (b n) -> p b n", b=TB)
        gl_st = A1[:, 1024:3072].rearrange("p (r h n) -> p r h n", r=2, h=4)
        gl_ex = A1[:, 3072:4608].rearrange("p (r e n) -> p r e n", r=2, e=3)
        gl_og = region(xf, G_OG, 2048).rearrange("p (b n) -> p b n", b=TB)
        gl_tmp = region(xf, G_OG, 1024).rearrange("p (b n) -> p b n", b=TB)
        gl_a = gl_a16[:].rearrange("p (b n) -> p b n", b=TB)
        gl_sq = A0[:, 0:2048].rearrange("p (b n) -> p b n", b=TB)
        gl_htmp = A0[:, 2048:3072].rearrange("p (r n) -> p r n", r=4)
        gl_at = xf[0:16, G_AT:G_AT + 256]
        gl_el = stat[:, 32:48].rearrange("p (h c) -> p h c", h=4)
        gl_ss = stat[:, 48:56]

        def chunks(off):
            return region(big, off, 2048).rearrange("p (k n) -> p k n", k=RNN_CHUNKS)
        r_xp = region(big, R_RXP, 2080).rearrange("p (k n) -> p k n", k=RNN_CHUNKS)
        r_xc, r_rg, r_r, r_i = chunks(0), chunks(5120), chunks(3072), chunks(8192)
        r_a = region(big, R_RXP, 2048).rearrange("p (k n) -> p k n", k=RNN_CHUNKS)
        r_t = chunks(R_W)
        r_w = region(big, R_W, 2048).rearrange("p (g k n) -> p g k n", g=2, k=RNN_CHUNKS)
        r_k8 = stat[:, 0:8]
        r_nk8 = stat[:, 8:16]

        @block.tensor
        def _(pe):
            mm = nc.tensor.matmul

            def products(t, r, parts, banks, first, last):
                pe.wait_ge(lo_ready, r * 8 + (t + 1))
                s = t % 4
                for c, (shi, slo, kc) in enumerate(parts):
                    for b in range(TB):
                        T = slice(b * P, (b + 1) * P)
                        o = bank[banks[b]][:]
                        st, en = first and c == 0, last and c == len(parts) - 1
                        mm(o, shi[:, kc, T], whi[:, s, c], start=st, stop=False)
                        mm(o, shi[:, kc, T], wlo[:, s, c], start=False, stop=False)
                        ins = mm(o, slo[:, kc, T], whi[:, s, c], start=False, stop=en)
                ins.then_inc(tile_used, 1)

            def group_free(n):
                pe.wait_ge(evac_act, n + 1)
                pe.wait_ge(evac_dve, n + 1)

            def gemm_tile(t0, n0, shi, slo, last_k=7, back=0):
                def tile(k, g, par):
                    if k == 0:
                        group_free(n0 + g)
                    products(t0 + k, g, [(shi, slo, 2 * k), (shi, slo, 2 * k + 1)], (2 * par, 2 * par + 1),
                             k == 0, k == last_k)
                return tile

            def norm(key):
                cfg = NORMS[key]
                src = xn if cfg["norm"] else cfg["src"]
                if cfg["norm"]:
                    pe.wait_ge(S("norm_xn"), 2 * cfg["stats"] + 2)
                for k in range(DC):
                    if k >= 4:
                        pe.wait_ge(S("norm_h"), 16 * cfg["no"] + k - 3)
                    for b in range(TB):
                        col = slice(k, D, DC) if cfg.get("strided") else slice(k * P, (k + 1) * P)
                        ins = nc.tensor.transpose(bank[4 + k % 4][:, b * P:(b + 1) * P], src[:, b, col], ident[:])
                    ins.then_inc(S("norm_T"), 1)

            def gate_broadcast(key):
                pe.wait_ge(S("gate_gd"), DC * GATE_NO[key])
                for q in range(4):
                    ins = mm(bank[q][:], ones[:, 0:P], gate_dg[:, q * COLS:(q + 1) * COLS], start=True, stop=True)
                ins.then_inc(S("gate_gb"), 1)

            def side(weights, n, dst, bias=None):
                for b in range(TB):
                    T = slice(b * P, (b + 1) * P)
                    o = dst[:, b * n:(b + 1) * n]
                    for k in range(DC):
                        mm(o, ahi[:, k, T].bitcast(F32), weights[:, k, :], start=(k == 0), stop=False)
                        ins = mm(o, alo[:, k, T].bitcast(F32), weights[:, k, :], start=False,
                                 stop=(k == DC - 1 and bias is None))
                    if bias is not None:
                        ins = mm(o, ones[0:1, 0:P], bias, start=False, stop=True)
                return ins

            def qk_transposes(kind, h, n):
                src, q, k, _ = att_cols(kind, h)
                if n >= 2:
                    pe.wait_ge(S(att(kind) + "_qkt"), 2 * HEAD0[kind] + 2 * (n - 1))
                for i, col in enumerate((q, k)):
                    for b in range(TB):
                        ins = nc.tensor.transpose(bank[n % 2][:, i * 256 + b * P:i * 256 + (b + 1) * P],
                                                  src[:, b, col:col + DH], ident[:])
                ins.then_inc(S(att(kind) + "_T"), 1)

            pe.wait_ge(S("small_landed"), 16 * 20)
            pe.wait_ge(S("ones_set"), 4)
            nc.tensor.transpose(bank[0][:, 0:96], vrows[0:96, 0:P], ident[0:96, 0:96])
            nc.tensor.transpose(bank[0][:, 96:224], vrows[:, P:2 * P], ident[:])
            nc.tensor.transpose(bank[0][:, 224:248], vrows[0:24, 2 * P:3 * P], ident[0:24, 0:24])\
                .then_inc(S("vec_T"), 1)
            stage_end(pe, "pe")

            def ada(g, par):
                pe.wait_ge(lo_ready, g * 8 + 8)
                pe.wait_ge(S("mod_done"), g + 1)
                for j in range(4):
                    ins = mm(bank[par][:, j:j + 1], acc[:, par, j * P:(j + 1) * P], ones[:, 0:1], start=True, stop=True)
                ins.then_inc(S("ada_cols"), 1)
            with pe.Fori(0, 12) as i:
                ada(i * 2, 0)
                ada(i * 2 + 1, 1)
            stage_end(pe, "pe")

            norm("n1")
            stage_end(pe, "pe")

            drive(pe, 15, 8, gemm_tile(t_proj1, n_proj1, ahi, alo))
            pe.wait_ge(S("side1_landed"), 16)
            side(side1, 16, bank[6]).then_inc(S("side1_done"), 1)
            stage_end(pe, "pe")

            H = SB_HEADS
            pe.wait_ge(S("sb_scaled"), 1)
            for i in range(H + 3):
                if i < H:
                    qk_transposes("sb", i, i)
                h = i - 1
                if 0 <= h < H:
                    pe.wait_ge(S("sb_qkt"), 2 * (h + 1))
                    if h >= 2:
                        pe.wait_ge(S("sb_sp"), h - 1)
                    q, k = qkt_sb[:, h % 2, 0], qkt_sb[:, h % 2, 1]
                    mm(bank[2 + h % 2][:, 0:256], k[:, 0:P], q[:, 0:256], start=True, stop=True)
                    mm(bank[2 + h % 2][:, 256:384], k[:, P:256], q[:, P:256], start=True, stop=True)\
                        .then_inc(S("sb_z"), 1)
                h = i - 2
                if 0 <= h < H:
                    pe.wait_ge(S("sb_spm"), h + 1)
                    if h >= 2:
                        pe.wait_ge(S("sb_e"), h - 1)
                    sp_, C = l_sb[:, h % 2], bank[4 + h % 2]
                    mm(C[:, 0:P], negtri, sp_[:, 0:P], start=True, stop=True)
                    mm(C[:, P:256], negtri, sp_[:, P:256], start=True, stop=False)
                    mm(C[:, P:256], negones, sp_[:, 256:384], start=False, stop=True)
                    mm(C[:, 256:384], negtri, sp_[:, 256:384], start=True, stop=True).then_inc(S("sb_c"), 1)
                h = i - 3
                if 0 <= h < H:
                    pe.wait_ge(S("sb_w"), h + 1)
                    if h >= 2:
                        pe.wait_ge(S("sb_out"), h - 1)
                    _, _, _, v = att_cols("sb", h)
                    W, O = z_sb[:, h % 2], bank[6 + h % 2]
                    mm(O[:, 0:P], proj1[:, 0, v:v + DH], W[:, 0:P], start=True, stop=True)
                    mm(O[:, P:256], proj1[:, 0, v:v + DH], W[:, P:256], start=True, stop=False)
                    mm(O[:, P:256], proj1[:, 1, v:v + DH], W[:, 256:384], start=False, stop=True).then_inc(S("sb_o"), 1)
            stage_end(pe, "pe")

            def pv(kind, u, i):
                a = ATT[kind]
                per, n = a["per"], u * a["per"] + i
                pe.wait_ge(S(att(kind) + "_pt"), HEAD0[kind] + n + 1)
                if i == 0 and u >= 2:
                    pe.wait_ge(S(att(kind) + "_out"), UNIT0[kind] + u - 1)
                src, _, _, v = att_cols(kind, a["head"](u, i))
                T, O = a["pt"][:, n % 2], bank[6 + u % 2]
                mm(O[:, 0:P], src[:, 0, v:v + DH], T[:, 0:P], start=(i == 0), stop=False, skip_group_check=True)
                mm(O[:, P:256], src[:, 0, v:v + DH], T[:, P:256], start=False, stop=False, skip_group_check=True)
                ins = mm(O[:, P:256], src[:, 1, v:v + DH], T[:, 256:384], start=False, stop=(i == per - 1),
                         skip_group_check=True)
                ins.then_inc(S(att(kind) + "_O"), 1)

            def attention(kind):
                a = ATT[kind]
                U, per = a["units"], a["per"]
                for u in range(U + 1):
                    for i in range(per):
                        if u == U:
                            break
                        n = u * per + i
                        qk_transposes(kind, a["head"](u, i), n)
                        pe.wait_ge(S(att(kind) + "_qkt"), 2 * HEAD0[kind] + 2 * (n + 1))
                        if n >= 2:
                            pe.wait_ge(S(att(kind) + "_log"), HEAD0[kind] + n - 1)
                        q, k, Z = a["qkt"][:, n % 2, 0], a["qkt"][:, n % 2, 1], bank[2 + n % 2]
                        fox = kind == "fox"
                        for qs, ks, zs in ((slice(0, P), slice(0, P), slice(0, P)),
                                           (slice(P, 256), slice(0, 256), slice(P, 384))):
                            ins = mm(Z[:, zs], q[:, qs], k[:, ks], start=True, stop=not fox)
                            if fox:
                                c = big[0:1, F_CROW + u * 256:F_CROW + (u + 1) * 256]
                                mm(Z[:, zs], c[:, qs], fox_ones[:, ks], start=False, stop=False)
                                ins = mm(Z[:, zs], fox_neg, c[:, ks], start=False, stop=True)
                        ins.then_inc(S(att(kind) + "_S"), 1)
                    if u >= 1:
                        w = u - 1
                        for i in range(per):
                            n = w * per + i
                            pe.wait_ge(S(att(kind) + "_P"), UNIT0[kind] + w + 1)
                            if n >= 2:
                                pe.wait_ge(S(att(kind) + "_pt"), HEAD0[kind] + n - 1)
                            L = a["logit"][:, w % 2, i]
                            for j in range(3):
                                ins = nc.tensor.transpose(bank[4 + n % 2][:, j * P:(j + 1) * P],
                                                          L[:, j * P:(j + 1) * P], ident[:])
                            ins.then_inc(S(att(kind) + "_PT"), 1)
                            pv(kind, w, i)

            attention("dil")
            stage_end(pe, "pe")

            pe.wait_ge(S("glac_landed"), 48)
            for b in range(TB):
                ins = nc.tensor.transpose(bank[0][0:16, b * P:(b + 1) * P], gl_a[:, b, :], ident[:])
            ins.then_inc(S("gl_aT"), 1)
            pe.wait_ge(S("gl_at"), 1)
            for b in range(TB):
                mm(bank[2 + b][:], gl_at[:, b * P:(b + 1) * P], xf[0:16, G_W:G_W + 512], start=True, stop=False)
                ins = mm(bank[2 + b][:], ones[0:1, 0:P], xf[0:1, G_B:G_B + 512], start=False, stop=True)
                ins.then_inc(S("gl_alin"), 1)
            pe.wait_ge(S("gl_ls"), 2)
            R = region(xf, G_R, 384)
            for b in range(TB):
                mm(bank[2 + b][:], R[:, 256:384], gl_ls[:, b, :], start=True, stop=True).then_inc(S("gl_lc"), 1)
            for h in range(GLA_HEADS):
                if h >= 2:
                    pe.wait_ge(S("gl_qkm"), h - 1)
                    pe.wait_ge(S("gl_ex"), 2 * (h - 1))
                for i, col in enumerate((4608 + h * P, 5120 + h * P)):
                    for b in range(TB):
                        nc.tensor.transpose(bank[h % 2][:, i * 256 + b * P:i * 256 + (b + 1) * P],
                                            proj1[:, b, col:col + P], ident[:])
                for b in range(TB):
                    ins = mm(bank[4 + h % 2][:, b * 256:(b + 1) * 256], gl_ls[:, b, h * P:(h + 1) * P], R[:, 0:256],
                             start=True, stop=True)
                ins.then_inc(S("gl_cum"), 1)
            for h in range(GLA_HEADS):
                pe.wait_ge(S("gl_qkm"), h + 1)
                for c in range(4):
                    b, rows = c // 2, slice(64 * (c % 2), 64 * (c % 2) + 64)
                    tok = slice(c * 64, (c + 1) * 64)
                    ins = mm(bank[6][rows, (h * 2 + b) * 64:(h * 2 + b + 1) * 64], gl_km[:, h, tok], gl_qm[:, h, tok],
                             start=True, stop=True)
            ins.then_inc(S("gl_sT"), 1)
            pe.wait_ge(S("gl_sc"), 1)
            pe.wait_ge(S("gl_kd"), 2)
            for c in range(4):
                b, rows = c // 2, slice(64 * (c % 2), 64 * (c % 2) + 64)
                tok = slice(c * 64, (c + 1) * 64)
                for h in range(GLA_HEADS):
                    v = 5632 + h * DV
                    O = bank[h][rows, 0:DV]
                    if c > 0:
                        pe.wait_ge(S("gl_og"), 4 * (c - 1) + h + 1)
                        pe.wait_ge(S("gl_state"), 4 * (c - 1) + h + 1)
                    mm(O, gl_sc[rows, h * 2 + b, :], proj1[rows, b, v:v + DV], start=True, stop=(c == 0))
                    if c > 0:
                        ins = mm(O, gl_qc[:, h, tok], gl_st[:, (c - 1) % 2, h], start=False, stop=True)
                    if c < 3:
                        ins = mm(bank[4 + h][:, 0:DV], gl_kd[rows, b, h * P:(h + 1) * P], proj1[rows, b, v:v + DV],
                                 start=True, stop=True)
                    ins.then_inc(S("gl_o"), 1)
            pe.wait_ge(S("gl_fin"), 1)
            for k in range(8):
                if k >= 4:
                    pe.wait_ge(S("gl_h"), k - 3)
                for b in range(TB):
                    ins = nc.tensor.transpose(bank[k % 4][:, b * P:(b + 1) * P], gl_og[:, b, k * P:(k + 1) * P], ident[:])
                ins.then_inc(S("gl_T"), 1)
            stage_end(pe, "pe")

            plan, base = [], 0
            for i in range(3):
                for s in range(8):
                    plan.append((2 * i, ahi, alo, 2 * s, s == 0, s == 7))
                for s in range(BR_TILES[i]):
                    plan.append((2 * i + 1, bhi, blo, base + 2 * s, s == 0, s == BR_TILES[i] - 1))
                base += 2 * BR_TILES[i]

            def branch_tile(k, g, par):
                j, shi, slo, kc, first, last = plan[k]
                if first:
                    pe.wait_ge(evac_act, g * 6 + (n_branch + j))
                    pe.wait_ge(evac_dve, g * 6 + (n_branch + j))
                products(t_branch + k, g * 4, [(shi, slo, kc), (shi, slo, kc + 1)], (2 * (j % 3), 2 * (j % 3) + 1),
                         first, last)
            drive(pe, 4, 32, branch_tile)
            stage_end(pe, "pe")
            norm("y")
            gate_broadcast("g1")
            stage_end(pe, "pe")
            drive(pe, 4, 8, gemm_tile(t_out1, n_out1, ahi, alo))
            stage_end(pe, "pe")
            norm("n2")
            gate_broadcast("g2")
            stage_end(pe, "pe")

            def hidden_rounds(t0, n0, parts, rnd, prefix, q0):
                def up_tile(k, g, par):
                    if k == 0:
                        group_free(rnd * 12 + g + n0)
                    products(t0 + k, rnd * 12 + g, [(ahi, alo, 2 * k), (ahi, alo, 2 * k + 1)],
                             (2 * par, 2 * par + 1), k == 0, k == 7)

                def turn(g, par):
                    pe.wait_ge(evac_dve, rnd * 12 + g + (n0 + 3))
                    for c in range(2):
                        for b in range(TB):
                            ins = nc.tensor.transpose(bank[4][:, c * 256 + b * P:c * 256 + (b + 1) * P],
                                                      hid[:, b, c * P:(c + 1) * P], ident[:])
                    ins.then_inc(S(prefix + "_hidT"), 1)

                def down_tile(i):
                    g, k = divmod(i, parts)
                    if k == 0:
                        group_free(rnd * 12 + (n0 + parts + g))
                    if i == parts - 1:
                        pe.wait_ge(S(prefix + "_hsplit"), rnd * 8 + (q0 + parts))
                    products(t0 + 8 * parts + i, rnd * 12, [(bhi, blo, 2 * k), (bhi, blo, 2 * k + 1)],
                             (2 * (g % 2), 2 * (g % 2) + 1), k == 0, k == parts - 1)
                drive(pe, parts, 8, up_tile, {9: turn}, down_tile)
                for i in range(4, 4 * parts):
                    down_tile(i)

            with pe.Fori(0, 2) as rnd:
                hidden_rounds(t_ffn, n_ffn, 8, rnd, "ffn", 0)
            hidden_rounds(t_ffn + 192, n_ffn + 24, 6, 0, "ffn", 16)
            stage_end(pe, "pe")

            norm("n3")
            stage_end(pe, "pe")
            drive(pe, 10, 8, gemm_tile(t_proj2, n_proj2, ahi, alo))
            pe.wait_ge(S("side2_landed"), 32)
            side(side2, 8, bank[6], big[0:1, F_BF:F_BF + 8]).then_inc(S("side2_done"), 1)
            stage_end(pe, "pe")

            fox_tri = region(big, F_U, P)
            fox_neg = big[0:1, F_NEGROW:F_NEGROW + P]
            fox_ones = ones[0:1, :]
            pe.wait_ge(S("foxc_landed"), 16)
            for h in range(FOX_HEADS):
                C = bank[h // 2][0:1, (h % 2) * 256:(h % 2) * 256 + 256]
                mm(C[:, 0:P], f_logit[:, 0, h:h + 1], fox_tri, start=True, stop=True)
                mm(C[:, P:256], f_logit[:, 0, h:h + 1], ones[:, 0:P], start=True, stop=False)
                ins = mm(C[:, P:256], f_logit[:, 1, h:h + 1], fox_tri, start=False, stop=True)
            ins.then_inc(S("fox_c"), 1)
            pe.wait_ge(S("fox_crow"), 4)
            pe.wait_ge(S("fox_scaled"), 1)
            attention("fox")
            stage_end(pe, "pe")

            for src_col, dst in ((4096, "rg"), (3072, "rx")):
                for k in range(RNN_CHUNKS):
                    n = (8 if dst == "rx" else 0) + k
                    if n >= 4:
                        pe.wait_ge(S("rnn_copied"), n - 3)
                    for b in range(TB):
                        ins = nc.tensor.transpose(bank[n % 4][:, b * P:(b + 1) * P],
                                                  proj2[:, b, src_col + k * P:src_col + (k + 1) * P], ident[:])
                    ins.then_inc(S("rnn_T"), 1)
            pe.wait_ge(S("wrec_landed"), 32)
            for k in range(RNN_CHUNKS):
                pe.wait_ge(S("rnn_xc"), k + 1)
                if k >= 4:
                    pe.wait_ge(S("rnn_sig"), 2 * (k - 3))
                mm(bank[4 + k % 4][:, 0:256], r_w[:, 0, k], r_xc[:, k], start=True, stop=True)
                mm(bank[4 + k % 4][:, 256:512], r_w[:, 1, k], r_xc[:, k], start=True, stop=True)\
                    .then_inc(S("rnn_lin"), 1)
            stage_end(pe, "pe")

            drive(pe, 4, 8, gemm_tile(t_out2, n_out2, bhi, blo))
            stage_end(pe, "pe")
            norm("n4")
            stage_end(pe, "pe")
            pe.wait_ge(S("route_landed"), 32)
            side(route, 36, bank[6]).then_inc(S("route_done"), 1)
            with pe.Fori(0, 4) as rnd:
                hidden_rounds(t_moe, n_moe, 8, rnd, "moe", 0)
            stage_end(pe, "pe")
            norm("n5")
            pe.wait_ge(S("p_landed"), 16)
            for k in range(2):
                for b in range(TB):
                    ins = nc.tensor.transpose(bank[0][:, k * 256 + b * P:k * 256 + (b + 1) * P],
                                              big[:, b * 256 + k * P:b * 256 + (k + 1) * P], ident[:])
            ins.then_inc(S("p_T"), 1)
            stage_end(pe, "pe")
            for g in range(4):
                for half in range(2):
                    group_free(n_ple + 2 * g + half)
                    for k in range(8 if half == 0 else 1):
                        shi, slo = (ahi, alo) if half == 0 else (bhi, blo)
                        products(t_ple + 9 * g + 8 * half + k, 0, [(shi, slo, 2 * k), (shi, slo, 2 * k + 1)],
                                 (2 * half, 2 * half + 1), k == 0, k == (7 if half == 0 else 0))

        @block.scalar
        def _(act):
            A = nc.scalar.activation
            chain = Chain(act, "act_chain")

            def split_hi(t, r, up=False):
                act.wait_ge(landed[t % 8], r * 16 + 16 * (t // 8 + 1))
                if up is not False:
                    act.wait_ge(landed_up[t % 8], up)
                act.wait_ge(tile_used, r * 8 + (t - T_ADA + 1))
                A(whi[:, t % 4], raw[:, t % 8], ACT.Copy).then_inc(hi_ready, 1)

            def gemm_split(t0):
                return lambda k, g, par: split_hi(t0 + k, g)

            def norm(key):
                cfg = NORMS[key]
                if cfg["norm"]:
                    for b in range(TB):
                        A(junk if b == 0 else region(big, N_JUNK + D, D), cfg["src"][:, b], ACT.Square,
                          accum_out=stat[:, b:b + 1]).then_inc(S("norm_ss"), 1)
                    act.wait_ge(S("norm_var"), 1 * cfg["stats"] + 1)
                    A(stat[:, 4:6], stat[:, 2:4], ACT.Sqrt).then_inc(S("norm_std"), 1)
                for k in range(DC):
                    act.wait_ge(S("norm_T"), 16 * cfg["no"] + k + 1)
                    if k >= 4:
                        act.wait_ge(S("norm_lo"), 16 * cfg["no"] + k - 3)
                    if k == 0 and key in ("n1", "n2"):
                        act.wait_ge(S("gate_geff"), 1 * GATE_NO[key])
                    kw = {}
                    if cfg["gain"] is not None:
                        kw["scale"] = cfg["gain"][:, k:k + 1]
                    if cfg["bias"] is not None:
                        kw["bias"] = cfg["bias"][:, k:k + 1]
                    dst = htmp[:, k % 4]
                    A(dst, bank[4 + k % 4][:, 0:256], ACT.Identity if kw else ACT.Copy, **kw)\
                        .then_inc(S("norm_h"), 1)

            def gate_broadcast(key):
                act.wait_ge(S("gate_gb"), 1 * GATE_NO[key])
                for q in range(4):
                    A(gate_bc[:, q * COLS:(q + 1) * COLS], bank[q][:], ACT.Copy)

            def qk_squares(kind, groups, sq):
                for n, (src, b, col, w) in enumerate(groups):
                    if n >= 2:
                        act.wait_ge(S("qk_sqsum"), 4 * NORM_NO[kind] + n - 1)
                    A(sq[:, n % 2, 0:w], src[:, b, col:col + w], ACT.Square).then_inc(S("qk_sq"), 1)
                act.wait_ge(S("qk_var"), 1 * NORM_NO[kind] + 1)
                A(stat[:, 0:48], stat[:, 0:48], ACT.Sqrt).then_inc(S("qk_std"), 1)

            def attention(kind):
                a = ATT[kind]
                U, per = a["units"], a["per"]
                for u in range(U + 1):
                    if u < U:
                        act.wait_ge(S(att(kind) + "_max"), UNIT0[kind] + u + 1)
                        L = a["logit"][:, u % 2]
                        for qb, cols in ((0, slice(0, P)), (1, slice(P, 384))):
                            j = (u % 2) * 2 + qb
                            A(L[:, :, cols], L[:, :, cols], ACT.Exp, bias=stat[:, j:j + 1],
                              accum_out=stat[:, 8 + j:9 + j]).then_inc(S(att(kind) + "_exp"), 1)
                    if u >= 1:
                        w = u - 1
                        for i in range(per):
                            n = w * per + i
                            act.wait_ge(S(att(kind) + "_PT"), HEAD0[kind] + n + 1)
                            if n >= 2:
                                act.wait_ge(S(att(kind) + "_O"), HEAD0[kind] + n - 1)
                            A(a["pt"][:, n % 2], bank[4 + n % 2][:, 0:384], ACT.Copy).then_inc(S(att(kind) + "_pt"), 1)
                        act.wait_ge(S(att(kind) + "_O"), HEAD0[kind] + per * (w + 1))
                        A(bhi[:, a["dst"] + w, :], bank[6 + w % 2][:, 0:256], ACT.Copy).then_inc(S(att(kind) + "_ohi"), 1)

            act.wait_ge(S("vec_cols"), 1)
            A(silu_c[:], vec[:, V_C:V_C + 16], ACT.Silu).then_inc(S("silu_c"), 1)
            stage_end(act, "act")
            stage_end(act, "act")
            act.wait_ge(S("x_landed"), 16)
            norm("n1")
            stage_end(act, "act")

            def proj_evac(proj, t0):
                def ev(g, par):
                    act.wait_ge(tile_used, g * 8 + (t0 - T_ADA + 8 + 4))
                    A(proj[:, 0, bass.ds(g * COLS, COLS)], bank[2 * par][:], ACT.Copy).then_inc(evac_act, 1)
                return ev
            drive(act, 15, 8, gemm_split(t_proj1), {11: proj_evac(proj1, t_proj1)})
            act.wait_ge(S("side1_done"), 1)
            A(gl_a16[:], bank[6][:, 0:32], ACT.Copy)
            stage_end(act, "act")

            qk_squares("sb", [(proj1, b, c, 1536) for c in (0, 2304) for b in range(TB)], SQ1)
            H = SB_HEADS
            for i in range(H + 3):
                h = i - 1
                if 0 <= h < H:
                    act.wait_ge(S("sb_z"), h + 1)
                    if h >= 2:
                        act.wait_ge(S("sb_o"), h - 1)
                        act.wait_ge(S("sb_c"), h - 1)
                    Z, L, ZS = bank[2 + h % 2][:, 0:384], l_sb[:, h % 2], z_sb[:, h % 2]
                    A(ZS, Z, ACT.Copy).then_inc(S("sb_zs"), 1)
                    chain.step(A(L, Z, ACT.Abs))
                    chain.step(A(L, L, ACT.Exp, scale=-1.0))
                    A(L, L, ACT.Ln, bias=1.0).then_inc(S("sb_ln"), 1)
                h = i - 2
                if 0 <= h < H:
                    act.wait_ge(S("sb_e"), h + 1)
                    act.wait_ge(S("sb_em"), h + 1)
                    A(z_sb[:, h % 2], z_sb[:, h % 2], ACT.Exp).then_inc(S("sb_w"), 1)
                h = i - 3
                if 0 <= h < H:
                    act.wait_ge(S("sb_o"), h + 1)
                    A(bhi[:, h, :], bank[6 + h % 2][:, 0:256], ACT.Copy).then_inc(S("sb_ohi"), 1)
            stage_end(act, "act")

            attention("dil")
            stage_end(act, "act")

            act.wait_ge(S("gl_aT"), 1)
            A(gl_at, bank[0][0:16, 0:256], ACT.Copy).then_inc(S("gl_at"), 1)
            for b in range(TB):
                act.wait_ge(S("gl_alin"), b + 1)
                chain.step(A(gl_tmp[:, b], bank[2 + b][:], ACT.Abs))
                chain.step(A(gl_tmp[:, b], gl_tmp[:, b], ACT.Exp, scale=-1.0))
                A(gl_tmp[:, b], gl_tmp[:, b], ACT.Ln, bias=1.0).then_inc(S("gl_ln"), 1)
            for b in range(TB):
                act.wait_ge(S("gl_lc"), b + 1)
                A(gl_kd[:, b], bank[2 + b][:], ACT.Exp).then_inc(S("gl_elc"), 1)
            for h in range(GLA_HEADS):
                act.wait_ge(S("gl_cum"), h + 1)
                if h >= 2:
                    act.wait_ge(S("gl_qkm"), h - 1)
                C = bank[4 + h % 2][:].rearrange("p (b e n) -> p b e n", b=TB, e=2)
                E = gl_ex[:, h % 2].rearrange("p e (b n) -> p b e n", b=TB)
                for e in range(2):
                    A(E[:, :, e], C[:, :, e], ACT.Exp)
                A(E[:, :, 2], C[:, :, 1], ACT.Exp, scale=-1.0).then_inc(S("gl_ex"), 2)
            for c in range(4):
                b, rows = c // 2, slice(64 * (c % 2), 64 * (c % 2) + 64)
                for h in range(GLA_HEADS):
                    act.wait_ge(S("gl_o"), 4 * c + h + 1)
                    A(gl_og[rows, b, h * DV:(h + 1) * DV], bank[h][rows, 0:DV], ACT.Copy).then_inc(S("gl_og"), 1)
            act.wait_ge(S("gl_og"), 16)
            for b in range(TB):
                A(gl_sq[:, b], gl_og[:, b], ACT.Square).then_inc(S("gl_sq"), 1)
            for b in range(TB):
                A(proj1[:, b, 6656:7680], proj1[:, b, 6656:7680], ACT.Silu).then_inc(S("gl_silu"), 1)
            act.wait_ge(S("gl_var"), 1)
            A(gl_ss, gl_ss, ACT.Sqrt).then_inc(S("gl_std"), 1)
            for k in range(8):
                act.wait_ge(S("gl_T"), k + 1)
                if k >= 4:
                    act.wait_ge(S("gl_lo"), k - 3)
                A(gl_htmp[:, k % 4], bank[k % 4][:, 0:256], ACT.Identity, scale=vec[:, V_GG + k % 2:V_GG + k % 2 + 1])\
                    .then_inc(S("gl_h"), 1)
            stage_end(act, "act")

            def gate_evac(i):
                end = (8, 19, 28)[i]

                def ev(g, par):
                    act.wait_ge(tile_used, g * 32 + (t_branch - T_ADA + end + 4))
                    n = 2 * i
                    act.wait_ge(evac_dve, g * 6 + (n_branch + n - 2))
                    A(gsig[:, i, 0], bank[2 * (n % 3)][:], ACT.Sigmoid)
                    A(gsig[:, i, 1], bank[2 * (n % 3) + 1][:], ACT.Sigmoid).then_inc(evac_act, 1)
                return ev

            def branch_seen(i):
                end = (11, 20, 32)[i]

                def ev(g, par):
                    act.wait_ge(evac_dve, g * 6 + (n_branch + 2 * i + 4))
                    act.sem_inc(evac_act, 1)
                return ev
            ev_act = {11: gate_evac(0), 14: branch_seen(0), 22: gate_evac(1), 23: branch_seen(1), 31: gate_evac(2),
                      35: branch_seen(2)}
            drive(act, 4, 32, lambda k, g, par: split_hi(t_branch + k, g * 4), ev_act)
            stage_end(act, "act")
            norm("y")
            gate_broadcast("g1")
            stage_end(act, "act")

            def skip_evac(n0):
                def ev(g, par):
                    act.wait_ge(evac_dve, g + (n0 + 3))
                    act.sem_inc(evac_act, 1)
                return ev
            drive(act, 4, 8, gemm_split(t_out1), {11: skip_evac(n_out1)})
            stage_end(act, "act")
            norm("n2")
            gate_broadcast("g2")
            stage_end(act, "act")

            def hidden_rounds(t0, n0, parts, rnd, prefix, q0, up0):
                def up_split(k, g, par):
                    split_hi(t0 + k, rnd * 12 + g, rnd * 128 + g * 16 + (up0 + 16))

                def silu_evac(g, par):
                    act.wait_ge(tile_used, rnd * 96 + g * 8 + (t0 - T_ADA + 8 + 4))
                    for b in range(TB):
                        ins = A(silu_g[:, b], bank[2 * par + b][:, 0:HID], ACT.Silu)
                    ins.then_inc(evac_act, 1)

                def hidden_hi(g, par):
                    act.wait_ge(S(prefix + "_hidT"), rnd * 8 + g + (q0 + 1))
                    A(bhi[:, bass.ds(g * 2, 2), :], bank[4][:].rearrange("p (c n) -> p c n", c=2), ACT.Copy)\
                        .then_inc(S(prefix + "_hhi"), 1)

                def down(i):
                    split_hi(t0 + 8 * parts + i, rnd * 12)

                def seen(g):
                    act.wait_ge(evac_dve, rnd * 12 + (n0 + parts + g + 3))
                    act.sem_inc(evac_act, 1)
                drive(act, parts, 8, up_split, {10: silu_evac, 11: hidden_hi}, down)
                for i in range(4, 4 * parts + 4):
                    if i < 4 * parts:
                        down(i)
                    if i >= parts and (i - 3) % parts == 0:
                        seen((i - 3) // parts - 1)

            with act.Fori(0, 2) as rnd:
                hidden_rounds(t_ffn, n_ffn, 8, rnd, "ffn", 0, 0)
            hidden_rounds(t_ffn + 192, n_ffn + 24, 6, 0, "ffn", 16, 16 * 16)
            stage_end(act, "act")

            norm("n3")
            stage_end(act, "act")
            drive(act, 10, 8, gemm_split(t_proj2), {11: proj_evac(proj2, t_proj2)})
            act.wait_ge(S("side2_done"), 1)
            fl = stat[:, 32:48]
            chain.step(A(stat[:, 48:64], bank[6][:, 0:16], ACT.Copy))
            chain.step(A(fl, bank[6][:, 0:16], ACT.Abs))
            chain.step(A(fl, fl, ACT.Exp, scale=-1.0))
            A(fl, fl, ACT.Ln, bias=1.0).then_inc(S("fox_ln"), 1)
            stage_end(act, "act")

            act.wait_ge(S("fox_c"), 1)
            for q in range(4):
                A(big[0:1, F_CROW + q * 512:F_CROW + (q + 1) * 512], bank[q][0:1, :], ACT.Copy).then_inc(S("fox_crow"), 1)
            qk_squares("fox", [(proj2, b, c, 1024) for c in (0, 1024) for b in range(TB)], SQ2F)
            attention("fox")
            stage_end(act, "act")

            chain.step(A(stat[:, 16:24], vec[:, V_LAM:V_LAM + 8], ACT.Abs))
            A(stat[:, 16:24], stat[:, 16:24], ACT.Exp, scale=-1.0).then_inc(S("rnn_elam"), 1)
            for n in range(2 * RNN_CHUNKS):
                act.wait_ge(S("rnn_T"), n + 1)
                dst = r_rg[:, n] if n < 8 else r_xp[:, n - 8, 3:259]
                A(dst, bank[n % 4][:, 0:256], ACT.Copy).then_inc(S("rnn_copied"), 1)
            for k in range(RNN_CHUNKS):
                act.wait_ge(S("rnn_lin"), k + 1)
                if k == 0:
                    act.wait_ge(S("rnn_T"), 16)
                A(r_r[:, k], bank[4 + k % 4][:, 0:256], ACT.Sigmoid, bias=vec[:, V_BR + k:V_BR + k + 1])\
                    .then_inc(S("rnn_sig"), 1)
                A(r_i[:, k], bank[4 + k % 4][:, 256:512], ACT.Sigmoid, bias=vec[:, V_BI + k:V_BI + k + 1])\
                    .then_inc(S("rnn_sig"), 1)
            act.wait_ge(S("rnn_k8"), 1)
            act.wait_ge(S("rnn_xc"), 8)
            act.wait_ge(S("rnn_sig"), 16)
            for k in range(RNN_CHUNKS):
                A(r_a[:, k], r_r[:, k], ACT.Exp, scale=r_nk8[:, k:k + 1]).then_inc(S("rnn_a"), 1)
            act.wait_ge(S("rnn_a"), 8)
            for k in range(RNN_CHUNKS):
                A(r_r[:, k], r_r[:, k], ACT.Tanh, scale=r_k8[:, k:k + 1]).then_inc(S("rnn_tanh"), 1)
            act.wait_ge(S("rnn_m"), 1)
            A(r_r[:], r_r[:], ACT.Sqrt).then_inc(S("rnn_sqrt"), 1)
            act.wait_ge(S("rnn_g3"), 1)
            A(r_t[:], r_t[:], ACT.Tanh, scale=0.7978845608028654).then_inc(S("rnn_gt"), 1)
            act.wait_ge(S("rnn_out"), 1)
            A(bhi[:, 8:16, :], r_t[:], ACT.Copy).then_inc(S("rnn_hi"), 1)
            stage_end(act, "act")

            drive(act, 4, 8, gemm_split(t_out2), {11: skip_evac(n_out2)})
            stage_end(act, "act")
            norm("n4")
            stage_end(act, "act")

            act.wait_ge(S("rt_sub"), 1)
            A(rt[:, 0:8], rt[:, 0:8], ACT.Exp).then_inc(S("rt_exp"), 1)
            act.wait_ge(S("rt_dif"), 1)
            A(rt[:, 40:42], rt[:, 40:42], ACT.Exp).then_inc(S("rt_exp"), 1)
            with act.Fori(0, 4) as rnd:
                hidden_rounds(t_moe, n_moe, 8, rnd, "moe", 0, 16 * FFN_PARTS)
            stage_end(act, "act")

            norm("n5")
            act.wait_ge(S("p_T"), 1)
            A(bhi[:, 0:2, :], bank[0][:].rearrange("p (c n) -> p c n", c=2), ACT.Copy).then_inc(S("p_hi"), 1)
            stage_end(act, "act")
            for i in range(4 * 9 + 4):
                if i < 36:
                    split_hi(t_ple + i, 0)
                if i >= 10 and (i - 10) % 9 == 0 and (i - 10) // 9 < 4:
                    g = (i - 10) // 9
                    act.wait_ge(tile_used, t_ple - T_ADA + 9 * g + 8 + 4)
                    if g >= 1:
                        act.wait_ge(evac_dve, 2 + n_ple + 2 * g)
                    A(gsig[:, 0, 0], bank[0][:], ACT.Sigmoid)
                    A(gsig[:, 0, 1], bank[1][:], ACT.Sigmoid).then_inc(evac_act, 1)
                if i >= 12 and (i - 12) % 9 == 0 and (i - 12) // 9 < 4:
                    g = (i - 12) // 9
                    act.wait_ge(evac_dve, 2 + n_ple + 2 * g + 2)
                    act.sem_inc(evac_act, 1)

        @block.vector
        def _(dve):
            V = nc.vector
            chain = Chain(dve, "dve_chain")
            step = chain.step

            def split_lo(t, r):
                dve.wait_ge(hi_ready, r * 8 + (t - T_ADA + 1))
                V.tensor_tensor(wlo[:, t % 4], raw[:, t % 8], whi[:, t % 4].bitcast(F32), ALU.subtract)\
                    .then_inc(lo_ready, 1)

            def gemm_split(t0):
                return lambda k, g, par: split_lo(t0 + k, g)

            def rsqrt_var(dst, src, n):
                step(V.tensor_scalar(dst, src, 1.0 / n, EPS, ALU.mult, ALU.add))

            def norm(key):
                cfg = NORMS[key]
                if cfg["norm"]:
                    dve.wait_ge(S("norm_ss"), 2 * cfg["stats"] + 2)
                    V.tensor_scalar(stat[:, 2:4], stat[:, 0:2], 1.0 / D, EPS, ALU.mult, ALU.add)\
                        .then_inc(S("norm_var"), 1)
                    dve.wait_ge(S("norm_std"), 1 * cfg["stats"] + 1)
                    step(V.reciprocal(stat[:, 6:8], stat[:, 4:6]))
                    for b in range(TB):
                        V.tensor_scalar(xn[:, b], cfg["src"][:, b], stat[:, 6 + b:7 + b], None, ALU.mult)\
                            .then_inc(S("norm_xn"), 1)
                for k in range(DC):
                    h = htmp[:, k % 4]
                    dve.wait_ge(S("norm_h"), 16 * cfg["no"] + k + 1)
                    step(V.tensor_copy(ahi[:, k], h))
                    V.tensor_tensor(alo[:, k], h, ahi[:, k].bitcast(F32), ALU.subtract).then_inc(S("norm_lo"), 1)

            def gate_diag(key, cols):
                for k in range(DC):
                    V.tensor_scalar(gate_dg[:, k * P:(k + 1) * P], ident[:], cols[:, k:k + 1], None, ALU.mult)\
                        .then_inc(S("gate_gd"), 1)

            def qk_norm(kind, groups, sq, heads, gq, gk):
                at = 0
                for n, (src, b, col, w) in enumerate(groups):
                    dve.wait_ge(S("qk_sq"), 4 * NORM_NO[kind] + n + 1)
                    k = w // DH
                    V.reduce_sum(stat[:, at:at + k], sq[:, n % 2, 0:w].rearrange("p (h n) -> p h n", n=DH), AX.X)\
                        .then_inc(S("qk_sqsum"), 1)
                    at += k
                dve.wait_ge(S("qk_sqsum"), 4 * NORM_NO[kind] + 4)
                if at < 48:
                    step(V.memset(stat[:, at:48], 1.0))
                V.tensor_scalar(stat[:, 0:48], stat[:, 0:48], 1.0 / DH, EPS, ALU.mult, ALU.add)\
                    .then_inc(S("qk_var"), 1)
                dve.wait_ge(S("qk_std"), 1 * NORM_NO[kind] + 1)
                step(V.reciprocal(stat[:, 0:48], stat[:, 0:48]))
                at = 0
                for n, (src, b, col, w) in enumerate(groups):
                    k = w // DH
                    v = src[:, b, col:col + w].rearrange("p (h n) -> p h n", n=DH)
                    ins = V.tensor_tensor(v, v, stat[:, at:at + k].rearrange("p (h a) -> p h a", a=1)
                                          .to_broadcast([P, k, DH]), ALU.mult)
                    step(ins)
                    at += k
                step(V.tensor_scalar(vec[:, gq:gq + 1], vec[:, gq:gq + 1], QSCALE, None, ALU.mult))
                if kind == "sb":
                    step(V.tensor_scalar(vec[:, V_DQ:V_DQ + 1], vec[:, V_DQ:V_DQ + 1], QSCALE, None, ALU.mult))

            def qkt_evac(kind, n, qkt, gq, gk):
                dve.wait_ge(S(att(kind) + "_T"), HEAD0[kind] + n + 1)
                if n >= 2:
                    dve.wait_ge(S("sb_z") if kind == "sb" else S("att_S"), HEAD0[kind] + n - 1)
                for i, g in enumerate((gq, gk)):
                    V.tensor_scalar(qkt[:, n % 2, i], bank[n % 2][:, i * 256:(i + 1) * 256], vec[:, g:g + 1], None,
                                    ALU.mult).then_inc(S(att(kind) + "_qkt"), 1)

            def out_lo(kind, n, chunk, O):
                dve.wait_ge(S(att(kind) + "_ohi"), UNIT0[kind] + n + 1)
                V.tensor_tensor(blo[:, chunk, :], O, bhi[:, chunk, :].bitcast(F32), ALU.subtract)\
                    .then_inc(S(att(kind) + "_out"), 1)

            def attention(kind, gq, gk):
                a = ATT[kind]
                U, per = a["units"], a["per"]
                for u in range(U + 2):
                    if u < U:
                        L = a["logit"][:, u % 2]
                        for i in range(per):
                            n = u * per + i
                            qkt_evac(kind, n, a["qkt"], gq, gk)
                            dve.wait_ge(S(att(kind) + "_S"), HEAD0[kind] + n + 1)
                            if u >= 2 and i == 0:
                                dve.wait_ge(S(att(kind) + "_PT"), HEAD0[kind] + (u - 1) * per)
                            Z = bank[2 + n % 2]
                            if kind == "dil":
                                ins = V.tensor_tensor(L[:, i], Z[:, 0:384], dil_mask[u][:, i], ALU.add)
                                ins.then_inc(S("att_log"), 1)
                            else:
                                caus = region(big, F_CAUS, P)
                                step(V.tensor_copy(L[:, i, P:256], Z[:, P:256]))
                                step(V.tensor_tensor(L[:, i, 0:P], Z[:, 0:P], caus, ALU.add))
                                V.tensor_tensor(L[:, i, 256:384], Z[:, 256:384], caus, ALU.add)\
                                    .then_inc(S("att_log"), 1)
                        dve.wait_ge(S(att(kind) + "_log"), HEAD0[kind] + (u + 1) * per)
                        j = (u % 2) * 2
                        V.tensor_reduce(stat[:, 4:5], L[:, :, 0:P], AX.XY, ALU.max).then_inc(S(att(kind) + "_mx"), 1)
                        V.tensor_reduce(stat[:, 5:6], L[:, :, P:384], AX.XY, ALU.max).then_inc(S(att(kind) + "_mx"), 1)
                        dve.wait_ge(S(att(kind) + "_mx"), 2 * UNIT0[kind] + 2 * u + 2)
                        V.tensor_scalar(stat[:, j:j + 2], stat[:, 4:6], -1.0, None, ALU.mult).then_inc(S(att(kind) + "_max"), 1)
                    if u < U:
                        dve.wait_ge(S(att(kind) + "_exp"), 2 * UNIT0[kind] + 2 * (u + 1))
                        j = (u % 2) * 2
                        L = a["logit"][:, u % 2]
                        step(V.reciprocal(stat[:, 12 + j:14 + j], stat[:, 8 + j:10 + j]))
                        step(V.tensor_scalar(L[:, :, 0:P], L[:, :, 0:P], stat[:, 12 + j:13 + j], None, ALU.mult))
                        V.tensor_scalar(L[:, :, P:384], L[:, :, P:384], stat[:, 13 + j:14 + j], None, ALU.mult)\
                            .then_inc(S(att(kind) + "_P"), 1)
                    if 1 <= u <= U:
                        w = u - 1
                        out_lo(kind, w, a["dst"] + w, bank[6 + w % 2][:, 0:256])

            V.memset(ones[:], 1.0).then_inc(S("ones_set"), 1)
            V.memset(stat[:], 0.0).then_inc(S("ones_set"), 1)
            V.memset(silu_c[:], 0.0).then_inc(S("ones_set"), 1)
            V.memset(geff[:], 0.0).then_inc(S("ones_set"), 1)
            dve.wait_ge(S("ones_set"), 4)
            V.memset(seed[:, 0:1], 0.0).then_inc(tile_used, 4)
            V.memset(seed[:, 1:2], 0.0).then_inc(evac_act, 2)
            V.memset(seed[:, 2:3], 0.0).then_inc(evac_dve, 2)
            V.memset(seed[:, 3:4], 0.0).then_inc(S("mod_done"), 2)
            dve.wait_ge(S("vec_T"), 1)
            V.tensor_copy(vec[:], bank[0][:, 0:V_ALL]).then_inc(S("vec_cols"), 1)
            dve.wait_ge(S("silu_c"), 1)
            stage_end(dve, "dve")

            def ada_tile(k, g, par):
                dve.wait_ge(landed[k], g * 16 + 16)
                w = raw[:, k]
                for c in range(2):
                    col = silu_c[:, 2 * k + c:2 * k + c + 1]
                    if k == 0 and c == 0:
                        V.tensor_scalar(acc[:, par], w[:, 0], col, None, ALU.mult).then_inc(S("ada_step"), 1)
                    elif c == 0:
                        dve.wait_ge(lo_ready, g * 8 + k)
                        V.scalar_tensor_tensor(acc[:, par], w[:, 0], col, acc[:, par], ALU.mult, ALU.add)\
                            .then_inc(S("ada_step"), 1)
                    else:
                        dve.wait_ge(S("ada_step"), g * 8 + (k + 1))
                        V.scalar_tensor_tensor(acc[:, par], w[:, 1], col, acc[:, par], ALU.mult, ALU.add)\
                            .then_inc(lo_ready, 1)

            def ada_evac(g, par):
                dve.wait_ge(S("ada_cols"), g + 1)
                V.tensor_tensor(modt[:, bass.ds(g * 4, 4)], bank[par][:, 0:4], vec[:, bass.ds(g * 4, 4)], ALU.add)\
                    .then_inc(S("mod_done"), 1)
            drive(dve, 24, 8, ada_tile, {11: ada_evac})
            dve.wait_ge(S("mod_done"), 26)
            stage_end(dve, "dve")

            def gain_eff(key, scale, gain):
                V.scalar_tensor_tensor(geff[:], modt[:, scale:scale + 16], 1.0, vec[:, gain:gain + 16], ALU.add, ALU.mult)\
                    .then_inc(S("gate_geff"), 1)
            gain_eff("n1", 16, V_N1)
            norm("n1")
            stage_end(dve, "dve")

            def proj_evac(proj, t0):
                def ev(g, par):
                    dve.wait_ge(tile_used, g * 8 + (t0 - T_ADA + 8 + 4))
                    V.tensor_copy(proj[:, 1, bass.ds(g * COLS, COLS)], bank[2 * par + 1][:]).then_inc(evac_dve, 1)
                return ev
            drive(dve, 15, 8, gemm_split(t_proj1), {11: proj_evac(proj1, t_proj1)})
            stage_end(dve, "dve")

            grp = [(proj1, b, c, 1536) for c in (0, 2304) for b in range(TB)]
            dve.wait_ge(S("sbc_landed"), 16)
            step(V.memset(negones, -1.0))
            step(V.tensor_scalar(negtri, u_tri, -1.0, None, ALU.mult))
            qk_norm("sb", grp, SQ1, 48, V_SBQ, V_SBK)
            dve.sem_inc(S("sb_scaled"), 1)
            H = SB_HEADS
            for i in range(H + 4):
                if i < H:
                    qkt_evac("sb", i, qkt_sb, V_SBQ, V_SBK)
                h = i - 1
                if 0 <= h < H:
                    L, Z = l_sb[:, h % 2], bank[2 + h % 2][:, 0:384]
                    dve.wait_ge(S("sb_ln"), h + 1)
                    V.scalar_tensor_tensor(L, Z, 0.0, L, ALU.max, ALU.add).then_inc(S("sb_sp"), 1)
                    dve.wait_ge(S("sb_sp"), h + 1)
                    step(V.tensor_tensor(L[:, 0:P], L[:, 0:P], strict, ALU.mult))
                    V.tensor_tensor(L[:, 256:384], L[:, 256:384], strict, ALU.mult).then_inc(S("sb_spm"), 1)
                h = i - 2
                if 0 <= h < H:
                    ZS = z_sb[:, h % 2]
                    dve.wait_ge(S("sb_c"), h + 1)
                    dve.wait_ge(S("sb_zs"), h + 1)
                    V.tensor_tensor(ZS, ZS, bank[4 + h % 2][:, 0:384], ALU.add).then_inc(S("sb_e"), 1)
                    dve.wait_ge(S("sb_e"), h + 1)
                    step(V.tensor_tensor(ZS[:, 0:P], ZS[:, 0:P], strictneg, ALU.add))
                    V.tensor_tensor(ZS[:, 256:384], ZS[:, 256:384], strictneg, ALU.add).then_inc(S("sb_em"), 1)
                h = i - 3
                if 0 <= h < H:
                    out_lo("sb", h, h, bank[6 + h % 2][:, 0:256])
            stage_end(dve, "dve")

            dve.wait_ge(S("dmask_landed"), 32)
            attention("dil", V_DQ, V_DK)
            stage_end(dve, "dve")

            for b in range(TB):
                dve.wait_ge(S("gl_ln"), b + 1)
                V.scalar_tensor_tensor(gl_ls[:, b], bank[2 + b][:], 0.0, gl_tmp[:, b], ALU.min, ALU.subtract)\
                    .then_inc(S("gl_ls"), 1)
            for b in range(TB):
                dve.wait_ge(S("gl_elc"), b + 1)
                V.tensor_tensor(gl_kd[:, b], gl_kd[:, b], proj1[:, b, 5120:5632], ALU.mult).then_inc(S("gl_kd"), 1)
            for h in range(GLA_HEADS):
                dve.wait_ge(S("gl_ex"), 2 * (h + 1))
                T, E = bank[h % 2], gl_ex[:, h % 2]
                V.scalar_tensor_tensor(gl_qc[:, h], T[:, 0:256], QSCALE, E[:, 0], ALU.mult, ALU.mult)
                V.scalar_tensor_tensor(gl_qm[:, h], T[:, 0:256], QSCALE, E[:, 1], ALU.mult, ALU.mult)
                V.tensor_copy(gl_el[:, h], E[:, 0, 63:256:64])
                V.tensor_tensor(gl_km[:, h], T[:, 256:512], E[:, 2], ALU.mult).then_inc(S("gl_qkm"), 1)
            dve.wait_ge(S("gl_sT"), 1)
            mask = region(xf, G_MASK, 64)
            V.tensor_tensor(gl_sc, bank[6][:].rearrange("p (s n) -> p s n", s=8),
                            mask.rearrange("p (a n) -> p a n", a=1).to_broadcast([P, 8, 64]), ALU.mult)\
                .then_inc(S("gl_sc"), 1)
            dve.wait_ge(S("gl_sc"), 1)
            for c in range(3):
                for h in range(GLA_HEADS):
                    dve.wait_ge(S("gl_o"), 4 * c + h + 1)
                    U = bank[4 + h][:, 0:DV]
                    if c == 0:
                        ins = V.tensor_copy(gl_st[:, 0, h], U)
                    else:
                        ins = V.scalar_tensor_tensor(gl_st[:, c % 2, h], gl_st[:, (c - 1) % 2, h], gl_el[:, h, c:c + 1],
                                                     U, ALU.mult, ALU.add)
                    ins.then_inc(S("gl_state"), 1)
                if c < 2:
                    dve.wait_ge(S("gl_state"), 4 * c + 4)
            for b in range(TB):
                dve.wait_ge(S("gl_sq"), b + 1)
                step(V.reduce_sum(gl_ss[:, 4 * b:4 * b + 4], gl_sq[:, b].rearrange("p (h n) -> p h n", n=DV), AX.X))
            V.tensor_scalar(gl_ss, gl_ss, 1.0 / DV, EPS, ALU.mult, ALU.add).then_inc(S("gl_var"), 1)
            dve.wait_ge(S("gl_std"), 1)
            step(V.reciprocal(gl_ss, gl_ss))
            for b in range(TB):
                dve.wait_ge(S("gl_silu"), b + 1)
                for h in range(GLA_HEADS):
                    o = gl_og[:, b, h * DV:(h + 1) * DV]
                    col = 6656 + h * DV
                    ins = V.scalar_tensor_tensor(o, o, gl_ss[:, 4 * b + h:4 * b + h + 1], proj1[:, b, col:col + DV],
                                                 ALU.mult, ALU.mult)
                    if b == 1 and h == 3:
                        ins.then_inc(S("gl_fin"), 1)
            for k in range(8):
                dve.wait_ge(S("gl_h"), k + 1)
                step(V.tensor_copy(bhi[:, 8 + k], gl_htmp[:, k % 4]))
                V.tensor_tensor(blo[:, 8 + k], gl_htmp[:, k % 4], bhi[:, 8 + k].bitcast(F32), ALU.subtract)\
                    .then_inc(S("gl_lo"), 1)
            stage_end(dve, "dve")

            def gate_seen(i):
                def ev(g, par):
                    dve.wait_ge(evac_act, g * 6 + (n_branch + 2 * i + 3))
                    dve.sem_inc(evac_dve, 1)
                return ev

            def branch_evac(i):
                end = (11, 20, 32)[i]

                def ev(g, par):
                    dve.wait_ge(tile_used, g * 32 + (t_branch - T_ADA + end + 4))
                    n = 2 * i + 1
                    dst = ysum[:, :, bass.ds(g * COLS, COLS)]
                    for b in range(TB):
                        Bk = bank[2 * (n % 3) + b][:]
                        o = ysum[:, b, bass.ds(g * COLS, COLS)]
                        if i == 0:
                            ins = V.tensor_tensor(o, gsig[:, i, b], Bk, ALU.mult)
                            ins.then_inc(S("y_step") if b == 0 else evac_dve, 1)
                        else:
                            V.tensor_tensor(ymul[:, b], gsig[:, i, b], Bk, ALU.mult)\
                                .then_inc(S("y_step") if b == 0 else evac_dve, 1)
                    if i > 0:
                        dve.wait_ge(evac_dve, g * 6 + (n_branch + n + 3))
                        for b in range(TB):
                            o = ysum[:, b, bass.ds(g * COLS, COLS)]
                            V.tensor_tensor(o, o, ymul[:, b], ALU.add).then_inc(S("y_step"), 1)
                return ev
            ev_dve = {11: gate_seen(0), 14: branch_evac(0), 22: gate_seen(1), 23: branch_evac(1), 31: gate_seen(2),
                      35: branch_evac(2)}
            drive(dve, 4, 32, lambda k, g, par: split_lo(t_branch + k, g * 4), ev_dve)
            stage_end(dve, "dve")
            gate_diag("g1", modt[:, 32:48])
            norm("y")
            stage_end(dve, "dve")

            def residual_add(banks, cols, gate, n_after, chained):
                for b in range(TB):
                    if gate is not None:
                        V.tensor_tensor(prod[:, b], gate_bc[:, cols], bank[banks[b]][:], ALU.mult)\
                            .then_inc(S("prod_step") if b == 0 else evac_dve, 1)
                    else:
                        o = xres[:, b, cols]
                        V.tensor_tensor(o, o, bank[banks[b]][:], ALU.add)\
                            .then_inc(S("prod_step") if b == 0 else evac_dve, 1)
                if gate is not None:
                    dve.wait_ge(evac_dve, n_after)
                    for b in range(TB):
                        o = xres[:, b, cols]
                        V.tensor_tensor(o, o, prod[:, b], ALU.add).then_inc(S("prod_step"), 1)

            def out_evac(t0, n0, gate):
                def ev(g, par):
                    dve.wait_ge(tile_used, g * 8 + (t0 - T_ADA + 8 + 4))
                    residual_add((2 * par, 2 * par + 1), bass.ds(g * COLS, COLS), gate, g + (n0 + 3), True)
                return ev
            dve.wait_ge(S("x_back"), 16)
            drive(dve, 4, 8, gemm_split(t_out1), {11: out_evac(t_out1, n_out1, True)})
            stage_end(dve, "dve")
            gain_eff("n2", 64, V_N2)
            norm("n2")
            gate_diag("g2", modt[:, 80:96])
            stage_end(dve, "dve")

            def hidden_rounds(t0, n0, parts, rnd, prefix, q0, gate):
                def up_split(k, g, par):
                    split_lo(t0 + k, rnd * 12 + g)

                def hid_evac(g, par):
                    dve.wait_ge(evac_act, rnd * 12 + g + (n0 + 3))
                    for b in range(TB):
                        Up = bank[2 * par + b][:, HID:2 * HID]
                        if prefix == "moe":
                            w = comb[:, b, bass.ds(rnd * 8 + g, 1)]
                            ins = V.scalar_tensor_tensor(hid[:, b], Up, w, silu_g[:, b], ALU.mult, ALU.mult)
                        else:
                            ins = V.tensor_tensor(hid[:, b], Up, silu_g[:, b], ALU.mult)
                    ins.then_inc(evac_dve, 1)

                def hidden_lo(g, par):
                    dve.wait_ge(S(prefix + "_hhi"), rnd * 8 + g + (q0 + 1))
                    V.tensor_tensor(blo[:, bass.ds(g * 2, 2), :], bank[4][:].rearrange("p (c n) -> p c n", c=2),
                                    bhi[:, bass.ds(g * 2, 2), :].bitcast(F32), ALU.subtract)\
                        .then_inc(S(prefix + "_hsplit"), 1)

                def down(i):
                    split_lo(t0 + 8 * parts + i, rnd * 12)

                def down_evac(g):
                    dve.wait_ge(tile_used, rnd * 96 + (t0 - T_ADA + 8 * parts + parts * (g + 1) + 4))
                    residual_add((2 * (g % 2), 2 * (g % 2) + 1), slice(g * COLS, (g + 1) * COLS), gate,
                                 rnd * 12 + (n0 + parts + g + 3), True)
                drive(dve, parts, 8, up_split, {10: hid_evac, 11: hidden_lo}, down)
                for i in range(4, 4 * parts + 4):
                    if i < 4 * parts:
                        down(i)
                    if i >= parts and (i - 3) % parts == 0:
                        down_evac((i - 3) // parts - 1)

            with dve.Fori(0, 2) as rnd:
                hidden_rounds(t_ffn, n_ffn, 8, rnd, "ffn", 0, True)
            hidden_rounds(t_ffn + 192, n_ffn + 24, 6, 0, "ffn", 16, True)
            stage_end(dve, "dve")

            norm("n3")
            stage_end(dve, "dve")
            drive(dve, 10, 8, gemm_split(t_proj2), {11: proj_evac(proj2, t_proj2)})
            dve.wait_ge(S("fox_ln"), 1)
            step(V.scalar_tensor_tensor(stat[:, 48:64], stat[:, 48:64], 0.0, stat[:, 32:48], ALU.min, ALU.subtract))
            stage_end(dve, "dve")

            dve.wait_ge(S("foxc_landed"), 16)
            step(V.memset(big[0:1, F_NEGROW:F_NEGROW + P], -1.0))
            grp = [(proj2, b, c, 1024) for c in (0, 1024) for b in range(TB)]
            qk_norm("fox", grp, SQ2F, 32, V_FQ, V_FK)
            dve.sem_inc(S("fox_scaled"), 1)
            attention("fox", V_FQ, V_FK)
            stage_end(dve, "dve")

            step(V.memset(r_xp[:, :, 0:3], 0.0))
            lam = vec[:, V_LAM:V_LAM + 8]
            e1, s1, s2, q1 = (stat[:, 16 + 8 * i:24 + 8 * i] for i in range(4))
            dve.wait_ge(S("rnn_elam"), 1)
            step(V.tensor_scalar(s1, e1, 2.0, None, ALU.add))
            step(V.reciprocal(s1, s1))
            step(V.tensor_tensor(s1, s1, e1, ALU.mult))
            step(V.tensor_tensor(s2, s1, s1, ALU.mult))
            step(V.tensor_scalar(q1, s2, 1.0 / 17, 1.0 / 15, ALU.mult, ALU.add))
            for d in (13, 11, 9, 7, 5, 3, 1):
                step(V.tensor_tensor(q1, q1, s2, ALU.mult))
                step(V.tensor_scalar(q1, q1, 1.0 / d, None, ALU.add))
            step(V.tensor_tensor(q1, q1, s1, ALU.mult))
            step(V.tensor_scalar(s2, lam, -1.0, 0.0, ALU.mult, ALU.max))
            step(V.scalar_tensor_tensor(s2, q1, 2.0, s2, ALU.mult, ALU.add))
            step(V.tensor_scalar(r_k8, s2, 8.0, None, ALU.mult))
            step(V.tensor_scalar(r_nk8, s2, -8.0, None, ALU.mult))
            dve.sem_inc(S("rnn_k8"), 1)
            for k in range(RNN_CHUNKS):
                dve.wait_ge(S("rnn_copied"), 8 + k + 1)
                w = lambda i: vec[:, V_CW + 8 * i + k:V_CW + 8 * i + k + 1]
                step(V.tensor_scalar(r_xc[:, k], r_xp[:, k, 0:256], w(0), vec[:, V_CB + k:V_CB + k + 1], ALU.mult, ALU.add))
                for i in range(1, CONV_W):
                    ins = V.scalar_tensor_tensor(r_xc[:, k], r_xp[:, k, i:i + 256], w(i), r_xc[:, k], ALU.mult, ALU.add)
                    if i < CONV_W - 1:
                        step(ins)
                    else:
                        ins.then_inc(S("rnn_xc"), 1)
            dve.wait_ge(S("rnn_sig"), 16)
            dve.wait_ge(S("rnn_lin"), 8)
            step(V.tensor_tensor(r_i[:], r_i[:], r_xc[:], ALU.mult))
            dve.wait_ge(S("rnn_tanh"), 8)
            step(V.tensor_scalar(r_t[:], r_r[:], 1.0, None, ALU.add))
            step(V.reciprocal(r_t[:], r_t[:]))
            V.scalar_tensor_tensor(r_r[:], r_r[:], 2.0, r_t[:], ALU.mult, ALU.mult).then_inc(S("rnn_m"), 1)
            dve.wait_ge(S("rnn_m"), 1)
            step(V.tensor_tensor(r_t[:], r_rg[:], r_rg[:], ALU.mult))
            step(V.tensor_scalar(r_t[:], r_t[:], 0.044715, 1.0, ALU.mult, ALU.add))
            V.tensor_tensor(r_t[:], r_t[:], r_rg[:], ALU.mult).then_inc(S("rnn_g3"), 1)
            dve.wait_ge(S("rnn_sqrt"), 1)
            step(V.tensor_tensor(r_i[:], r_i[:], r_r[:], ALU.mult))
            for k in range(RNN_CHUNKS):
                ins = V.tensor_tensor_scan(r_r[:, k], r_a[:, k], r_i[:, k], 0.0, ALU.mult, ALU.add)
            step(ins)
            dve.wait_ge(S("rnn_gt"), 1)
            step(V.scalar_tensor_tensor(r_t[:], r_t[:], 1.0, r_rg[:], ALU.add, ALU.mult))
            V.scalar_tensor_tensor(r_t[:], r_t[:], 0.5, r_r[:], ALU.mult, ALU.mult).then_inc(S("rnn_out"), 1)
            dve.wait_ge(S("rnn_hi"), 1)
            V.tensor_tensor(blo[:, 8:16, :], r_t[:], bhi[:, 8:16, :].bitcast(F32), ALU.subtract)
            stage_end(dve, "dve")

            drive(dve, 4, 8, gemm_split(t_out2), {11: out_evac(t_out2, n_out2, None)})
            stage_end(dve, "dve")
            norm("n4")
            stage_end(dve, "dve")

            dve.wait_ge(S("route_done"), 1)
            lg = rt[:, 64:136].rearrange("p (b n) -> p b n", b=TB)
            step(V.tensor_copy(lg, bank[6][:, 0:72].rearrange("p (b n) -> p b n", b=TB)))
            gmax, gone = rt[:, 8:10], rt[:, 16:24].rearrange("p (b n) -> p b n", b=TB)
            ex = rt[:, 0:8].rearrange("p (b n) -> p b n", b=TB)

            def wide(v, n):
                return v.rearrange("p (b a) -> p b a", a=1).to_broadcast([P, TB, n])
            step(V.tensor_reduce(gmax, lg[:, :, 0:4], AX.X, ALU.max))
            step(V.tensor_tensor(gone, lg[:, :, 0:4], wide(gmax, 4), ALU.is_equal))
            V.tensor_tensor(ex, lg[:, :, 0:4], wide(gmax, 4), ALU.subtract).then_inc(S("rt_sub"), 1)
            step(V.tensor_scalar(gone, gone, 1.0, -BIG_NEG, ALU.subtract, ALU.mult))
            el = rt[:, 160:224].rearrange("p (b g n) -> p b g n", b=TB, g=4)
            el2 = rt[:, 160:224].rearrange("p (b n) -> p b n", b=TB)
            for b in range(TB):
                step(V.tensor_tensor(el[:, b], lg[:, b, 4:36].rearrange("p (g n) -> p g n", g=4),
                                     gone[:, b].rearrange("p (g a) -> p g a", a=1).to_broadcast([P, 4, 8]), ALU.add))
            m1, m2 = rt[:, 24:26], rt[:, 26:28]
            eq1 = rt[:, 256:320].rearrange("p (b n) -> p b n", b=TB)
            eq2 = rt[:, 320:384].rearrange("p (b n) -> p b n", b=TB)
            rest = rt[:, 384:448].rearrange("p (b n) -> p b n", b=TB)
            step(V.tensor_reduce(m1, el2, AX.X, ALU.max))
            step(V.tensor_tensor(eq1, el2, wide(m1, 32), ALU.is_equal))
            step(V.scalar_tensor_tensor(rest, eq1, BIG_NEG, el2, ALU.mult, ALU.add))
            step(V.tensor_reduce(m2, rest, AX.X, ALU.max))
            step(V.tensor_tensor(eq2, rest, wide(m2, 32), ALU.is_equal))
            V.tensor_tensor(rt[:, 40:42], m2, m1, ALU.subtract).then_inc(S("rt_dif"), 1)
            dve.wait_ge(S("rt_exp"), 2)
            gw, w1, w2 = rt[:, 28:30], rt[:, 30:32], rt[:, 32:34]
            step(V.reduce_sum(gw, ex, AX.X))
            step(V.reciprocal(gw, gw))
            step(V.tensor_scalar(w1, rt[:, 40:42], 1.0, None, ALU.add))
            step(V.reciprocal(w1, w1))
            step(V.tensor_tensor(w1, w1, gw, ALU.mult))
            step(V.tensor_tensor(w2, w1, rt[:, 40:42], ALU.mult))
            step(V.tensor_tensor(eq1, eq1, wide(w1, 32), ALU.mult))
            step(V.tensor_tensor(eq2, eq2, wide(w2, 32), ALU.mult))
            step(V.tensor_tensor(comb, eq1, eq2, ALU.add))
            with dve.Fori(0, 4) as rnd:
                hidden_rounds(t_moe, n_moe, 8, rnd, "moe", 0, None)
            stage_end(dve, "dve")

            norm("n5")
            dve.wait_ge(S("p_hi"), 1)
            V.tensor_tensor(blo[:, 0:2, :], bank[0][:].rearrange("p (c n) -> p c n", c=2),
                            bhi[:, 0:2, :].bitcast(F32), ALU.subtract)
            stage_end(dve, "dve")
            for i in range(4 * 9 + 4):
                if i < 36:
                    split_lo(t_ple + i, 0)
                if i >= 10 and (i - 10) % 9 == 0 and (i - 10) // 9 < 4:
                    g = (i - 10) // 9
                    dve.wait_ge(evac_act, 2 + n_ple + 2 * g + 1)
                    dve.sem_inc(evac_dve, 1)
                if i >= 12 and (i - 12) % 9 == 0 and (i - 12) // 9 < 4:
                    g = (i - 12) // 9
                    dve.wait_ge(tile_used, t_ple - T_ADA + 9 * g + 9 + 4)
                    for b in range(TB):
                        V.tensor_tensor(prod[:, b], gsig[:, 0, b], bank[2 + b][:], ALU.mult).then_inc(S("ple_prod"), 1)
                    dve.wait_ge(S("ple_prod"), 2 * g + 2)
                    for b in range(TB):
                        o = xres[:, b, g * COLS:(g + 1) * COLS]
                        V.tensor_tensor(o, o, prod[:, b], ALU.add)\
                            .then_inc(S("ple_sum") if b == 0 else evac_dve, 1)


INPUTS = ["x", "c", "w_ada", "b_ada", "norm1_gain", "norm2_gain", "w_in", "sb_q_gain", "sb_k_gain", "dil_q_gain",
          "dil_k_gain", "w_gla_a", "b_gla_a", "gla_out_gain", "w_br_sb", "w_br_dil", "w_br_gla", "w_out", "w_ffn_in",
          "w_ffn_out", "p_2", "mix_norm_2", "w_in_2", "b_forget_2", "q_norm_2", "k_norm_2", "conv_w_2", "conv_b_2",
          "w_rec_gate_2", "b_rec_gate_2", "w_in_gate_2", "b_in_gate_2", "lru_lambda_2", "w_out_2", "ffn_norm_2",
          "w_router_group_2", "w_router_expert_2", "w_expert_gate_2", "w_expert_up_2", "w_expert_down_2",
          "ple_norm_2", "w_ple_gate_2", "w_ple_up_2"]


def kernel(**inputs):
    import concourse.bacc as _bacc
    from concourse.bass_utils import run_bass_kernel_spmd as _run

    nc = _bacc.Bacc("TRN2", target_bir_lowering=False, num_devices=1)
    arrays, aps = {}, {}
    for name in INPUTS:
        a = np.ascontiguousarray(inputs[name])
        a = a.reshape([d for i, d in enumerate(a.shape) if d != 1 or i >= 2] or [1])
        arrays["in_" + name] = a
        aps[name] = nc.dram_tensor("in_" + name, a.shape, F32, kind="ExternalInput").ap()
    arrays["in_consts"] = shape_constants()
    aps["consts"] = nc.dram_tensor("in_consts", (P, C_ALL), F32, kind="ExternalInput").ap()
    out = nc.dram_tensor("out_0", (TB * P, D), F32, kind="ExternalOutput").ap()
    program(nc, aps, out)
    r = _run(nc, [arrays], core_ids=[0])
    return r.results[0]["out_0"].reshape(1, TB * P, D)
```

```python
import concourse.bass as bass
from concourse import mybir
from contextlib import ExitStack
import numpy as np

F32 = mybir.dt.float32
F32R = mybir.dt.float32r
ACT = mybir.ActivationFunctionType
ALU = mybir.AluOpType
AX = mybir.AxisListType

P = 128
D = 2048
TB = 2
DC = D // P
COLS = 512
EPS = 1e-6
DH = 128
QSCALE = DH ** -0.5
SB_HEADS, DIL_SLOTS, DIL_GROUPS, GLA_HEADS, FOX_HEADS = 6, 2, 3, 4, 8
DILATION = (1, 4, 16)
DV = 256
RNN_CHUNKS = 8
CONV_W = 4
D_FF = 5632
N_EXPERTS = 32
HID = 256
FFN_PARTS = D_FF // HID
BIG_NEG = -1.0e30

PROJ1 = 7680
A_COL = PROJ1
GATE_COL = A_COL + 16
PROJ2_QKV, F_COLS = 3072, 8
PROJ2 = 5120

V_BADA, V_N1, V_N2, V_MIX, V_PLE, V_CB, V_BR, V_BI, V_LAM, V_CW = 0, 96, 112, 128, 144, 160, 168, 176, 184, 192
V_SBQ, V_SBK, V_DQ, V_DK, V_FQ, V_FK, V_GG, V_C = 224, 225, 226, 227, 228, 229, 230, 232
V_ALL = 248

C_ID, C_U, C_STRICT, C_STRICTNEG, C_CAUSNEG, C_TRI, C_R, C_GMASK, C_DIL = 0, 128, 256, 384, 512, 640, 768, 1152, 1216
C_ALL = C_DIL + 2 * 3 * 384


def shape_constants():
    c = np.zeros((P, C_ALL), np.float32)
    i = np.arange(P)[:, None]
    j = np.arange(P)[None, :]
    c[:, C_ID:C_ID + P] = i == j
    c[:, C_U:C_U + P] = np.where(i >= j, 1.0, 0.0)
    c[:, C_STRICT:C_STRICT + P] = i < j
    c[:, C_STRICTNEG:C_STRICTNEG + P] = np.where(i < j, 0.0, BIG_NEG)
    c[:, C_CAUSNEG:C_CAUSNEG + P] = np.where(j <= i, 0.0, BIG_NEG)
    c[:, C_TRI:C_TRI + P] = i <= j
    same = (i // 64) == (j // 64)
    mid = (j // 64) * 64 + 31
    c[:, C_R:C_R + P] = (same & (i <= j)) / 16.0
    c[:, C_R + P:C_R + 2 * P] = ((same & (i <= j)) * 1.0 - (same & (i <= mid)) * 1.0) / 16.0
    c[:, C_R + 2 * P:C_R + 3 * P] = (same & (i > j)) / 16.0
    jj = np.arange(64)[None, :]
    c[:, C_GMASK:C_GMASK + 64] = (i % 64) <= jj
    n_heads = 2 * 3
    for slot in range(2):
        for g in range(3):
            head = g * 2 + slot
            slope = np.float32(2.0 ** (-8.0 * (head + 1) / n_heads))
            dil = DILATION[g]

            def bias(t, s):
                d = t - s
                ok = (d >= 0) & (d % dil == 0) & (d // dil <= 128)
                return np.where(ok, -slope * d, BIG_NEG)
            at = C_DIL + (slot * 3 + g) * 384
            c[:, at:at + 128] = bias(i, j)
            c[:, at + 128:at + 384] = bias(i + 128, np.arange(256)[None, :])
    return c


def program(nc, I, out):
    ctx = ExitStack()
    with ctx:
        def sb(name, shape, dt=F32):
            return ctx.enter_context(nc.sbuf_tensor(name, shape, dt))

        sems = {}

        def S(name):
            if name not in sems:
                sems[name] = ctx.enter_context(nc.semaphore(name))
            return sems[name]

        raw = sb("raw", [P, 8, 2, COLS])
        whi = sb("whi", [P, 4, 2, COLS], F32R)
        wlo = sb("wlo", [P, 4, 2, COLS], F32R)
        ahi = sb("ahi", [P, DC, TB * P], F32R)
        alo = sb("alo", [P, DC, TB * P], F32R)
        bhi = sb("bhi", [P, DC, TB * P], F32R)
        blo = sb("blo", [P, DC, TB * P], F32R)
        xres = sb("xres", [P, TB, D])
        big = sb("big", [P, TB * PROJ1])
        ident = sb("ident", [P, P])
        ones = sb("ones", [P, 2 * P])
        vec = sb("vec", [P, V_ALL])
        modt = sb("modt", [P, 96])
        gain_ffn2 = sb("gain_ffn2", [P, DC])
        geff = sb("geff", [P, DC])
        stat = sb("stat", [P, 64])
        silu_c = sb("silu_c", [P, DC])
        gl_a16 = sb("gl_a16", [P, TB * 16])
        forget_bias = sb("forget_bias", [1, 8])
        seed = sb("seed", [P, 4])
        bank = [ctx.enter_context(nc.psum_tensor(f"bank{i}", [P, COLS], F32)) for i in range(8)]

        xf = xres[:].rearrange("p b n -> p (b n)")

        def region(base, off, n):
            return base[:, off:off + n]

        landed = [S(f"raw_landed{i}") for i in range(8)]
        landed_up = [S(f"raw_up_landed{i}") for i in range(8)]
        hi_ready = S("hi_ready")
        lo_ready = S("lo_ready")
        tile_used = S("tile_used")
        evac_act = S("evac_act")
        evac_dve = S("evac_dve")
        ENG = ("pe", "act", "dve")
        stage_sem = {e: S(f"stage_{e}") for e in ENG}
        stage_no = {e: 0 for e in ENG}
        T_ADA = 24 * 8

        def stage_end(eng, key):
            eng.drain().then_inc(stage_sem[key], 1)
            stage_no[key] += 1
            for e in ENG:
                if e != key:
                    eng.wait_ge(stage_sem[e], stage_no[key])

        def wait_stage(eng, n, keys=ENG):
            for e in keys:
                eng.wait_ge(stage_sem[e], n)

        class Chain:

            def __init__(self, eng, name):
                self.eng, self.sem, self.n = eng, S(name), 0

            def step(self, ins):
                ins.then_inc(self.sem, 1)
                self.n += 1
                self.eng.wait_ge(self.sem, self.n)

        (ST_LOAD, ST_ADA, ST_PROJ1, ST_SB, ST_DIL, ST_GLA, ST_BRANCH, ST_OUT1, ST_FFN, ST_PROJ2, ST_FOX, ST_OUT2,
         ST_MOE) = range(1, 14)

        ADA_FIRST = 9
        t_proj1 = ADA_FIRST * 8
        t_branch = t_proj1 + 7 * 24 + 8
        t_out1 = t_branch + 4 * 48
        u_branch = 15 * 8
        t_ffn = t_out1 + 4 * 8
        t_proj2 = t_ffn + 22 * 8 + 8 * 8 + 4 * 6
        t_out2 = t_proj2 + 10 * 8
        t_moe = t_out2 + 4 * 8
        t_ple = t_moe + 4 * 12 * 8
        n_proj1, n_branch = 0, 15
        n_out1 = n_branch + 24
        n_ffn = n_out1 + 4
        n_proj2 = n_ffn + 22 + 12
        n_out2 = n_proj2 + 10
        n_moe = n_out2 + 4
        n_ple = n_moe + 48

        def drive(eng, groups, tiles, tile, events=None, follow=None, prologue=True, ahead=4, single=False):
            events = events or {}
            if prologue:
                for k in range(ahead):
                    tile(k, 0, 0)

            def body(g, par, last):
                for k in range(ahead, tiles + ahead):
                    if k < tiles:
                        tile(k, g, par)
                    elif not last:
                        tile(k - tiles, g + 1, 1 - par)
                    elif follow:
                        follow(k - tiles)
                    if k in events:
                        events[k](g, par)
            if single:
                with eng.Fori(0, groups - 1) as i:
                    body(i, 0, False)
                body(groups - 1, 0, True)
                return
            pairs = (groups - 1) // 2
            if pairs > 0:
                with eng.Fori(0, pairs) as i:
                    body(i * 2, 0, False)
                    body(i * 2 + 1, 1, False)
            for g in range(2 * pairs, groups):
                body(g, g % 2, g == groups - 1)

        def shared_order(products):
            order = [(True, j) for j in range(4)]
            for a in range(products // 2):
                order.append((False, a))
                order += [(True, 4 + 2 * a + c) for c in range(2) if 4 + 2 * a + c < products]
            return order
        PROJ1_ORDER, BRANCH_ORDER = shared_order(16), shared_order(32)
        assert len(PROJ1_ORDER) == 24 and len(BRANCH_ORDER) == 48

        def item(j):
            return BRANCH_ORDER.index((True, j))

        def nat(w):
            return w.rearrange("(k p) n -> p k n", p=P)

        w_ada_v = nat(I["w_ada"])
        w_in_v = nat(I["w_in"])
        w_out_v = nat(I["w_out"])
        w_in2_v = nat(I["w_in_2"])
        w_out2_v = nat(I["w_out_2"])
        w_ple_v = nat(I["w_ple_gate_2"])
        w_up_v = nat(I["w_ple_up_2"])
        br_v = [nat(I["w_br_sb"]), nat(I["w_br_dil"]), nat(I["w_br_gla"])]
        BR_TILES = (3, 1, 4)
        ffn_in_v = I["w_ffn_in"].rearrange("(k p) (h n) -> p k h n", p=P, h=2)
        ffn_out_v = nat(I["w_ffn_out"])
        eg_v = I["w_expert_gate_2"].rearrange("e (p k) n -> p e k n", k=DC)
        eu_v = I["w_expert_up_2"].rearrange("e (p k) n -> p e k n", k=DC)
        ed_v = I["w_expert_down_2"].rearrange("e (k p) n -> p e k n", p=P)

        block = ctx.enter_context(nc.Block())

        @block.sync
        def _(sp):
            def slot_free(t, r):
                if isinstance(r, int):
                    if t + 8 * r >= 8:
                        sp.wait_ge(lo_ready, t + 8 * r - 7)
                else:
                    sp.wait_ge(lo_ready, r * 8 + (t - 7))

            def load(t, src, r=0):
                sp.lower_ap_dma(src)
                slot_free(t, r)
                sp.dma_start(raw[:, t % 8], src).then_inc(landed[t % 8], 16)

            sp.dma_start(ident[:], I["consts"][:, C_ID:C_ID + P]).then_inc(S("small_landed"), 16)
            vrows = region(big, 0, 3 * P)
            r1 = lambda name, k: I[name].rearrange("(k p) -> k p", p=P)
            rows = [(0, 0, "b_ada", 96), (1, 0, "norm1_gain", 16), (1, 16, "norm2_gain", 16), (1, 32, "mix_norm_2", 16),
                    (1, 48, "ple_norm_2", 16), (1, 64, "conv_b_2", 8), (1, 72, "b_rec_gate_2", 8),
                    (1, 80, "b_in_gate_2", 8), (1, 88, "lru_lambda_2", 8),
                    (2, 0, "sb_q_gain", 1), (2, 1, "sb_k_gain", 1), (2, 2, "dil_q_gain", 1), (2, 3, "dil_k_gain", 1),
                    (2, 4, "q_norm_2", 1), (2, 5, "k_norm_2", 1), (2, 6, "gla_out_gain", 2), (2, 8, "c", 16)]
            for tile_no, at, name, k in rows:
                sp.dma_start(vrows[at:at + k, tile_no * P:(tile_no + 1) * P], r1(name, k)).then_inc(S("small_landed"), 16)
            sp.dma_start(vrows[96:128, P:2 * P], I["conv_w_2"].rearrange("w (k p) -> (w k) p", p=P))\
              .then_inc(S("small_landed"), 16)
            sp.dma_start(gain_ffn2[:], I["ffn_norm_2"].rearrange("(p k) -> p k", k=DC)).then_inc(S("small_landed"), 16)

            sp.dma_start(xres[:], I["x"].rearrange("(b p) n -> p b n", p=P)).then_inc(S("x_landed"), 16)

            for s in range(8):
                load(s, w_ada_v[:, 2 * s:2 * s + 2, 0:COLS])
            with sp.Fori(1, ADA_FIRST) as g:
                for s in range(8):
                    load(s, w_ada_v[:, 2 * s:2 * s + 2, bass.ds(g * COLS, COLS)], g)
            def ada_src(k, g):
                return w_ada_v[:, 2 * k:2 * k + 2, bass.ds(g * COLS, COLS)]

            def in_src(k, col):
                return w_in_v[:, 2 * k:2 * k + 2, bass.ds(col, COLS)]
            with sp.Fori(0, 7) as g:
                for k, (is_product, j) in enumerate(PROJ1_ORDER):
                    src = in_src(j % 8, g * (2 * COLS) + (j // 8) * COLS) if is_product else ada_src(j, g + ADA_FIRST)
                    load(t_proj1 + k, src, g * 3)
            for k in range(8):
                load(t_proj1 + 7 * 24 + k, in_src(k, 14 * COLS))
            with sp.Fori(0, 4) as g:
                srcs = []
                for i in range(3):
                    srcs += [in_src(s, g * COLS + (GATE_COL + i * D)) for s in range(8)]
                    srcs += [br_v[i][:, 2 * s:2 * s + 2, bass.ds(g * COLS, COLS)] for s in range(BR_TILES[i])]
                for k, (is_product, j) in enumerate(BRANCH_ORDER):
                    load(t_branch + k, srcs[j] if is_product else ada_src(j % 8, g * 2 + (ADA_FIRST + 7 + j // 8)), g * 6)
            with sp.Fori(0, 4) as g:
                for s in range(8):
                    load(t_out1 + s, w_out_v[:, 2 * s:2 * s + 2, bass.ds(g * COLS, COLS)], g)

            def ffn_in_tile(t, s, part, r=0):
                slot_free(t, r)
                for half, sem in ((0, landed), (1, landed_up)):
                    sp.dma_start(raw[:, t % 8, :, half * HID:(half + 1) * HID],
                                 ffn_in_v[:, 2 * s:2 * s + 2, half, bass.ds(part * HID, HID)]).then_inc(sem[t % 8], 16)
            with sp.Fori(0, 2) as rnd:
                with sp.Fori(0, 8) as e:
                    for s in range(8):
                        ffn_in_tile(t_ffn + s, s, rnd * 8 + e, rnd * 12 + e)
                with sp.Fori(0, 4) as g:
                    for s in range(8):
                        load(t_ffn + 64 + s, ffn_out_v[:, bass.ds(rnd * 16 + 2 * s, 2), bass.ds(g * COLS, COLS)],
                             rnd * 12 + g)
            t = t_ffn + 192
            with sp.Fori(0, 6) as e:
                for s in range(8):
                    ffn_in_tile(t + s, s, e + 16, e)
            for g in range(4):
                for s in range(6):
                    load(t + 48 + 6 * g + s, ffn_out_v[:, 32 + 2 * s:34 + 2 * s, g * COLS:(g + 1) * COLS])

            with sp.Fori(0, 6) as g:
                for s in range(8):
                    load(t_proj2 + s, w_in2_v[:, 2 * s:2 * s + 2, bass.ds(g * COLS, COLS)], g)
            with sp.Fori(0, 4) as g:
                for s in range(8):
                    load(t_proj2 + 48 + s,
                         w_in2_v[:, 2 * s:2 * s + 2, bass.ds(g * COLS + (PROJ2_QKV + F_COLS), COLS)], g)
            with sp.Fori(0, 4) as g:
                for s in range(8):
                    load(t_out2 + s, w_out2_v[:, 2 * s:2 * s + 2, bass.ds(g * COLS, COLS)], g)

            with sp.Fori(0, 4) as rnd:
                with sp.Fori(0, 8) as e:
                    for s in range(8):
                        t = t_moe + s
                        slot_free(t, rnd * 12 + e)
                        for half, v, sem in ((0, eg_v, landed), (1, eu_v, landed_up)):
                            src = v[:, bass.ds(rnd * 8 + e, 1), 2 * s:2 * s + 2, :].rearrange("p e k n -> p (e k) n")
                            sp.dma_start(raw[:, t % 8, :, half * HID:(half + 1) * HID], src).then_inc(sem[t % 8], 16)
                with sp.Fori(0, 4) as g:
                    for s in range(8):
                        src = ed_v[:, bass.ds(rnd * 8 + s, 1), :, bass.ds(g * COLS, COLS)]
                        load(t_moe + 64 + s, src.rearrange("p e k n -> p (e k) n"), rnd * 12 + g)

            for g in range(4):
                for s in range(8):
                    load(t_ple + 9 * g + s, w_ple_v[:, 2 * s:2 * s + 2, g * COLS:(g + 1) * COLS])
                load(t_ple + 9 * g + 8, w_up_v[:, 0:2, g * COLS:(g + 1) * COLS])
            for g in range(4):
                sp.wait_ge(evac_dve, 2 + n_ple + 2 * g + 2)
                sp.dma_start(out.rearrange("(b p) n -> p b n", p=P)[:, :, g * COLS:(g + 1) * COLS],
                             xres[:, :, g * COLS:(g + 1) * COLS]).then_inc(S(f"stored{g}"), 16)
            for g in range(4):
                sp.wait_ge(S(f"stored{g}"), 16)

        X_QKT, X_L, X_ZS, X_SBC = 0, 1024, 1792, 3328
        X_L2, X_PT = 1024, 3328
        proj1 = big[:].rearrange("p (b n) -> p b n", b=TB)
        proj2 = big[:, 0:TB * PROJ2].rearrange("p (b n) -> p b n", b=TB)
        T2 = TB * PROJ2
        side1 = region(big, 3072, DC * 16).rearrange("p (k n) -> p k n", k=DC)
        side2 = region(big, 3072, DC * 8).rearrange("p (k n) -> p k n", k=DC)
        route = region(big, 2048, DC * 36).rearrange("p (k n) -> p k n", k=DC)
        dil_mask = [proj1[:, j, 0:3 * 384].rearrange("p (h n) -> p h n", h=3) for j in range(2)]
        G_R, G_MASK, G_W, G_B, G_AT, G_OG = 0, 384, 448, 960, 1472, 1728
        F_QKT, F_L, F_PT, F_CROW, F_NEGROW, F_CAUS, F_U = (T2, T2 + 1024, T2 + 1792, T2 + 2560, T2 + 4608,
                                                            T2 + 4736, T2 + 4864)
        side_t = {1: region(xf, 1280, 256), 2: region(big, T2, 256), 3: region(big, 5376, 256)}
        R_RXP, R_W = T2, T2 + 2080

        @block.gpsimd
        def _(pool):
            def fetch(name, dst, src):
                pool.dma_start(dst, src).then_inc(S(name), 16)

            wait_stage(pool, ST_LOAD)
            fetch("side1_landed", side1, w_in_v[:, :, A_COL:A_COL + 16])
            wait_stage(pool, ST_PROJ1)
            fetch("sbc_landed", region(xf, X_SBC, 3 * P), I["consts"][:, C_U:C_U + 3 * P])
            wait_stage(pool, ST_SB)
            for j in range(2):
                at = C_DIL + j * 3 * 384
                fetch("dmask_landed", proj1[:, j, 0:3 * 384], I["consts"][:, at:at + 3 * 384])
            wait_stage(pool, ST_DIL)
            fetch("glac_landed", region(xf, G_R, 448), I["consts"][:, C_R:C_R + 448])
            fetch("glac_landed", xf[0:16, G_W:G_W + 512], I["w_gla_a"])
            fetch("glac_landed", xf[0:1, G_B:G_B + 512], I["b_gla_a"].rearrange("(a n) -> a n", a=1))
            wait_stage(pool, ST_BRANCH)
            fetch("x_back", xres[:], I["x"].rearrange("(b p) n -> p b n", p=P))
            wait_stage(pool, ST_OUT1)
            fetch("side2_landed", side2, w_in2_v[:, :, PROJ2_QKV:PROJ2_QKV + F_COLS])
            fetch("side2_landed", forget_bias[:], I["b_forget_2"].rearrange("(a n) -> a n", a=1))
            wait_stage(pool, ST_PROJ2)
            fetch("foxc_landed", region(big, F_CAUS, 2 * P), I["consts"][:, C_CAUSNEG:C_CAUSNEG + 2 * P])
            wait_stage(pool, ST_FOX)
            wrec = region(big, R_W, 2048).rearrange("p (g k n) -> p g k n", g=2, k=RNN_CHUNKS)
            fetch("wrec_landed", wrec[:, 0], I["w_rec_gate_2"].rearrange("k p n -> p k n"))
            fetch("wrec_landed", wrec[:, 1], I["w_in_gate_2"].rearrange("k p n -> p k n"))
            pool.wait_ge(S("rnn_lo"), 2)
            fetch("route_landed", route[:, :, 0:4], I["w_router_group_2"].rearrange("(p k) n -> p k n", k=DC))
            fetch("route_landed", route[:, :, 4:36], I["w_router_expert_2"].rearrange("(p k) n -> p k n", k=DC))
            wait_stage(pool, ST_MOE)
            fetch("p_landed", region(big, 0, 512).rearrange("p (b n) -> p b n", b=TB),
                  I["p_2"].rearrange("(b p) n -> p b n", p=P))

        vrows = region(big, 0, 3 * P)
        acc = region(big, 1024, 2 * COLS).rearrange("p (r n) -> p r n", r=2)
        acc2 = region(xf, 256, 2 * COLS).rearrange("p (r n) -> p r n", r=2)
        N_JUNK, N_XN = 6144, 10240
        xn = region(big, N_XN, TB * D).rearrange("p (b n) -> p b n", b=TB)
        htmp = region(big, 14336, 4 * TB * P).rearrange("p (r n) -> p r n", r=4)
        gate_bc = {"g1": region(big, 12288, D), "g2": region(big, 4096, D)}
        gate_dg = region(big, 8192, D)
        ysum = region(big, 0, TB * D).rearrange("p (b n) -> p b n", b=TB)
        gsig = region(big, TB * D, 3 * TB * COLS).rearrange("p (i b n) -> p i b n", i=3, b=TB)
        ymul = region(big, TB * D + 3 * TB * COLS, TB * COLS).rearrange("p (b n) -> p b n", b=TB)
        silu_g = region(big, 0, TB * HID).rearrange("p (b n) -> p b n", b=TB)
        hid = region(big, 512, TB * HID).rearrange("p (b n) -> p b n", b=TB)
        prod = region(big, 1024, TB * COLS).rearrange("p (b n) -> p b n", b=TB)
        comb = region(big, 2048 + 2048, TB * N_EXPERTS).rearrange("p (b n) -> p b n", b=TB)
        rt = region(big, 4352, 1024)

        GATE_NO = {"g1": 1, "g2": 2, "n1": 1, "n2": 2}
        NORMS = {
            "n1": dict(no=0, stats=0, src=xres, gain=geff, bias=modt[:, 0:16], norm=True),
            "y": dict(no=1, src=ysum, gain=None, bias=None, norm=False),
            "n2": dict(no=2, stats=1, src=xres, gain=geff, bias=modt[:, 48:64], norm=True),
            "n3": dict(no=3, stats=2, src=xres, gain=vec[:, V_MIX:V_MIX + 16], bias=None, norm=True),
            "n4": dict(no=4, stats=3, src=xres, gain=gain_ffn2[:], bias=None, norm=True, strided=True),
            "n5": dict(no=5, stats=4, src=xres, gain=vec[:, V_PLE:V_PLE + 16], bias=None, norm=True),
        }

        def att_cols(kind, h):
            if kind == "sb":
                return proj1, h * DH, 768 + h * DH, 1536 + h * DH
            if kind == "dil":
                return proj1, 2304 + h * DH, 3072 + h * DH, 3840 + h * DH
            return proj2, h * DH, 1024 + h * DH, 2048 + h * DH

        HEAD0 = {"sb": 0, "dil": 0, "fox": 6}
        UNIT0 = {"sb": 0, "dil": 0, "fox": 2}
        NORM_NO = {"sb": 0, "fox": 1}

        def att(kind):
            return "sb" if kind == "sb" else "att"

        def finished_unit(n, per, later):
            w, rest = divmod(n - later, per)
            return w - 1 if rest == 0 and w >= 1 else None

        ATT = {
            "dil": dict(units=DIL_SLOTS, per=DIL_GROUPS, head=lambda u, i: i * 2 + u, qkt=region(xf, X_QKT, 1024),
                        logit=region(xf, X_L2, 2304), pt=region(xf, X_PT, 768), dst=6),
            "fox": dict(units=FOX_HEADS, per=1, head=lambda u, i: u, qkt=region(big, F_QKT, 1024),
                        logit=region(big, F_L, 768), pt=region(big, F_PT, 768), dst=0),
        }
        for a in ATT.values():
            a["qkt"] = a["qkt"].rearrange("p (r i n) -> p r i n", r=2, i=2)
            a["logit"] = a["logit"].rearrange("p (r h n) -> p r h n", r=2, h=a["per"])
            a["pt"] = a["pt"].rearrange("p (r n) -> p r n", r=2)
        qkt_sb = region(xf, X_QKT, 1024).rearrange("p (r i n) -> p r i n", r=2, i=2)
        l_sb = region(xf, X_L, 768).rearrange("p (r n) -> p r n", r=2)
        z_sb = region(xf, X_ZS, 768).rearrange("p (r n) -> p r n", r=2)
        u_tri, strict, strictneg = (region(xf, X_SBC + i * P, P) for i in range(3))
        negones = region(xf, X_SBC + 3 * P, P)
        negtri = region(xf, X_SBC + 4 * P, P)
        SQ1 = region(xf, 256, 3072).rearrange("p (r n) -> p r n", r=2)
        SQ2F = region(big, T2, 2048).rearrange("p (r n) -> p r n", r=2)
        f_logit = stat[:, 48:64].rearrange("p (b n) -> p b n", b=TB)

        A0, A1 = proj1[:, 0, 0:4608], proj1[:, 1, 0:4608]
        gl_ls = A0[:, 0:1024].rearrange("p (b n) -> p b n", b=TB)
        gl_qm = A0[:, 1024:2048].rearrange("p (h n) -> p h n", h=4)
        gl_km = A0[:, 2048:3072].rearrange("p (h n) -> p h n", h=4)
        gl_qc = A0[:, 3072:4096].rearrange("p (h n) -> p h n", h=4)
        gl_sc = A0[:, 4096:4608].rearrange("p (s n) -> p s n", s=8)
        gl_kd = A1[:, 0:1024].rearrange("p (b n) -> p b n", b=TB)
        gl_st = A1[:, 1024:3072].rearrange("p (r h n) -> p r h n", r=2, h=4)
        gl_ex = A1[:, 3072:4608].rearrange("p (r e n) -> p r e n", r=2, e=3)
        gl_og = region(xf, G_OG, 2048).rearrange("p (b n) -> p b n", b=TB)
        gl_tmp = region(xf, G_OG, 1024).rearrange("p (b n) -> p b n", b=TB)
        gl_a = gl_a16[:].rearrange("p (b n) -> p b n", b=TB)
        gl_sq = A0[:, 0:2048].rearrange("p (b n) -> p b n", b=TB)
        gl_htmp = A0[:, 2048:3072].rearrange("p (r n) -> p r n", r=4)
        gl_at = xf[0:16, G_AT:G_AT + 256]
        gl_el = stat[:, 32:48].rearrange("p (h c) -> p h c", h=4)
        gl_ss = stat[:, 48:56]

        def chunks(off):
            return region(big, off, 2048).rearrange("p (k n) -> p k n", k=RNN_CHUNKS)
        r_xp = region(big, R_RXP, 2080).rearrange("p (k n) -> p k n", k=RNN_CHUNKS)
        r_xc, r_rg = chunks(0), chunks(5120)
        r_a = region(big, R_RXP, 2048).rearrange("p (k n) -> p k n", k=RNN_CHUNKS)
        r_r, r_i = chunks(3072), chunks(8192)
        r_g = chunks(R_W)
        r_m = [region(big, off, 1024).rearrange("p (k n) -> p k n", k=4) for off in (2048, 7168)]
        RNN_HALVES = (slice(0, 4), slice(4, 8))
        r_w = region(big, R_W, 2048).rearrange("p (g k n) -> p g k n", g=2, k=RNN_CHUNKS)
        r_k8 = stat[:, 0:8]
        r_nk8 = stat[:, 8:16]

        def side_parts(n):
            return tuple(t[:, 0:3, :].rearrange("p a b -> p (a b)")[:, 0:DC * n].rearrange("p (k n) -> p k n", k=DC)
                         for t in (bhi, blo))

        @block.tensor
        def _(pe):
            mm = nc.tensor.matmul

            def products(t, r, parts, banks, first, last, slot=None):
                pe.wait_ge(lo_ready, r * 8 + (t + 1))
                s = (t if slot is None else slot) % 4
                for c, (shi, slo, kc) in enumerate(parts):
                    for b in range(TB):
                        T = slice(b * P, (b + 1) * P)
                        o = bank[banks[b]][:]
                        st, en = first and c == 0, last and c == len(parts) - 1
                        mm(o, shi[:, kc, T], whi[:, s, c], start=st, stop=False)
                        mm(o, shi[:, kc, T], wlo[:, s, c], start=False, stop=False)
                        ins = mm(o, slo[:, kc, T], whi[:, s, c], start=False, stop=en)
                ins.then_inc(tile_used, 1)

            def group_free(n):
                pe.wait_ge(evac_act, n + 1)
                pe.wait_ge(evac_dve, n + 1)

            def gemm_tile(t0, n0, shi, slo):
                def tile(k, g, par):
                    if k == 0:
                        group_free(n0 + g)
                    products(t0 + k, g, [(shi, slo, 2 * k), (shi, slo, 2 * k + 1)], (2 * par, 2 * par + 1),
                             k == 0, k == 7)
                return tile

            def norm(key):
                cfg = NORMS[key]
                src = xn if cfg["norm"] else cfg["src"]
                if cfg["norm"]:
                    pe.wait_ge(S("norm_xn"), 2 * cfg["stats"] + 2)
                for k in range(DC):
                    if k >= 4:
                        pe.wait_ge(S("norm_h"), 16 * cfg["no"] + k - 3)
                    for b in range(TB):
                        col = slice(k, D, DC) if cfg.get("strided") else slice(k * P, (k + 1) * P)
                        ins = nc.tensor.transpose(bank[4 + k % 4][:, b * P:(b + 1) * P], src[:, b, col], ident[:])
                    ins.then_inc(S("norm_T"), 1)

            def gate_broadcast(key):
                pe.wait_ge(S("gate_gd"), DC * GATE_NO[key])
                for q in range(4):
                    if q >= 2:
                        pe.wait_ge(S("gate_bc"), 4 * (GATE_NO[key] - 1) + q - 1)
                    mm(bank[6 + q % 2][:], ones[:, 0:P], gate_dg[:, q * COLS:(q + 1) * COLS], start=True, stop=True)\
                        .then_inc(S("gate_gb"), 1)

            def normed(key, chunks=DC):
                pe.wait_ge(S("norm_lo"), 8 * NORMS[key]["no"] + chunks // 2)

            def side(n, no, bias=None):
                pe.wait_ge(S("side_lo"), no)
                shi, slo = side_parts(n)
                o = bank[6][0:n, 0:256]
                for k in range(DC):
                    mm(o, shi[:, k, 0:n], ahi[:, k], start=(k == 0), stop=False)
                    mm(o, shi[:, k, 0:n], alo[:, k], start=False, stop=False)
                    ins = mm(o, slo[:, k, 0:n], ahi[:, k], start=False, stop=(k == DC - 1 and bias is None))
                if bias is not None:
                    ins = mm(o, bias, ones[0:1, :], start=False, stop=True)
                ins.then_inc(S("side_mm"), 1)
                pe.wait_ge(S("side_t"), no)
                for b in range(TB):
                    ins = nc.tensor.transpose(bank[7][:, b * n:(b + 1) * n], side_t[no][0:n, b * P:(b + 1) * P],
                                              ident[0:n, 0:n])
                ins.then_inc(S("side_done"), 1)

            def qk_transposes(kind, h, n):
                src, q, k, _ = att_cols(kind, h)
                if n >= 2:
                    pe.wait_ge(S(att(kind) + "_qkt"), 2 * HEAD0[kind] + 2 * (n - 1))
                for i, col in enumerate((q, k)):
                    for b in range(TB):
                        ins = nc.tensor.transpose(bank[n % 2][:, i * 256 + b * P:i * 256 + (b + 1) * P],
                                                  src[:, b, col:col + DH], ident[:])
                ins.then_inc(S(att(kind) + "_T"), 1)

            def start(key, tile):
                for k in range(4):
                    normed(key, 4 * (k + 1) if k < 3 else DC)
                    tile(k, 0, 0)

            pe.wait_ge(S("small_landed"), 16 * 20)
            pe.wait_ge(S("ones_set"), 4)
            nc.tensor.transpose(bank[0][:, 0:96], vrows[0:96, 0:P], ident[0:96, 0:96])
            nc.tensor.transpose(bank[0][:, 96:224], vrows[:, P:2 * P], ident[:])
            nc.tensor.transpose(bank[0][:, 224:248], vrows[0:24, 2 * P:3 * P], ident[0:24, 0:24])\
                .then_inc(S("vec_T"), 1)
            stage_end(pe, "pe")

            def ada_columns(done, n, src, dst):
                pe.wait_ge(lo_ready, done)
                pe.wait_ge(S("mod_done"), n + 1)
                for j in range(4):
                    ins = mm(dst[:, j:j + 1], src[:, j * P:(j + 1) * P], ones[:, 0:1], start=True, stop=True)
                ins.then_inc(S("ada_cols"), 1)
            with pe.Fori(0, ADA_FIRST // 2) as i:
                for par in range(2):
                    ada_columns(i * 16 + (8 + 8 * par), i * 2 + par, acc[:, par], bank[par])
            ada_columns(8 * ADA_FIRST, ADA_FIRST - 1, acc[:, 0], bank[0])
            stage_end(pe, "pe")

            norm("n1")
            def proj1_tile(k, g, par):
                is_product, j = PROJ1_ORDER[k]
                if is_product:
                    half = j // 8
                    if j % 8 == 0:
                        group_free(g * 2 + (n_proj1 + half))
                    products(t_proj1 + k, g * 3, [(ahi, alo, 2 * (j % 8)), (ahi, alo, 2 * (j % 8) + 1)],
                             (2 * half, 2 * half + 1), j % 8 == 0, j % 8 == 7, j)

            def proj1_ada(g, par):
                ada_columns(g * 24 + (t_proj1 + 24), g + ADA_FIRST, acc2[:, par], bank[6 + par])

            def proj1_last(k):
                if k == 0:
                    group_free(n_proj1 + 14)
                products(t_proj1 + 7 * 24 + k, 0, [(ahi, alo, 2 * k), (ahi, alo, 2 * k + 1)], (0, 1), k == 0, k == 7, k)
            start("n1", proj1_tile)
            drive(pe, 7, 24, proj1_tile, {23: proj1_ada}, proj1_last, prologue=False)
            for k in range(4, 8):
                proj1_last(k)
            side(16, 1)
            stage_end(pe, "pe")

            H = SB_HEADS
            pe.wait_ge(S("sb_scaled"), 1)
            for i in range(H + 3):
                if i < H:
                    qk_transposes("sb", i, i)
                h = i - 1
                if 0 <= h < H:
                    pe.wait_ge(S("sb_qkt"), 2 * (h + 1))
                    if h >= 2:
                        pe.wait_ge(S("sb_sp"), h - 1)
                    q, k = qkt_sb[:, h % 2, 0], qkt_sb[:, h % 2, 1]
                    mm(bank[2 + h % 2][:, 0:256], k[:, 0:P], q[:, 0:256], start=True, stop=True)
                    mm(bank[2 + h % 2][:, 256:384], k[:, P:256], q[:, P:256], start=True, stop=True)\
                        .then_inc(S("sb_z"), 1)
                h = i - 2
                if 0 <= h < H:
                    pe.wait_ge(S("sb_spm"), h + 1)
                    if h >= 2:
                        pe.wait_ge(S("sb_e"), h - 1)
                    sp_, C = l_sb[:, h % 2], bank[4 + h % 2]
                    mm(C[:, 0:P], negtri, sp_[:, 0:P], start=True, stop=True)
                    mm(C[:, P:256], negtri, sp_[:, P:256], start=True, stop=False)
                    mm(C[:, P:256], negones, sp_[:, 256:384], start=False, stop=True)
                    mm(C[:, 256:384], negtri, sp_[:, 256:384], start=True, stop=True).then_inc(S("sb_c"), 1)
                h = i - 3
                if 0 <= h < H:
                    pe.wait_ge(S("sb_w"), h + 1)
                    if h >= 2:
                        pe.wait_ge(S("sb_out"), h - 1)
                    _, _, _, v = att_cols("sb", h)
                    W, O = z_sb[:, h % 2], bank[6 + h % 2]
                    mm(O[:, 0:P], proj1[:, 0, v:v + DH], W[:, 0:P], start=True, stop=True)
                    mm(O[:, P:256], proj1[:, 0, v:v + DH], W[:, P:256], start=True, stop=False)
                    mm(O[:, P:256], proj1[:, 1, v:v + DH], W[:, 256:384], start=False, stop=True).then_inc(S("sb_o"), 1)
            stage_end(pe, "pe")

            def pv(kind, u, i):
                a = ATT[kind]
                per, n = a["per"], u * a["per"] + i
                pe.wait_ge(S(att(kind) + "_pt"), HEAD0[kind] + n + 1)
                if i == 0 and u >= 2:
                    pe.wait_ge(S(att(kind) + "_out"), UNIT0[kind] + u - 1)
                src, _, _, v = att_cols(kind, a["head"](u, i))
                T, O = a["pt"][:, n % 2], bank[6 + u % 2]
                mm(O[:, 0:P], src[:, 0, v:v + DH], T[:, 0:P], start=(i == 0), stop=False, skip_group_check=True)
                mm(O[:, P:256], src[:, 0, v:v + DH], T[:, P:256], start=False, stop=False, skip_group_check=True)
                ins = mm(O[:, P:256], src[:, 1, v:v + DH], T[:, 256:384], start=False, stop=(i == per - 1),
                         skip_group_check=True)
                ins.then_inc(S(att(kind) + "_O"), 1)

            def attention(kind):
                a = ATT[kind]
                U, per = a["units"], a["per"]
                fox = kind == "fox"
                qk_transposes(kind, a["head"](0, 0), 0)
                for n in range(U * per + 2):
                    if n + 1 < U * per:
                        qk_transposes(kind, a["head"](*divmod(n + 1, per)), n + 1)
                    if n < U * per:
                        pe.wait_ge(S(att(kind) + "_qkt"), 2 * HEAD0[kind] + 2 * (n + 1))
                        if n >= 2:
                            pe.wait_ge(S(att(kind) + "_log"), HEAD0[kind] + n - 1)
                        q, k, Z = a["qkt"][:, n % 2, 0], a["qkt"][:, n % 2, 1], bank[2 + n % 2]
                        for qs, ks, zs in ((slice(0, P), slice(0, P), slice(0, P)),
                                           (slice(P, 256), slice(0, 256), slice(P, 384))):
                            ins = mm(Z[:, zs], q[:, qs], k[:, ks], start=True, stop=not fox)
                            if fox:
                                c = big[0:1, F_CROW + n * 256:F_CROW + (n + 1) * 256]
                                mm(Z[:, zs], c[:, qs], fox_ones[:, ks], start=False, stop=False)
                                ins = mm(Z[:, zs], fox_neg, c[:, ks], start=False, stop=True)
                        ins.then_inc(S(att(kind) + "_S"), 1)
                    w = finished_unit(n, per, 1)
                    if w is None:
                        continue
                    pe.wait_ge(S(att(kind) + "_P"), UNIT0[kind] + w + 1)
                    for i in range(per + 1):
                        if i < per:
                            m = w * per + i
                            if m >= 2:
                                pe.wait_ge(S(att(kind) + "_pt"), HEAD0[kind] + m - 1)
                            L = a["logit"][:, w % 2, i]
                            for j in range(3):
                                ins = nc.tensor.transpose(bank[4 + m % 2][:, j * P:(j + 1) * P],
                                                          L[:, j * P:(j + 1) * P], ident[:])
                            ins.then_inc(S(att(kind) + "_PT"), 1)
                        if i >= 1:
                            pv(kind, w, i - 1)

            attention("dil")
            stage_end(pe, "pe")

            pe.wait_ge(S("glac_landed"), 48)
            for b in range(TB):
                ins = nc.tensor.transpose(bank[0][0:16, b * P:(b + 1) * P], gl_a[:, b, :], ident[:])
            ins.then_inc(S("gl_aT"), 1)
            pe.wait_ge(S("gl_at"), 1)
            for b in range(TB):
                mm(bank[2 + b][:], gl_at[:, b * P:(b + 1) * P], xf[0:16, G_W:G_W + 512], start=True, stop=False)
                ins = mm(bank[2 + b][:], ones[0:1, 0:P], xf[0:1, G_B:G_B + 512], start=False, stop=True)
                ins.then_inc(S("gl_alin"), 1)
            pe.wait_ge(S("gl_ls"), 2)
            R = region(xf, G_R, 384)
            for b in range(TB):
                mm(bank[2 + b][:], R[:, 256:384], gl_ls[:, b, :], start=True, stop=True).then_inc(S("gl_lc"), 1)
            for h in range(GLA_HEADS):
                if h >= 2:
                    pe.wait_ge(S("gl_qkm"), h - 1)
                    pe.wait_ge(S("gl_ex"), 2 * (h - 1))
                for i, col in enumerate((4608 + h * P, 5120 + h * P)):
                    for b in range(TB):
                        nc.tensor.transpose(bank[h % 2][:, i * 256 + b * P:i * 256 + (b + 1) * P],
                                            proj1[:, b, col:col + P], ident[:])
                for b in range(TB):
                    ins = mm(bank[4 + h % 2][:, b * 256:(b + 1) * 256], gl_ls[:, b, h * P:(h + 1) * P], R[:, 0:256],
                             start=True, stop=True)
                ins.then_inc(S("gl_cum"), 1)
            for h in range(GLA_HEADS):
                pe.wait_ge(S("gl_qkm"), h + 1)
                for c in range(4):
                    b, rows = c // 2, slice(64 * (c % 2), 64 * (c % 2) + 64)
                    tok = slice(c * 64, (c + 1) * 64)
                    ins = mm(bank[6][rows, (h * 2 + b) * 64:(h * 2 + b + 1) * 64], gl_km[:, h, tok], gl_qm[:, h, tok],
                             start=True, stop=True)
            ins.then_inc(S("gl_sT"), 1)
            pe.wait_ge(S("gl_sc"), 1)
            pe.wait_ge(S("gl_kd"), 2)
            for c in range(4):
                b, rows = c // 2, slice(64 * (c % 2), 64 * (c % 2) + 64)
                tok = slice(c * 64, (c + 1) * 64)
                for h in range(GLA_HEADS):
                    v = 5632 + h * DV
                    O = bank[h][rows, 0:DV]
                    if c > 0:
                        pe.wait_ge(S("gl_og"), 4 * (c - 1) + h + 1)
                        pe.wait_ge(S("gl_state"), 4 * (c - 1) + h + 1)
                    mm(O, gl_sc[rows, h * 2 + b, :], proj1[rows, b, v:v + DV], start=True, stop=(c == 0))
                    if c > 0:
                        ins = mm(O, gl_qc[:, h, tok], gl_st[:, (c - 1) % 2, h], start=False, stop=True)
                    if c < 3:
                        ins = mm(bank[4 + h][:, 0:DV], gl_kd[rows, b, h * P:(h + 1) * P], proj1[rows, b, v:v + DV],
                                 start=True, stop=True)
                    ins.then_inc(S("gl_o"), 1)
            pe.wait_ge(S("gl_fin"), 1)
            for k in range(8):
                if k >= 4:
                    pe.wait_ge(S("gl_h"), k - 3)
                for b in range(TB):
                    ins = nc.tensor.transpose(bank[k % 4][:, b * P:(b + 1) * P], gl_og[:, b, k * P:(k + 1) * P], ident[:])
                ins.then_inc(S("gl_T"), 1)
            stage_end(pe, "pe")

            plan, base = [], 0
            for i in range(3):
                for s in range(8):
                    plan.append((2 * i, ahi, alo, 2 * s, s == 0, s == 7))
                for s in range(BR_TILES[i]):
                    plan.append((2 * i + 1, bhi, blo, base + 2 * s, s == 0, s == BR_TILES[i] - 1))
                base += 2 * BR_TILES[i]

            def branch_tile(k, g, par):
                is_product, tile = BRANCH_ORDER[k]
                if not is_product:
                    return
                j, shi, slo, kc, first, last = plan[tile]
                if first:
                    pe.wait_ge(evac_act, g * 6 + (n_branch + j))
                    pe.wait_ge(evac_dve, g * 6 + (n_branch + j))
                products(t_branch + k, g * 6, [(shi, slo, kc), (shi, slo, kc + 1)], (2 * (j % 3), 2 * (j % 3) + 1),
                         first, last, tile)

            def branch_ada(half):
                return lambda g, par: ada_columns(g * 48 + (t_branch + (26, 48)[half]), g * 2 + (ADA_FIRST + 7 + half),
                                                  acc2[:, half], bank[6 + half])
            for k in range(4):
                branch_tile(k, 0, 0)
            gate_broadcast("g1")
            drive(pe, 4, 48, branch_tile, {26: branch_ada(0), 47: branch_ada(1)}, prologue=False, single=True)
            stage_end(pe, "pe")
            norm("y")
            start("y", gemm_tile(t_out1, n_out1, ahi, alo))
            drive(pe, 4, 8, gemm_tile(t_out1, n_out1, ahi, alo), prologue=False)
            stage_end(pe, "pe")

            def hidden_rounds(t0, n0, parts, rnd, prefix, q0, first=None):
                def up_tile(k, g, par):
                    if k == 0:
                        group_free(rnd * 12 + g + n0)
                    products(t0 + k, rnd * 12 + g, [(ahi, alo, 2 * k), (ahi, alo, 2 * k + 1)],
                             (2 * par, 2 * par + 1), k == 0, k == 7)

                def turn(g, par):
                    pe.wait_ge(evac_dve, rnd * 12 + g + (n0 + 3))
                    for c in range(2):
                        for b in range(TB):
                            ins = nc.tensor.transpose(bank[4][:, c * 256 + b * P:c * 256 + (b + 1) * P],
                                                      hid[:, b, c * P:(c + 1) * P], ident[:])
                    ins.then_inc(S(prefix + "_hidT"), 1)

                def down_tile(i):
                    g, k = divmod(i, parts)
                    if k == 0:
                        group_free(rnd * 12 + (n0 + parts + g))
                    if i == parts - 1:
                        pe.wait_ge(S(prefix + "_hsplit"), rnd * 8 + (q0 + parts))
                    products(t0 + 8 * parts + i, rnd * 12, [(bhi, blo, 2 * k), (bhi, blo, 2 * k + 1)],
                             (2 * (g % 2), 2 * (g % 2) + 1), k == 0, k == parts - 1)
                if first:
                    start(first, up_tile)
                    if prefix == "ffn":
                        gate_broadcast("g2")
                drive(pe, parts, 8, up_tile, {9: turn}, down_tile, prologue=not first)
                for i in range(4, 4 * parts):
                    down_tile(i)

            norm("n2")
            hidden_rounds(t_ffn, n_ffn, 8, 0, "ffn", 0, "n2")
            hidden_rounds(t_ffn + 96, n_ffn + 12, 8, 0, "ffn", 8)
            hidden_rounds(t_ffn + 192, n_ffn + 24, 6, 0, "ffn", 16)
            stage_end(pe, "pe")

            norm("n3")
            start("n3", gemm_tile(t_proj2, n_proj2, ahi, alo))
            drive(pe, 10, 8, gemm_tile(t_proj2, n_proj2, ahi, alo), prologue=False)
            pe.wait_ge(S("side2_landed"), 32)
            side(8, 2, forget_bias[:])
            stage_end(pe, "pe")

            fox_tri = region(big, F_U, P)
            fox_neg = big[0:1, F_NEGROW:F_NEGROW + P]
            fox_ones = ones[0:1, :]
            pe.wait_ge(S("foxc_landed"), 16)
            for h in range(FOX_HEADS):
                C = bank[h // 2][0:1, (h % 2) * 256:(h % 2) * 256 + 256]
                mm(C[:, 0:P], f_logit[:, 0, h:h + 1], fox_tri, start=True, stop=True)
                mm(C[:, P:256], f_logit[:, 0, h:h + 1], ones[:, 0:P], start=True, stop=False)
                ins = mm(C[:, P:256], f_logit[:, 1, h:h + 1], fox_tri, start=False, stop=True)
            ins.then_inc(S("fox_c"), 1)
            pe.wait_ge(S("fox_crow"), 4)
            pe.wait_ge(S("fox_scaled"), 1)
            attention("fox")
            stage_end(pe, "pe")

            def rnn_turn(n):
                if n >= 4:
                    pe.wait_ge(S("rnn_copied"), n - 3)
                for b in range(TB):
                    ins = nc.tensor.transpose(bank[n % 4][:, b * P:(b + 1) * P],
                                              proj2[:, b, 3072 + n * P:3072 + (n + 1) * P], ident[:])
                ins.then_inc(S("rnn_T"), 1)

            for n in range(2 * RNN_CHUNKS):
                rnn_turn(n)
            pe.wait_ge(S("wrec_landed"), 32)
            for k in range(RNN_CHUNKS):
                pe.wait_ge(S("rnn_xc"), k + 1)
                if k >= 4:
                    pe.wait_ge(S("rnn_sig"), 2 * (k - 3))
                mm(bank[4 + k % 4][:, 0:256], r_w[:, 0, k], r_xc[:, k], start=True, stop=True)
                mm(bank[4 + k % 4][:, 256:512], r_w[:, 1, k], r_xc[:, k], start=True, stop=True)\
                    .then_inc(S("rnn_lin"), 1)

            pe.wait_ge(S("rnn_copied"), 16)

            def out2_tile(k, g, par):
                if k in (4, 6):
                    pe.wait_ge(S("rnn_lo"), 1 + (k - 4) // 2)
                gemm_tile(t_out2, n_out2, bhi, blo)(k, g, par)
            drive(pe, 4, 8, out2_tile)
            stage_end(pe, "pe")
            norm("n4")
            normed("n4")
            pe.wait_ge(S("norm_h"), 16 * 5)
            side(36, 3)
            hidden_rounds(t_moe, n_moe, 8, 0, "moe", 0, "n4")
            with pe.Fori(0, 3) as rnd:
                hidden_rounds(t_moe + 96, n_moe + 12, 8, rnd, "moe", 8)
            stage_end(pe, "pe")
            norm("n5")
            pe.wait_ge(S("p_landed"), 16)
            for k in range(2):
                for b in range(TB):
                    ins = nc.tensor.transpose(bank[3][:, k * 256 + b * P:k * 256 + (b + 1) * P],
                                              big[:, b * 256 + k * P:b * 256 + (k + 1) * P], ident[:])
            ins.then_inc(S("p_T"), 1)
            for g in range(4):
                for half in range(2):
                    group_free(n_ple + 2 * g + half)
                    for k in range(8 if half == 0 else 1):
                        shi, slo = (ahi, alo) if half == 0 else (bhi, blo)
                        if g == 0 and half == 0 and k < 4:
                            normed("n5", 4 * (k + 1))
                        if g == 0 and half == 1:
                            pe.wait_ge(S("p_lo"), 1)
                        products(t_ple + 9 * g + 8 * half + k, 0, [(shi, slo, 2 * k), (shi, slo, 2 * k + 1)],
                                 (2 * half, 2 * half + 1), k == 0, k == (7 if half == 0 else 0))

        @block.scalar
        def _(act):
            A = nc.scalar.activation
            chain = Chain(act, "act_chain")

            def split_item(t, r, u, ru):
                act.wait_ge(landed[t % 8], r * 16 + 16 * (t // 8 + 1))
                act.wait_ge(tile_used, ru * 8 + (u + 1))
                A(whi[:, u % 4], raw[:, t % 8], ACT.Copy).then_inc(hi_ready, 1)

            def split_hi(t, r, up=False):
                act.wait_ge(landed[t % 8], r * 16 + 16 * (t // 8 + 1))
                if up is not False:
                    act.wait_ge(landed_up[t % 8], up)
                act.wait_ge(tile_used, r * 8 + (t - T_ADA + 1))
                A(whi[:, t % 4], raw[:, t % 8], ACT.Copy).then_inc(hi_ready, 1)

            def gemm_split(t0):
                return lambda k, g, par: split_hi(t0 + k, g)

            def side_hi(src, n, name, count):
                act.wait_ge(S(name), count)
                A(side_parts(n)[0], src, ACT.Copy).then_inc(S("side_hi"), 1)

            def ffn_first(k):
                split_hi(t_ffn + k, 0, 16)

            def moe_first(k):
                split_hi(t_moe + k, 0, 16 * (FFN_PARTS + 1))

            def norm_stats(key):
                cfg = NORMS[key]
                for b in range(TB):
                    A(region(big, N_JUNK + b * D, D), cfg["src"][:, b], ACT.Square,
                      accum_out=stat[:, b:b + 1]).then_inc(S("norm_ss"), 1)
                act.wait_ge(S("norm_var"), cfg["stats"] + 1)
                A(stat[:, 4:6], stat[:, 2:4], ACT.Sqrt).then_inc(S("norm_std"), 1)

            def norm_chunks(key):
                cfg = NORMS[key]
                for k in range(DC):
                    act.wait_ge(S("norm_T"), 16 * cfg["no"] + k + 1)
                    if k >= 4:
                        act.wait_ge(S("norm_lo"), 8 * cfg["no"] + k // 2 - 1)
                    if k == 0 and key in ("n1", "n2"):
                        act.wait_ge(S("gate_geff"), GATE_NO[key])
                    kw = {}
                    if cfg["gain"] is not None:
                        kw["scale"] = cfg["gain"][:, k:k + 1]
                    if cfg["bias"] is not None:
                        kw["bias"] = cfg["bias"][:, k:k + 1]
                    A(htmp[:, k % 4], bank[4 + k % 4][:, 0:256], ACT.Identity if kw else ACT.Copy, **kw)\
                        .then_inc(S("norm_h"), 1)

            def norm(key):
                if NORMS[key]["norm"]:
                    norm_stats(key)
                norm_chunks(key)

            def gate_broadcast(key):
                for q in range(4):
                    act.wait_ge(S("gate_gb"), 4 * (GATE_NO[key] - 1) + q + 1)
                    A(gate_bc[key][:, q * COLS:(q + 1) * COLS], bank[6 + q % 2][:], ACT.Copy).then_inc(S("gate_bc"), 1)

            def side_turn(no, n):
                act.wait_ge(S("side_mm"), no)
                A(side_t[no][0:n, :], bank[6][0:n, 0:256], ACT.Copy).then_inc(S("side_t"), 1)
                act.wait_ge(S("side_done"), no)

            def qk_squares(kind, groups, sq):
                for n, (src, b, col, w) in enumerate(groups):
                    if n >= 2:
                        act.wait_ge(S("qk_sqsum"), 4 * NORM_NO[kind] + n - 1)
                    A(sq[:, n % 2, 0:w], src[:, b, col:col + w], ACT.Square).then_inc(S("qk_sq"), 1)
                act.wait_ge(S("qk_var"), NORM_NO[kind] + 1)
                A(stat[:, 0:48], stat[:, 0:48], ACT.Sqrt).then_inc(S("qk_std"), 1)

            def attention(kind):
                a = ATT[kind]
                U, per = a["units"], a["per"]
                for n in range(U * per + 2):
                    w = finished_unit(n, per, 1)
                    if w is not None:
                        for i in range(per):
                            m = w * per + i
                            act.wait_ge(S(att(kind) + "_PT"), HEAD0[kind] + m + 1)
                            if m >= 2:
                                act.wait_ge(S(att(kind) + "_O"), HEAD0[kind] + m - 1)
                            A(a["pt"][:, m % 2], bank[4 + m % 2][:, 0:384], ACT.Copy).then_inc(S(att(kind) + "_pt"), 1)
                    u = finished_unit(n, per, -1)
                    if u is not None and u < U:
                        act.wait_ge(S(att(kind) + "_max"), UNIT0[kind] + u + 1)
                        L = a["logit"][:, u % 2]
                        for qb, cols in ((0, slice(0, P)), (1, slice(P, 384))):
                            j = (u % 2) * 2 + qb
                            A(L[:, :, cols], L[:, :, cols], ACT.Exp, bias=stat[:, j:j + 1],
                              accum_out=stat[:, 8 + j:9 + j]).then_inc(S(att(kind) + "_exp"), 1)
                    if w is not None:
                        act.wait_ge(S(att(kind) + "_O"), HEAD0[kind] + per * (w + 1))
                        A(bhi[:, a["dst"] + w, :], bank[6 + w % 2][:, 0:256], ACT.Copy).then_inc(S(att(kind) + "_ohi"), 1)

            act.wait_ge(S("vec_cols"), 1)
            A(silu_c[:], vec[:, V_C:V_C + 16], ACT.Silu).then_inc(S("silu_c"), 1)
            stage_end(act, "act")
            act.wait_ge(S("x_landed"), 16)
            norm_stats("n1")
            stage_end(act, "act")

            def proj_evac(proj, t0):
                def ev(g, par):
                    act.wait_ge(tile_used, g * 8 + (t0 - T_ADA + 8 + 4))
                    A(proj[:, 0, bass.ds(g * COLS, COLS)], bank[2 * par][:], ACT.Copy).then_inc(evac_act, 1)
                return ev
            def proj1_split(k, g, par):
                is_product, j = PROJ1_ORDER[k]
                if is_product:
                    split_item(t_proj1 + k, g * 3, j, g * 2)

            def proj1_evac(half):
                def ev(g, par):
                    act.wait_ge(tile_used, g * 16 + (8 * half + 8 + 4))
                    A(proj1[:, 0, bass.ds(g * (2 * COLS) + half * COLS, COLS)], bank[2 * half][:], ACT.Copy)\
                        .then_inc(evac_act, 1)
                return ev

            def proj1_last(k):
                split_item(t_proj1 + 7 * 24 + k, 0, 14 * 8 + k, 0)

            def branch_split(k, g, par):
                is_product, j = BRANCH_ORDER[k]
                if is_product:
                    split_item(t_branch + k, g * 6, u_branch + j, g * 4)
            for k in range(4):
                proj1_split(k, 0, 0)
            side_hi(side1, 16, "side1_landed", 16)
            norm_chunks("n1")
            drive(act, 7, 24, proj1_split, {item(11): proj1_evac(0), 27: proj1_evac(1)},
                  proj1_last, prologue=False)
            for k in range(4, 8):
                proj1_last(k)
            for k in range(4):
                branch_split(k, 0, 0)
            act.wait_ge(tile_used, 15 * 8 + 4)
            A(proj1[:, 0, 14 * COLS:15 * COLS], bank[0][:], ACT.Copy).then_inc(evac_act, 1)
            side_turn(1, 16)
            A(gl_a16[:], bank[7][:, 0:32], ACT.Copy)
            stage_end(act, "act")

            qk_squares("sb", [(proj1, b, c, 1536) for c in (0, 2304) for b in range(TB)], SQ1)
            H = SB_HEADS
            for i in range(H + 3):
                h = i - 1
                if 0 <= h < H:
                    act.wait_ge(S("sb_z"), h + 1)
                    if h >= 2:
                        act.wait_ge(S("sb_o"), h - 1)
                        act.wait_ge(S("sb_c"), h - 1)
                    Z, L, ZS = bank[2 + h % 2][:, 0:384], l_sb[:, h % 2], z_sb[:, h % 2]
                    A(ZS, Z, ACT.Copy).then_inc(S("sb_zs"), 1)
                    chain.step(A(L, Z, ACT.Abs))
                    chain.step(A(L, L, ACT.Exp, scale=-1.0))
                    A(L, L, ACT.Ln, bias=1.0).then_inc(S("sb_ln"), 1)
                h = i - 2
                if 0 <= h < H:
                    act.wait_ge(S("sb_e"), h + 1)
                    act.wait_ge(S("sb_em"), h + 1)
                    A(z_sb[:, h % 2], z_sb[:, h % 2], ACT.Exp).then_inc(S("sb_w"), 1)
                h = i - 3
                if 0 <= h < H:
                    act.wait_ge(S("sb_o"), h + 1)
                    A(bhi[:, h, :], bank[6 + h % 2][:, 0:256], ACT.Copy).then_inc(S("sb_ohi"), 1)
            stage_end(act, "act")

            attention("dil")
            stage_end(act, "act")

            act.wait_ge(S("gl_aT"), 1)
            A(gl_at, bank[0][0:16, 0:256], ACT.Copy).then_inc(S("gl_at"), 1)
            for b in range(TB):
                act.wait_ge(S("gl_alin"), b + 1)
                chain.step(A(gl_tmp[:, b], bank[2 + b][:], ACT.Abs))
                chain.step(A(gl_tmp[:, b], gl_tmp[:, b], ACT.Exp, scale=-1.0))
                A(gl_tmp[:, b], gl_tmp[:, b], ACT.Ln, bias=1.0).then_inc(S("gl_ln"), 1)
            for b in range(TB):
                act.wait_ge(S("gl_lc"), b + 1)
                A(gl_kd[:, b], bank[2 + b][:], ACT.Exp).then_inc(S("gl_elc"), 1)
            for h in range(GLA_HEADS):
                act.wait_ge(S("gl_cum"), h + 1)
                if h >= 2:
                    act.wait_ge(S("gl_qkm"), h - 1)
                C = bank[4 + h % 2][:].rearrange("p (b e n) -> p b e n", b=TB, e=2)
                E = gl_ex[:, h % 2].rearrange("p e (b n) -> p b e n", b=TB)
                for e in range(2):
                    A(E[:, :, e], C[:, :, e], ACT.Exp)
                A(E[:, :, 2], C[:, :, 1], ACT.Exp, scale=-1.0).then_inc(S("gl_ex"), 2)
            for c in range(4):
                b, rows = c // 2, slice(64 * (c % 2), 64 * (c % 2) + 64)
                for h in range(GLA_HEADS):
                    act.wait_ge(S("gl_o"), 4 * c + h + 1)
                    A(gl_og[rows, b, h * DV:(h + 1) * DV], bank[h][rows, 0:DV], ACT.Copy).then_inc(S("gl_og"), 1)
            act.wait_ge(S("gl_og"), 16)
            for b in range(TB):
                A(gl_sq[:, b], gl_og[:, b], ACT.Square).then_inc(S("gl_sq"), 1)
            for b in range(TB):
                A(proj1[:, b, 6656:7680], proj1[:, b, 6656:7680], ACT.Silu).then_inc(S("gl_silu"), 1)
            act.wait_ge(S("gl_var"), 1)
            A(gl_ss, gl_ss, ACT.Sqrt).then_inc(S("gl_std"), 1)
            for k in range(8):
                act.wait_ge(S("gl_T"), k + 1)
                if k >= 4:
                    act.wait_ge(S("gl_lo"), k - 3)
                A(gl_htmp[:, k % 4], bank[k % 4][:, 0:256], ACT.Identity, scale=vec[:, V_GG + k % 2:V_GG + k % 2 + 1])\
                    .then_inc(S("gl_h"), 1)
            stage_end(act, "act")

            gate_broadcast("g1")

            def gate_evac(i):
                end = (8, 19, 28)[i]

                def ev(g, par):
                    act.wait_ge(tile_used, g * 32 + (u_branch + end + 4))
                    n = 2 * i
                    act.wait_ge(evac_dve, g * 6 + (n_branch + n - 2))
                    A(gsig[:, i, 0], bank[2 * (n % 3)][:], ACT.Sigmoid)
                    A(gsig[:, i, 1], bank[2 * (n % 3) + 1][:], ACT.Sigmoid).then_inc(evac_act, 1)
                return ev

            def branch_seen(i):
                end = (11, 20, 32)[i]

                def ev(g, par):
                    act.wait_ge(evac_dve, g * 6 + (n_branch + 2 * i + 4))
                    act.sem_inc(evac_act, 1)
                return ev
            ev_act = {item(11): gate_evac(0), item(14): branch_seen(0), item(22): gate_evac(1), item(23): branch_seen(1),
                      item(31): gate_evac(2), 51: branch_seen(2)}
            drive(act, 4, 48, branch_split, ev_act, lambda k: split_hi(t_out1 + k, 0), prologue=False, single=True)
            stage_end(act, "act")
            norm("y")

            def skip_evac(n0):
                def ev(g, par):
                    act.wait_ge(evac_dve, g + (n0 + 3))
                    act.sem_inc(evac_act, 1)
                return ev
            drive(act, 4, 8, gemm_split(t_out1), {11: skip_evac(n_out1)}, ffn_first, prologue=False)
            stage_end(act, "act")
            norm("n2")
            gate_broadcast("g2")

            def hidden_rounds(t0, n0, parts, rnd, prefix, q0, up0, follow):
                def up_split(k, g, par):
                    split_hi(t0 + k, rnd * 12 + g, rnd * 128 + g * 16 + (up0 + 16))

                def silu_evac(g, par):
                    act.wait_ge(tile_used, rnd * 96 + g * 8 + (t0 - T_ADA + 8 + 4))
                    for b in range(TB):
                        ins = A(silu_g[:, b], bank[2 * par + b][:, 0:HID], ACT.Silu)
                    ins.then_inc(evac_act, 1)

                def hidden_hi(g, par):
                    act.wait_ge(S(prefix + "_hidT"), rnd * 8 + g + (q0 + 1))
                    A(bhi[:, bass.ds(g * 2, 2), :], bank[4][:].rearrange("p (c n) -> p c n", c=2), ACT.Copy)\
                        .then_inc(S(prefix + "_hhi"), 1)

                def down(i):
                    split_hi(t0 + 8 * parts + i, rnd * 12)

                def seen(g):
                    act.wait_ge(evac_dve, rnd * 12 + (n0 + parts + g + 3))
                    act.sem_inc(evac_act, 1)
                drive(act, parts, 8, up_split, {10: silu_evac, 11: hidden_hi}, down, prologue=False)
                for i in range(4, 4 * parts + 4):
                    if i < 4 * parts:
                        down(i)
                    else:
                        follow(i - 4 * parts)
                    if i >= parts and (i - 3) % parts == 0:
                        seen((i - 3) // parts - 1)

            with act.Fori(0, 2) as rnd:
                hidden_rounds(t_ffn, n_ffn, 8, rnd, "ffn", 0, 0,
                              lambda k: split_hi(t_ffn + 96 + k, rnd * 12, rnd * 128 + (128 + 16)))
            hidden_rounds(t_ffn + 192, n_ffn + 24, 6, 0, "ffn", 16, 16 * 16, lambda k: split_hi(t_proj2 + k, 0))
            stage_end(act, "act")

            side_hi(side2, 8, "side2_landed", 32)
            norm("n3")
            drive(act, 10, 8, gemm_split(t_proj2), {11: proj_evac(proj2, t_proj2)}, lambda k: split_hi(t_out2 + k, 0),
                  prologue=False)
            side_turn(2, 8)
            fl = stat[:, 32:48]
            chain.step(A(stat[:, 48:64], bank[7][:, 0:16], ACT.Copy))
            chain.step(A(fl, bank[7][:, 0:16], ACT.Abs))
            chain.step(A(fl, fl, ACT.Exp, scale=-1.0))
            A(fl, fl, ACT.Ln, bias=1.0).then_inc(S("fox_ln"), 1)
            stage_end(act, "act")

            act.wait_ge(S("fox_c"), 1)
            for q in range(4):
                A(big[0:1, F_CROW + q * 512:F_CROW + (q + 1) * 512], bank[q][0:1, :], ACT.Copy).then_inc(S("fox_crow"), 1)
            qk_squares("fox", [(proj2, b, c, 1024) for c in (0, 1024) for b in range(TB)], SQ2F)
            attention("fox")
            stage_end(act, "act")

            chain.step(A(stat[:, 16:24], vec[:, V_LAM:V_LAM + 8], ACT.Abs))
            A(stat[:, 16:24], stat[:, 16:24], ACT.Exp, scale=-1.0).then_inc(S("rnn_elam"), 1)
            def rnn_copy(n):
                act.wait_ge(S("rnn_T"), n + 1)
                dst = r_xp[:, n, 3:259] if n < RNN_CHUNKS else r_rg[:, n - RNN_CHUNKS]
                A(dst, bank[n % 4][:, 0:256], ACT.Copy).then_inc(S("rnn_copied"), 1)

            for n in range(2 * RNN_CHUNKS):
                rnn_copy(n)
            for k in range(RNN_CHUNKS):
                act.wait_ge(S("rnn_lin"), k + 1)
                A(r_r[:, k], bank[4 + k % 4][:, 0:256], ACT.Sigmoid, bias=vec[:, V_BR + k:V_BR + k + 1])\
                    .then_inc(S("rnn_sig"), 1)
                A(r_i[:, k], bank[4 + k % 4][:, 256:512], ACT.Sigmoid, bias=vec[:, V_BI + k:V_BI + k + 1])\
                    .then_inc(S("rnn_sig"), 1)
            act.wait_ge(S("rnn_k8"), 1)
            act.wait_ge(S("rnn_sig"), 16)
            for k in range(RNN_CHUNKS):
                A(r_m[k // 4][:, k % 4], r_r[:, k], ACT.Tanh, scale=r_k8[:, k:k + 1]).then_inc(S("rnn_tanh"), 1)
            act.wait_ge(S("rnn_g3"), 1)
            A(r_g, r_g, ACT.Tanh, scale=0.7978845608028654).then_inc(S("rnn_gt"), 1)
            act.wait_ge(S("rnn_xc"), 8)
            for k in range(RNN_CHUNKS):
                A(r_a[:, k], r_r[:, k], ACT.Exp, scale=r_nk8[:, k:k + 1]).then_inc(S("rnn_a"), 1)
            for i, H in enumerate(RNN_HALVES):
                act.wait_ge(S("rnn_m"), i + 1)
                A(r_m[i], r_m[i], ACT.Sqrt).then_inc(S("rnn_sqrt"), 1)
            for i, H in enumerate(RNN_HALVES):
                act.wait_ge(S("rnn_out"), i + 1)
                A(bhi[:, 8 + 4 * i:12 + 4 * i, :], r_g[:, H], ACT.Copy).then_inc(S("rnn_hi"), 1)

            drive(act, 4, 8, gemm_split(t_out2), {11: skip_evac(n_out2)}, moe_first, prologue=False)
            stage_end(act, "act")
            side_hi(route, 36, "route_landed", 32)
            norm("n4")

            side_turn(3, 36)
            act.wait_ge(S("rt_sub"), 1)
            A(rt[:, 0:8], rt[:, 0:8], ACT.Exp).then_inc(S("rt_exp"), 1)
            act.wait_ge(S("rt_dif"), 1)
            A(rt[:, 40:42], rt[:, 40:42], ACT.Exp).then_inc(S("rt_exp"), 1)
            with act.Fori(0, 3) as rnd:
                hidden_rounds(t_moe, n_moe, 8, rnd, "moe", 0, 16 * FFN_PARTS,
                              lambda k: split_hi(t_moe + 96 + k, rnd * 12, rnd * 128 + (16 * FFN_PARTS + 128 + 16)))
            hidden_rounds(t_moe + 288, n_moe + 36, 8, 0, "moe", 24, 16 * (FFN_PARTS + 24), lambda k: split_hi(t_ple + k, 0))
            stage_end(act, "act")

            norm("n5")
            act.wait_ge(S("p_T"), 1)
            A(bhi[:, 0:2, :], bank[3][:].rearrange("p (c n) -> p c n", c=2), ACT.Copy).then_inc(S("p_hi"), 1)
            for i in range(4, 4 * 9 + 4):
                if i < 36:
                    split_hi(t_ple + i, 0)
                if i >= 10 and (i - 10) % 9 == 0 and (i - 10) // 9 < 4:
                    g = (i - 10) // 9
                    act.wait_ge(tile_used, t_ple - T_ADA + 9 * g + 8 + 4)
                    if g >= 1:
                        act.wait_ge(evac_dve, 2 + n_ple + 2 * g)
                    A(gsig[:, 0, 0], bank[0][:], ACT.Sigmoid)
                    A(gsig[:, 0, 1], bank[1][:], ACT.Sigmoid).then_inc(evac_act, 1)
                if i >= 12 and (i - 12) % 9 == 0 and (i - 12) // 9 < 4:
                    g = (i - 12) // 9
                    act.wait_ge(evac_dve, 2 + n_ple + 2 * g + 2)
                    act.sem_inc(evac_act, 1)

        @block.vector
        def _(dve):
            V = nc.vector
            chain = Chain(dve, "dve_chain")
            step = chain.step

            def split_lo(t, r):
                dve.wait_ge(hi_ready, r * 8 + (t - T_ADA + 1))
                V.tensor_tensor(wlo[:, t % 4], raw[:, t % 8], whi[:, t % 4].bitcast(F32), ALU.subtract)\
                    .then_inc(lo_ready, 1)

            def gemm_split(t0):
                return lambda k, g, par: split_lo(t0 + k, g)

            def ffn_first(k):
                split_lo(t_ffn + k, 0)

            def moe_first(k):
                split_lo(t_moe + k, 0)

            def side_lo(src, n, no):
                dve.wait_ge(S("side_hi"), no)
                shi, slo = side_parts(n)
                V.tensor_tensor(slo, src, shi.bitcast(F32), ALU.subtract).then_inc(S("side_lo"), 1)

            def norm_rows(key):
                cfg = NORMS[key]
                dve.wait_ge(S("norm_ss"), 2 * cfg["stats"] + 2)
                V.tensor_scalar(stat[:, 2:4], stat[:, 0:2], 1.0 / D, EPS, ALU.mult, ALU.add).then_inc(S("norm_var"), 1)
                dve.wait_ge(S("norm_std"), cfg["stats"] + 1)
                step(V.reciprocal(stat[:, 6:8], stat[:, 4:6]))
                for b in range(TB):
                    V.tensor_scalar(xn[:, b], cfg["src"][:, b], stat[:, 6 + b:7 + b], None, ALU.mult)\
                        .then_inc(S("norm_xn"), 1)

            def norm_split(key):
                cfg = NORMS[key]
                for k in range(0, DC, 2):
                    h = htmp[:, k % 4:k % 4 + 2]
                    dve.wait_ge(S("norm_h"), 16 * cfg["no"] + k + 2)
                    step(V.tensor_copy(ahi[:, k:k + 2], h))
                    V.tensor_tensor(alo[:, k:k + 2], h, ahi[:, k:k + 2].bitcast(F32), ALU.subtract)\
                        .then_inc(S("norm_lo"), 1)

            def norm(key):
                if NORMS[key]["norm"]:
                    norm_rows(key)
                norm_split(key)

            def gate_diag(key, cols):
                for k in range(DC):
                    V.tensor_scalar(gate_dg[:, k * P:(k + 1) * P], ident[:], cols[:, k:k + 1], None, ALU.mult)\
                        .then_inc(S("gate_gd"), 1)

            def qk_norm(kind, groups, sq, gq):
                at = 0
                for n, (src, b, col, w) in enumerate(groups):
                    dve.wait_ge(S("qk_sq"), 4 * NORM_NO[kind] + n + 1)
                    k = w // DH
                    V.reduce_sum(stat[:, at:at + k], sq[:, n % 2, 0:w].rearrange("p (h n) -> p h n", n=DH), AX.X)\
                        .then_inc(S("qk_sqsum"), 1)
                    at += k
                dve.wait_ge(S("qk_sqsum"), 4 * NORM_NO[kind] + 4)
                if at < 48:
                    step(V.memset(stat[:, at:48], 1.0))
                V.tensor_scalar(stat[:, 0:48], stat[:, 0:48], 1.0 / DH, EPS, ALU.mult, ALU.add)\
                    .then_inc(S("qk_var"), 1)
                dve.wait_ge(S("qk_std"), NORM_NO[kind] + 1)
                step(V.reciprocal(stat[:, 0:48], stat[:, 0:48]))
                at = 0
                for n, (src, b, col, w) in enumerate(groups):
                    k = w // DH
                    v = src[:, b, col:col + w].rearrange("p (h n) -> p h n", n=DH)
                    ins = V.tensor_tensor(v, v, stat[:, at:at + k].rearrange("p (h a) -> p h a", a=1)
                                          .to_broadcast([P, k, DH]), ALU.mult)
                    step(ins)
                    at += k
                step(V.tensor_scalar(vec[:, gq:gq + 1], vec[:, gq:gq + 1], QSCALE, None, ALU.mult))
                if kind == "sb":
                    step(V.tensor_scalar(vec[:, V_DQ:V_DQ + 1], vec[:, V_DQ:V_DQ + 1], QSCALE, None, ALU.mult))

            def qkt_evac(kind, n, qkt, gq, gk):
                dve.wait_ge(S(att(kind) + "_T"), HEAD0[kind] + n + 1)
                if n >= 2:
                    dve.wait_ge(S("sb_z") if kind == "sb" else S("att_S"), HEAD0[kind] + n - 1)
                for i, g in enumerate((gq, gk)):
                    V.tensor_scalar(qkt[:, n % 2, i], bank[n % 2][:, i * 256:(i + 1) * 256], vec[:, g:g + 1], None,
                                    ALU.mult).then_inc(S(att(kind) + "_qkt"), 1)

            def out_lo(kind, n, chunk, O):
                dve.wait_ge(S(att(kind) + "_ohi"), UNIT0[kind] + n + 1)
                V.tensor_tensor(blo[:, chunk, :], O, bhi[:, chunk, :].bitcast(F32), ALU.subtract)\
                    .then_inc(S(att(kind) + "_out"), 1)

            def attention(kind, gq, gk):
                a = ATT[kind]
                U, per = a["units"], a["per"]
                qkt_evac(kind, 0, a["qkt"], gq, gk)
                for n in range(U * per + 3):
                    if n + 1 < U * per:
                        qkt_evac(kind, n + 1, a["qkt"], gq, gk)
                    if n < U * per:
                        u, i = divmod(n, per)
                        L, Z = a["logit"][:, u % 2], bank[2 + n % 2]
                        dve.wait_ge(S(att(kind) + "_S"), HEAD0[kind] + n + 1)
                        if u >= 2 and i == 0:
                            dve.wait_ge(S(att(kind) + "_PT"), HEAD0[kind] + (u - 1) * per)
                        if kind == "dil":
                            V.tensor_tensor(L[:, i], Z[:, 0:384], dil_mask[u][:, i], ALU.add).then_inc(S("att_log"), 1)
                        else:
                            caus = region(big, F_CAUS, P)
                            step(V.tensor_copy(L[:, i, P:256], Z[:, P:256]))
                            step(V.tensor_tensor(L[:, i, 0:P], Z[:, 0:P], caus, ALU.add))
                            V.tensor_tensor(L[:, i, 256:384], Z[:, 256:384], caus, ALU.add)\
                                .then_inc(S("att_log"), 1)
                    u = finished_unit(n, per, -1)
                    if u is not None and u < U:
                        L, j = a["logit"][:, u % 2], (u % 2) * 2
                        dve.wait_ge(S(att(kind) + "_log"), HEAD0[kind] + (u + 1) * per)
                        V.tensor_reduce(stat[:, 4:5], L[:, :, 0:P], AX.XY, ALU.max).then_inc(S(att(kind) + "_mx"), 1)
                        V.tensor_reduce(stat[:, 5:6], L[:, :, P:384], AX.XY, ALU.max).then_inc(S(att(kind) + "_mx"), 1)
                        dve.wait_ge(S(att(kind) + "_mx"), 2 * UNIT0[kind] + 2 * u + 2)
                        V.tensor_scalar(stat[:, j:j + 2], stat[:, 4:6], -1.0, None, ALU.mult).then_inc(S(att(kind) + "_max"), 1)
                    u = finished_unit(n, per, 0)
                    if u is not None and u < U:
                        L, j = a["logit"][:, u % 2], (u % 2) * 2
                        dve.wait_ge(S(att(kind) + "_exp"), 2 * UNIT0[kind] + 2 * (u + 1))
                        step(V.reciprocal(stat[:, 12 + j:14 + j], stat[:, 8 + j:10 + j]))
                        step(V.tensor_scalar(L[:, :, 0:P], L[:, :, 0:P], stat[:, 12 + j:13 + j], None, ALU.mult))
                        V.tensor_scalar(L[:, :, P:384], L[:, :, P:384], stat[:, 13 + j:14 + j], None, ALU.mult)\
                            .then_inc(S(att(kind) + "_P"), 1)
                    w = finished_unit(n, per, 2)
                    if w is not None:
                        out_lo(kind, w, a["dst"] + w, bank[6 + w % 2][:, 0:256])

            V.memset(ones[:], 1.0).then_inc(S("ones_set"), 1)
            V.memset(stat[:], 0.0).then_inc(S("ones_set"), 1)
            V.memset(silu_c[:], 0.0).then_inc(S("ones_set"), 1)
            V.memset(geff[:], 0.0).then_inc(S("ones_set"), 1)
            dve.wait_ge(S("ones_set"), 4)
            V.memset(seed[:, 0:1], 0.0).then_inc(tile_used, 4)
            V.memset(seed[:, 1:2], 0.0).then_inc(evac_act, 2)
            V.memset(seed[:, 2:3], 0.0).then_inc(evac_dve, 2)
            V.memset(seed[:, 3:4], 0.0).then_inc(S("mod_done"), 2)
            dve.wait_ge(S("vec_T"), 1)
            V.tensor_copy(vec[:], bank[0][:, 0:V_ALL]).then_inc(S("vec_cols"), 1)
            dve.wait_ge(S("silu_c"), 1)
            stage_end(dve, "dve")

            norm_rows("n1")
            def ada_rows(t, r, n, k, sums):
                dve.wait_ge(landed[t % 8], r * 16 + 16 * (t // 8 + 1))
                w = raw[:, t % 8]
                for c in range(2):
                    col = silu_c[:, 2 * k + c:2 * k + c + 1]
                    if k == 0 and c == 0:
                        V.tensor_scalar(sums, w[:, 0], col, None, ALU.mult).then_inc(S("ada_step"), 1)
                    elif c == 0:
                        dve.wait_ge(lo_ready, r * 8 + t)
                        V.scalar_tensor_tensor(sums, w[:, 0], col, sums, ALU.mult, ALU.add)\
                            .then_inc(S("ada_step"), 1)
                    else:
                        dve.wait_ge(S("ada_step"), n * 8 + (k + 1))
                        V.scalar_tensor_tensor(sums, w[:, 1], col, sums, ALU.mult, ALU.add).then_inc(lo_ready, 1)

            def ada_store(n, src):
                dve.wait_ge(S("ada_cols"), n + 1)
                cols = bass.ds(n * 4, 4)
                V.tensor_tensor(modt[:, cols], src[:, 0:4], vec[:, cols], ALU.add).then_inc(S("mod_done"), 1)
            drive(dve, ADA_FIRST, 8, lambda k, g, par: ada_rows(k, g, g, k, acc[:, par]),
                  {11: lambda g, par: ada_store(g, bank[par])})
            dve.wait_ge(S("mod_done"), 2 + ADA_FIRST)
            stage_end(dve, "dve")

            def gain_eff(key, scale, gain):
                V.scalar_tensor_tensor(geff[:], modt[:, scale:scale + 16], 1.0, vec[:, gain:gain + 16], ALU.add, ALU.mult)\
                    .then_inc(S("gate_geff"), 1)
            gain_eff("n1", 16, V_N1)

            def proj_evac(proj, t0):
                def ev(g, par):
                    dve.wait_ge(tile_used, g * 8 + (t0 - T_ADA + 8 + 4))
                    V.tensor_copy(proj[:, 1, bass.ds(g * COLS, COLS)], bank[2 * par + 1][:]).then_inc(evac_dve, 1)
                return ev
            def split_item(t, r, u, ru):
                dve.wait_ge(hi_ready, ru * 8 + (u + 1))
                V.tensor_tensor(wlo[:, u % 4], raw[:, t % 8], whi[:, u % 4].bitcast(F32), ALU.subtract)\
                    .then_inc(lo_ready, 1)

            def proj1_split(k, g, par):
                is_product, j = PROJ1_ORDER[k]
                if is_product:
                    split_item(t_proj1 + k, g * 3, j, g * 2)
                else:
                    ada_rows(t_proj1 + k, g * 3, g + ADA_FIRST, j, acc2[:, par])

            def proj1_evac(half):
                def ev(g, par):
                    dve.wait_ge(tile_used, g * 16 + (8 * half + 8 + 4))
                    V.tensor_copy(proj1[:, 1, bass.ds(g * (2 * COLS) + half * COLS, COLS)], bank[2 * half + 1][:])\
                        .then_inc(evac_dve, 1)
                return ev

            def proj1_last(k):
                split_item(t_proj1 + 7 * 24 + k, 0, 14 * 8 + k, 0)

            def branch_split(k, g, par):
                is_product, j = BRANCH_ORDER[k]
                if is_product:
                    split_item(t_branch + k, g * 6, u_branch + j, g * 4)
                else:
                    ada_rows(t_branch + k, g * 6, g * 2 + (ADA_FIRST + 7 + j // 8), j % 8, acc2[:, j // 8])
            for k in range(4):
                proj1_split(k, 0, 0)
            side_lo(side1, 16, 1)
            norm_split("n1")
            drive(dve, 7, 24, proj1_split, {item(11): proj1_evac(0),
                                            27: lambda g, par: (proj1_evac(1)(g, par),
                                                                ada_store(g + ADA_FIRST, bank[6 + par]))},
                  proj1_last, prologue=False)
            for k in range(4, 8):
                proj1_last(k)
            for k in range(4):
                branch_split(k, 0, 0)
            dve.wait_ge(tile_used, 15 * 8 + 4)
            V.tensor_copy(proj1[:, 1, 14 * COLS:15 * COLS], bank[1][:]).then_inc(evac_dve, 1)
            stage_end(dve, "dve")

            grp = [(proj1, b, c, 1536) for c in (0, 2304) for b in range(TB)]
            dve.wait_ge(S("sbc_landed"), 16)
            step(V.memset(negones, -1.0))
            step(V.tensor_scalar(negtri, u_tri, -1.0, None, ALU.mult))
            qk_norm("sb", grp, SQ1, V_SBQ)
            dve.sem_inc(S("sb_scaled"), 1)
            H = SB_HEADS
            for i in range(H + 4):
                if i < H:
                    qkt_evac("sb", i, qkt_sb, V_SBQ, V_SBK)
                h = i - 1
                if 0 <= h < H:
                    L, Z = l_sb[:, h % 2], bank[2 + h % 2][:, 0:384]
                    dve.wait_ge(S("sb_ln"), h + 1)
                    V.scalar_tensor_tensor(L, Z, 0.0, L, ALU.max, ALU.add).then_inc(S("sb_sp"), 1)
                    dve.wait_ge(S("sb_sp"), h + 1)
                    step(V.tensor_tensor(L[:, 0:P], L[:, 0:P], strict, ALU.mult))
                    V.tensor_tensor(L[:, 256:384], L[:, 256:384], strict, ALU.mult).then_inc(S("sb_spm"), 1)
                h = i - 2
                if 0 <= h < H:
                    ZS = z_sb[:, h % 2]
                    dve.wait_ge(S("sb_c"), h + 1)
                    dve.wait_ge(S("sb_zs"), h + 1)
                    V.tensor_tensor(ZS, ZS, bank[4 + h % 2][:, 0:384], ALU.add).then_inc(S("sb_e"), 1)
                    dve.wait_ge(S("sb_e"), h + 1)
                    step(V.tensor_tensor(ZS[:, 0:P], ZS[:, 0:P], strictneg, ALU.add))
                    V.tensor_tensor(ZS[:, 256:384], ZS[:, 256:384], strictneg, ALU.add).then_inc(S("sb_em"), 1)
                h = i - 3
                if 0 <= h < H:
                    out_lo("sb", h, h, bank[6 + h % 2][:, 0:256])
            stage_end(dve, "dve")

            dve.wait_ge(S("dmask_landed"), 32)
            attention("dil", V_DQ, V_DK)
            stage_end(dve, "dve")

            for b in range(TB):
                dve.wait_ge(S("gl_ln"), b + 1)
                V.scalar_tensor_tensor(gl_ls[:, b], bank[2 + b][:], 0.0, gl_tmp[:, b], ALU.min, ALU.subtract)\
                    .then_inc(S("gl_ls"), 1)
            for b in range(TB):
                dve.wait_ge(S("gl_elc"), b + 1)
                V.tensor_tensor(gl_kd[:, b], gl_kd[:, b], proj1[:, b, 5120:5632], ALU.mult).then_inc(S("gl_kd"), 1)
            for h in range(GLA_HEADS):
                dve.wait_ge(S("gl_ex"), 2 * (h + 1))
                T, E = bank[h % 2], gl_ex[:, h % 2]
                V.scalar_tensor_tensor(gl_qc[:, h], T[:, 0:256], QSCALE, E[:, 0], ALU.mult, ALU.mult)
                V.scalar_tensor_tensor(gl_qm[:, h], T[:, 0:256], QSCALE, E[:, 1], ALU.mult, ALU.mult)
                V.tensor_copy(gl_el[:, h], E[:, 0, 63:256:64])
                V.tensor_tensor(gl_km[:, h], T[:, 256:512], E[:, 2], ALU.mult).then_inc(S("gl_qkm"), 1)
            dve.wait_ge(S("gl_sT"), 1)
            mask = region(xf, G_MASK, 64)
            V.tensor_tensor(gl_sc, bank[6][:].rearrange("p (s n) -> p s n", s=8),
                            mask.rearrange("p (a n) -> p a n", a=1).to_broadcast([P, 8, 64]), ALU.mult)\
                .then_inc(S("gl_sc"), 1)
            dve.wait_ge(S("gl_sc"), 1)
            for c in range(3):
                for h in range(GLA_HEADS):
                    dve.wait_ge(S("gl_o"), 4 * c + h + 1)
                    U = bank[4 + h][:, 0:DV]
                    if c == 0:
                        ins = V.tensor_copy(gl_st[:, 0, h], U)
                    else:
                        ins = V.scalar_tensor_tensor(gl_st[:, c % 2, h], gl_st[:, (c - 1) % 2, h], gl_el[:, h, c:c + 1],
                                                     U, ALU.mult, ALU.add)
                    ins.then_inc(S("gl_state"), 1)
                if c < 2:
                    dve.wait_ge(S("gl_state"), 4 * c + 4)
            for b in range(TB):
                dve.wait_ge(S("gl_sq"), b + 1)
                step(V.reduce_sum(gl_ss[:, 4 * b:4 * b + 4], gl_sq[:, b].rearrange("p (h n) -> p h n", n=DV), AX.X))
            V.tensor_scalar(gl_ss, gl_ss, 1.0 / DV, EPS, ALU.mult, ALU.add).then_inc(S("gl_var"), 1)
            dve.wait_ge(S("gl_std"), 1)
            step(V.reciprocal(gl_ss, gl_ss))
            for b in range(TB):
                dve.wait_ge(S("gl_silu"), b + 1)
                for h in range(GLA_HEADS):
                    o = gl_og[:, b, h * DV:(h + 1) * DV]
                    col = 6656 + h * DV
                    ins = V.scalar_tensor_tensor(o, o, gl_ss[:, 4 * b + h:4 * b + h + 1], proj1[:, b, col:col + DV],
                                                 ALU.mult, ALU.mult)
                    if b == 1 and h == 3:
                        ins.then_inc(S("gl_fin"), 1)
            for k in range(8):
                dve.wait_ge(S("gl_h"), k + 1)
                step(V.tensor_copy(bhi[:, 8 + k], gl_htmp[:, k % 4]))
                V.tensor_tensor(blo[:, 8 + k], gl_htmp[:, k % 4], bhi[:, 8 + k].bitcast(F32), ALU.subtract)\
                    .then_inc(S("gl_lo"), 1)
            stage_end(dve, "dve")

            gate_diag("g1", modt[:, 32:48])

            def gate_seen(i):
                def ev(g, par):
                    dve.wait_ge(evac_act, g * 6 + (n_branch + 2 * i + 3))
                    dve.sem_inc(evac_dve, 1)
                return ev

            def branch_evac(i):
                end = (11, 20, 32)[i]

                def ev(g, par):
                    dve.wait_ge(tile_used, g * 32 + (u_branch + end + 4))
                    n = 2 * i + 1
                    dst = ysum[:, :, bass.ds(g * COLS, COLS)]
                    for b in range(TB):
                        Bk = bank[2 * (n % 3) + b][:]
                        o = ysum[:, b, bass.ds(g * COLS, COLS)]
                        if i == 0:
                            ins = V.tensor_tensor(o, gsig[:, i, b], Bk, ALU.mult)
                            ins.then_inc(S("y_step") if b == 0 else evac_dve, 1)
                        else:
                            V.tensor_tensor(ymul[:, b], gsig[:, i, b], Bk, ALU.mult)\
                                .then_inc(S("y_step") if b == 0 else evac_dve, 1)
                    if i > 0:
                        dve.wait_ge(evac_dve, g * 6 + (n_branch + n + 3))
                        for b in range(TB):
                            o = ysum[:, b, bass.ds(g * COLS, COLS)]
                            V.tensor_tensor(o, o, ymul[:, b], ALU.add).then_inc(S("y_step"), 1)
                return ev
            ev_dve = {item(11): gate_seen(0), item(14): branch_evac(0), item(22): gate_seen(1), item(23): branch_evac(1),
                      item(31): gate_seen(2), 51: branch_evac(2)}
            for half in range(2):
                at = (32, 51)[half]
                store = (lambda half: lambda g, par: ada_store(g * 2 + (ADA_FIRST + 7 + half), bank[6 + half]))(half)
                ev_dve[at] = (lambda a, b: lambda g, par: (a(g, par), b(g, par)))(ev_dve[at], store) if at in ev_dve \
                    else store
            drive(dve, 4, 48, branch_split, ev_dve, lambda k: split_lo(t_out1 + k, 0), prologue=False, single=True)
            stage_end(dve, "dve")
            norm("y")

            def residual_add(banks, cols, gate, n_after):
                for b in range(TB):
                    if gate is not None:
                        V.tensor_tensor(prod[:, b], gate_bc[gate][:, cols], bank[banks[b]][:], ALU.mult)\
                            .then_inc(S("prod_step") if b == 0 else evac_dve, 1)
                    else:
                        o = xres[:, b, cols]
                        V.tensor_tensor(o, o, bank[banks[b]][:], ALU.add)\
                            .then_inc(S("prod_step") if b == 0 else evac_dve, 1)
                if gate is not None:
                    dve.wait_ge(evac_dve, n_after)
                    for b in range(TB):
                        o = xres[:, b, cols]
                        V.tensor_tensor(o, o, prod[:, b], ALU.add).then_inc(S("prod_step"), 1)

            def out_evac(t0, n0, gate):
                def ev(g, par):
                    dve.wait_ge(tile_used, g * 8 + (t0 - T_ADA + 8 + 4))
                    residual_add((2 * par, 2 * par + 1), bass.ds(g * COLS, COLS), gate, g + (n0 + 3))
                return ev
            dve.wait_ge(S("x_back"), 16)
            drive(dve, 4, 8, gemm_split(t_out1), {11: out_evac(t_out1, n_out1, "g1")}, ffn_first, prologue=False)
            stage_end(dve, "dve")
            gain_eff("n2", 64, V_N2)
            norm("n2")
            gate_diag("g2", modt[:, 80:96])

            def hidden_rounds(t0, n0, parts, rnd, prefix, q0, gate, follow):
                def up_split(k, g, par):
                    split_lo(t0 + k, rnd * 12 + g)

                def hid_evac(g, par):
                    dve.wait_ge(evac_act, rnd * 12 + g + (n0 + 3))
                    for b in range(TB):
                        Up = bank[2 * par + b][:, HID:2 * HID]
                        if prefix == "moe":
                            w = comb[:, b, bass.ds(rnd * 8 + g + q0, 1)]
                            ins = V.scalar_tensor_tensor(hid[:, b], Up, w, silu_g[:, b], ALU.mult, ALU.mult)
                        else:
                            ins = V.tensor_tensor(hid[:, b], Up, silu_g[:, b], ALU.mult)
                    ins.then_inc(evac_dve, 1)

                def hidden_lo(g, par):
                    dve.wait_ge(S(prefix + "_hhi"), rnd * 8 + g + (q0 + 1))
                    V.tensor_tensor(blo[:, bass.ds(g * 2, 2), :], bank[4][:].rearrange("p (c n) -> p c n", c=2),
                                    bhi[:, bass.ds(g * 2, 2), :].bitcast(F32), ALU.subtract)\
                        .then_inc(S(prefix + "_hsplit"), 1)

                def down(i):
                    split_lo(t0 + 8 * parts + i, rnd * 12)

                def down_evac(g):
                    dve.wait_ge(tile_used, rnd * 96 + (t0 - T_ADA + 8 * parts + parts * (g + 1) + 4))
                    residual_add((2 * (g % 2), 2 * (g % 2) + 1), slice(g * COLS, (g + 1) * COLS), gate,
                                 rnd * 12 + (n0 + parts + g + 3))
                drive(dve, parts, 8, up_split, {10: hid_evac, 11: hidden_lo}, down, prologue=False)
                for i in range(4, 4 * parts + 4):
                    if i < 4 * parts:
                        down(i)
                    else:
                        follow(i - 4 * parts)
                    if i >= parts and (i - 3) % parts == 0:
                        down_evac((i - 3) // parts - 1)

            with dve.Fori(0, 2) as rnd:
                hidden_rounds(t_ffn, n_ffn, 8, rnd, "ffn", 0, "g2", lambda k: split_lo(t_ffn + 96 + k, rnd * 12))
            hidden_rounds(t_ffn + 192, n_ffn + 24, 6, 0, "ffn", 16, "g2", lambda k: split_lo(t_proj2 + k, 0))
            stage_end(dve, "dve")

            side_lo(side2, 8, 2)
            norm("n3")
            drive(dve, 10, 8, gemm_split(t_proj2), {11: proj_evac(proj2, t_proj2)}, lambda k: split_lo(t_out2 + k, 0),
                  prologue=False)
            dve.wait_ge(S("fox_ln"), 1)
            step(V.scalar_tensor_tensor(stat[:, 48:64], stat[:, 48:64], 0.0, stat[:, 32:48], ALU.min, ALU.subtract))
            stage_end(dve, "dve")

            dve.wait_ge(S("foxc_landed"), 16)
            step(V.memset(big[0:1, F_NEGROW:F_NEGROW + P], -1.0))
            grp = [(proj2, b, c, 1024) for c in (0, 1024) for b in range(TB)]
            qk_norm("fox", grp, SQ2F, V_FQ)
            dve.sem_inc(S("fox_scaled"), 1)
            attention("fox", V_FQ, V_FK)
            stage_end(dve, "dve")

            step(V.memset(r_xp[:, :, 0:3], 0.0))
            for k in range(RNN_CHUNKS):
                dve.wait_ge(S("rnn_copied"), k + 1)
                w = lambda i: vec[:, V_CW + 8 * i + k:V_CW + 8 * i + k + 1]
                step(V.tensor_scalar(r_xc[:, k], r_xp[:, k, 0:256], w(0), vec[:, V_CB + k:V_CB + k + 1], ALU.mult, ALU.add))
                for i in range(1, CONV_W):
                    ins = V.scalar_tensor_tensor(r_xc[:, k], r_xp[:, k, i:i + 256], w(i), r_xc[:, k], ALU.mult, ALU.add)
                    if i < CONV_W - 1:
                        step(ins)
                    else:
                        ins.then_inc(S("rnn_xc"), 1)
            lam = vec[:, V_LAM:V_LAM + 8]
            e1, s1, s2, q1 = (stat[:, 16 + 8 * i:24 + 8 * i] for i in range(4))
            dve.wait_ge(S("rnn_elam"), 1)
            step(V.tensor_scalar(s1, e1, 2.0, None, ALU.add))
            step(V.reciprocal(s1, s1))
            step(V.tensor_tensor(s1, s1, e1, ALU.mult))
            step(V.tensor_tensor(s2, s1, s1, ALU.mult))
            step(V.tensor_scalar(q1, s2, 1.0 / 17, 1.0 / 15, ALU.mult, ALU.add))
            for d in (13, 11, 9, 7, 5, 3, 1):
                step(V.tensor_tensor(q1, q1, s2, ALU.mult))
                step(V.tensor_scalar(q1, q1, 1.0 / d, None, ALU.add))
            step(V.tensor_tensor(q1, q1, s1, ALU.mult))
            step(V.tensor_scalar(s2, lam, -1.0, 0.0, ALU.mult, ALU.max))
            step(V.scalar_tensor_tensor(s2, q1, 2.0, s2, ALU.mult, ALU.add))
            step(V.tensor_scalar(r_k8, s2, 8.0, None, ALU.mult))
            step(V.tensor_scalar(r_nk8, s2, -8.0, None, ALU.mult))
            dve.sem_inc(S("rnn_k8"), 1)
            dve.wait_ge(S("rnn_copied"), 16)
            dve.wait_ge(S("rnn_lin"), 8)
            step(V.scalar_tensor_tensor(r_g, r_rg, 0.044715, r_rg, ALU.mult, ALU.mult))
            V.scalar_tensor_tensor(r_g, r_g, 1.0, r_rg, ALU.add, ALU.mult).then_inc(S("rnn_g3"), 1)
            for i, H in enumerate(RNN_HALVES):
                dve.wait_ge(S("rnn_sig"), 8 * (i + 1))
                step(V.tensor_tensor(r_i[:, H], r_i[:, H], r_xc[:, H], ALU.mult))
            for i, H in enumerate(RNN_HALVES):
                dve.wait_ge(S("rnn_tanh"), 4 * (i + 1))
                step(V.tensor_scalar(r_xc[:, H], r_m[i], 1.0, None, ALU.add))
                step(V.reciprocal(r_xc[:, H], r_xc[:, H]))
                V.scalar_tensor_tensor(r_m[i], r_m[i], 2.0, r_xc[:, H], ALU.mult, ALU.mult).then_inc(S("rnn_m"), 1)
            dve.wait_ge(S("rnn_gt"), 1)
            step(V.scalar_tensor_tensor(r_g, r_g, 1.0, r_rg, ALU.add, ALU.mult))
            dve.wait_ge(S("rnn_a"), 8)
            for i, H in enumerate(RNN_HALVES):
                dve.wait_ge(S("rnn_sqrt"), i + 1)
                step(V.tensor_tensor(r_i[:, H], r_i[:, H], r_m[i], ALU.mult))
                for k in range(4 * i, 4 * i + 4):
                    ins = V.tensor_tensor_scan(r_xc[:, k], r_a[:, k], r_i[:, k], 0.0, ALU.mult, ALU.add)
                step(ins)
                V.scalar_tensor_tensor(r_g[:, H], r_g[:, H], 0.5, r_xc[:, H], ALU.mult, ALU.mult).then_inc(S("rnn_out"), 1)
            for i, H in enumerate(RNN_HALVES):
                dve.wait_ge(S("rnn_hi"), i + 1)
                at = slice(8 + 4 * i, 12 + 4 * i)
                V.tensor_tensor(blo[:, at, :], r_g[:, H], bhi[:, at, :].bitcast(F32), ALU.subtract)\
                    .then_inc(S("rnn_lo"), 1)

            drive(dve, 4, 8, gemm_split(t_out2), {11: out_evac(t_out2, n_out2, None)}, moe_first, prologue=False)
            stage_end(dve, "dve")
            side_lo(route, 36, 3)
            norm("n4")

            dve.wait_ge(S("side_done"), 3)
            lg = rt[:, 64:136].rearrange("p (b n) -> p b n", b=TB)
            step(V.tensor_copy(lg, bank[7][:, 0:72].rearrange("p (b n) -> p b n", b=TB)))
            gmax, gone = rt[:, 8:10], rt[:, 16:24].rearrange("p (b n) -> p b n", b=TB)
            ex = rt[:, 0:8].rearrange("p (b n) -> p b n", b=TB)

            def wide(v, n):
                return v.rearrange("p (b a) -> p b a", a=1).to_broadcast([P, TB, n])
            step(V.tensor_reduce(gmax, lg[:, :, 0:4], AX.X, ALU.max))
            step(V.tensor_tensor(gone, lg[:, :, 0:4], wide(gmax, 4), ALU.is_equal))
            V.tensor_tensor(ex, lg[:, :, 0:4], wide(gmax, 4), ALU.subtract).then_inc(S("rt_sub"), 1)
            step(V.tensor_scalar(gone, gone, 1.0, -BIG_NEG, ALU.subtract, ALU.mult))
            el = rt[:, 160:224].rearrange("p (b g n) -> p b g n", b=TB, g=4)
            el2 = rt[:, 160:224].rearrange("p (b n) -> p b n", b=TB)
            for b in range(TB):
                step(V.tensor_tensor(el[:, b], lg[:, b, 4:36].rearrange("p (g n) -> p g n", g=4),
                                     gone[:, b].rearrange("p (g a) -> p g a", a=1).to_broadcast([P, 4, 8]), ALU.add))
            m1, m2 = rt[:, 24:26], rt[:, 26:28]
            eq1 = rt[:, 256:320].rearrange("p (b n) -> p b n", b=TB)
            eq2 = rt[:, 320:384].rearrange("p (b n) -> p b n", b=TB)
            rest = rt[:, 384:448].rearrange("p (b n) -> p b n", b=TB)
            step(V.tensor_reduce(m1, el2, AX.X, ALU.max))
            step(V.tensor_tensor(eq1, el2, wide(m1, 32), ALU.is_equal))
            step(V.scalar_tensor_tensor(rest, eq1, BIG_NEG, el2, ALU.mult, ALU.add))
            step(V.tensor_reduce(m2, rest, AX.X, ALU.max))
            step(V.tensor_tensor(eq2, rest, wide(m2, 32), ALU.is_equal))
            V.tensor_tensor(rt[:, 40:42], m2, m1, ALU.subtract).then_inc(S("rt_dif"), 1)
            dve.wait_ge(S("rt_exp"), 2)
            gw, w1, w2 = rt[:, 28:30], rt[:, 30:32], rt[:, 32:34]
            step(V.reduce_sum(gw, ex, AX.X))
            step(V.reciprocal(gw, gw))
            step(V.tensor_scalar(w1, rt[:, 40:42], 1.0, None, ALU.add))
            step(V.reciprocal(w1, w1))
            step(V.tensor_tensor(w1, w1, gw, ALU.mult))
            step(V.tensor_tensor(w2, w1, rt[:, 40:42], ALU.mult))
            step(V.tensor_tensor(eq1, eq1, wide(w1, 32), ALU.mult))
            step(V.tensor_tensor(eq2, eq2, wide(w2, 32), ALU.mult))
            step(V.tensor_tensor(comb, eq1, eq2, ALU.add))
            with dve.Fori(0, 3) as rnd:
                hidden_rounds(t_moe, n_moe, 8, rnd, "moe", 0, None, lambda k: split_lo(t_moe + 96 + k, rnd * 12))
            hidden_rounds(t_moe + 288, n_moe + 36, 8, 0, "moe", 24, None, lambda k: split_lo(t_ple + k, 0))
            stage_end(dve, "dve")

            norm("n5")
            dve.wait_ge(S("p_hi"), 1)
            V.tensor_tensor(blo[:, 0:2, :], bank[3][:].rearrange("p (c n) -> p c n", c=2),
                            bhi[:, 0:2, :].bitcast(F32), ALU.subtract).then_inc(S("p_lo"), 1)
            for i in range(4, 4 * 9 + 4):
                if i < 36:
                    split_lo(t_ple + i, 0)
                if i >= 10 and (i - 10) % 9 == 0 and (i - 10) // 9 < 4:
                    g = (i - 10) // 9
                    dve.wait_ge(evac_act, 2 + n_ple + 2 * g + 1)
                    dve.sem_inc(evac_dve, 1)
                if i >= 12 and (i - 12) % 9 == 0 and (i - 12) // 9 < 4:
                    g = (i - 12) // 9
                    dve.wait_ge(tile_used, t_ple - T_ADA + 9 * g + 9 + 4)
                    for b in range(TB):
                        V.tensor_tensor(prod[:, b], gsig[:, 0, b], bank[2 + b][:], ALU.mult).then_inc(S("ple_prod"), 1)
                    dve.wait_ge(S("ple_prod"), 2 * g + 2)
                    for b in range(TB):
                        o = xres[:, b, g * COLS:(g + 1) * COLS]
                        V.tensor_tensor(o, o, prod[:, b], ALU.add)\
                            .then_inc(S("ple_sum") if b == 0 else evac_dve, 1)


INPUTS = ["x", "c", "w_ada", "b_ada", "norm1_gain", "norm2_gain", "w_in", "sb_q_gain", "sb_k_gain", "dil_q_gain",
          "dil_k_gain", "w_gla_a", "b_gla_a", "gla_out_gain", "w_br_sb", "w_br_dil", "w_br_gla", "w_out", "w_ffn_in",
          "w_ffn_out", "p_2", "mix_norm_2", "w_in_2", "b_forget_2", "q_norm_2", "k_norm_2", "conv_w_2", "conv_b_2",
          "w_rec_gate_2", "b_rec_gate_2", "w_in_gate_2", "b_in_gate_2", "lru_lambda_2", "w_out_2", "ffn_norm_2",
          "w_router_group_2", "w_router_expert_2", "w_expert_gate_2", "w_expert_up_2", "w_expert_down_2",
          "ple_norm_2", "w_ple_gate_2", "w_ple_up_2"]


def kernel(**inputs):
    import concourse.bacc as _bacc
    from concourse.bass_utils import run_bass_kernel_spmd as _run

    nc = _bacc.Bacc("TRN2", target_bir_lowering=False, num_devices=1)
    arrays, aps = {}, {}
    for name in INPUTS:
        a = np.ascontiguousarray(inputs[name])
        a = a.reshape([d for i, d in enumerate(a.shape) if d != 1 or i >= 2] or [1])
        arrays["in_" + name] = a
        aps[name] = nc.dram_tensor("in_" + name, a.shape, F32, kind="ExternalInput").ap()
    arrays["in_consts"] = shape_constants()
    aps["consts"] = nc.dram_tensor("in_consts", (P, C_ALL), F32, kind="ExternalInput").ap()
    out = nc.dram_tensor("out_0", (TB * P, D), F32, kind="ExternalOutput").ap()
    program(nc, aps, out)
    r = _run(nc, [arrays], core_ids=[0])
    return r.results[0]["out_0"].reshape(1, TB * P, D)
```
